# Optimizing a Trainium2 kernel written in Bass

```python
import math
import jax, jax.numpy as jnp
from jax import lax
import numpy as np

D_MODEL = 1024
BATCH = 1
SEQ = 256
DEPTH = 2
DEC_BATCH = 8
DEC_SEQ = 4
PAST_LEN = 1024
PAGE_SIZE = 128

HG_HEADS = 4
HG_DIM = 128
HG_WIDTH = HG_HEADS * HG_DIM
SSM_HEADS = 8
SSM_HEAD_DIM = 64
SSM_WIDTH = SSM_HEADS * SSM_HEAD_DIM
SSM_GROUPS = 2
SSM_STATE = 128
SSM_CONV = 4
SSM_CONV_DIM = SSM_WIDTH + 2 * SSM_GROUPS * SSM_STATE
ATT_WINDOWS = (128, 512, 2048)
ATT_DILATIONS = (1, 4, 16)
ATT_N_GROUPS = 3
ATT_HEADS = 4
ATT_HEAD_DIM = 64
ATT_WIDTH = ATT_HEADS * ATT_HEAD_DIM
ATT_KEYS = 128
ATT_BLOCK = 128
ATT_SCALE = ATT_HEAD_DIM ** -0.5
SCAN_CHUNK = 64
OFF_HG = 0
OFF_SSM = OFF_HG + 4 * HG_WIDTH
OFF_ATT = OFF_SSM + SSM_WIDTH + SSM_CONV_DIM + SSM_HEADS
OFF_GATE = OFF_ATT + ATT_N_GROUPS * 3 * ATT_WIDTH
N_IN = OFF_GATE + 3 * D_MODEL
D_FF = 11 * D_MODEL // 4
N_EXPERTS = 8
TOP_K = 2
D_FF_EXPERT = 7 * D_MODEL // 2
N_DENSE = (DEPTH + 1) // 2
N_MOE = DEPTH // 2
EPS = 1e-6

kernel_name = 'hybrid_hgrn2_ssd_dilated_decoder_step'

def rms_norm(x, gain):
    xf = x.astype(jnp.float32)
    y = xf * lax.rsqrt(jnp.mean(xf * xf, axis=-1, keepdims=True) + EPS)
    return (y * gain.astype(jnp.float32)).astype(x.dtype)

def _pad_time(a, pad):
    return jnp.pad(a, [(0, 0), (0, pad)] + [(0, 0)] * (a.ndim - 2))

def _to_chunks(a, c):
    b, l = a.shape[:2]
    return jnp.moveaxis(a.reshape((b, l // c, c) + a.shape[2:]), 1, 0)

def _from_chunks(a):
    n, b, c = a.shape[:3]
    return jnp.moveaxis(a, 0, 1).reshape((b, n * c) + a.shape[3:])

def hgrn2_recurrence(q, k, logf, v, s0):
    L = q.shape[1]
    c = min(SCAN_CHUNK, L)
    pad = (-L) % c
    qs, ks, fs, vs = [_to_chunks(_pad_time(a.astype(jnp.float32), pad), c) for a in (q, k, logf, v)]
    causal = jnp.tril(jnp.ones((c, c), dtype=bool))

    def step(S, inp):
        qc, kc, fc, vc = inp
        G = jnp.cumsum(fc, axis=1)
        rel = jnp.where(causal[None, :, :, None, None], G[:, :, None] - G[:, None, :], -jnp.inf)
        attn = jnp.einsum('bthd,bshd,btshd->bhts', qc, kc, jnp.exp(rel))
        o = (jnp.einsum('bhts,bshv->bthv', attn, vc)
             + jnp.einsum('bthd,bhdv->bthv', qc * jnp.exp(G), S))
        g_last = G[:, -1]
        k_dec = kc * jnp.exp(g_last[:, None] - G)
        S = jnp.exp(g_last)[..., None] * S + jnp.einsum('bshd,bshv->bhdv', k_dec, vc)
        return S, o

    S, o = lax.scan(step, s0.astype(jnp.float32), (qs, ks, fs, vs))
    return _from_chunks(o)[:, :L], S

def ssd_recurrence(x, dt, a, bm, cm, h0):
    b, L, H, P = x.shape
    G, N = bm.shape[2], bm.shape[3]
    R = H // G
    c = min(SCAN_CHUNK, L)
    pad = (-L) % c
    x = x.reshape(b, L, G, R, P)
    dt = dt.reshape(b, L, G, R)
    xs, dts, bs, cs = [_to_chunks(_pad_time(t.astype(jnp.float32), pad), c) for t in (x, dt, bm, cm)]
    la = a.astype(jnp.float32).reshape(G, R)
    causal = jnp.tril(jnp.ones((c, c), dtype=bool))

    def step(h, inp):
        xc, dtc, bc, cc = inp
        cum = jnp.cumsum(dtc * la, axis=1)
        rel = jnp.where(causal[None, :, :, None, None], cum[:, :, None] - cum[:, None, :], -jnp.inf)
        cb = jnp.einsum('btgn,bsgn->btsg', cc, bc)
        w = cb[..., None] * jnp.exp(rel) * dtc[:, None]
        y = jnp.einsum('btsgr,bsgrp->btgrp', w, xc)
        y = y + jnp.einsum('btgn,bgrpn->btgrp', cc, h) * jnp.exp(cum)[..., None]
        c_last = cum[:, -1]
        w_in = jnp.exp(c_last[:, None] - cum) * dtc
        h = jnp.exp(c_last)[..., None, None] * h + jnp.einsum('bsgrp,bsgn,bsgr->bgrpn', xc, bc, w_in)
        return h, y

    h, y = lax.scan(step, h0.astype(jnp.float32).reshape(b, G, R, P, N), (xs, dts, bs, cs))
    y = _from_chunks(y)[:, :L].reshape(b, L, H, P)
    return y, h.reshape(b, H, P, N)

def causal_dwconv(prefix, u, w, bias):
    L = u.shape[1]
    full = jnp.concatenate([prefix.astype(u.dtype), u], axis=1)
    y = bias
    for j in range(SSM_CONV):
        y = y + full[:, j:j + L] * w[j]
    return y, full[:, -(SSM_CONV - 1):]

def dilated_attention_prompt(q, k, v, dil):
    b, L, H, D = q.shape
    M = L // dil
    P = min(ATT_BLOCK, M)
    Mp = -(-M // P) * P
    nb = Mp // P

    def classes(a):
        return jnp.pad(a.reshape(b, M, dil, H, D), ((0, 0), (0, Mp - M), (0, 0), (0, 0), (0, 0)))

    def band(a):
        ap = jnp.pad(a, ((0, 0), (P, 0), (0, 0), (0, 0), (0, 0)))
        prev = ap[:, :Mp].reshape(b, nb, P, dil, H, D)
        cur = ap[:, P:].reshape(b, nb, P, dil, H, D)
        return jnp.concatenate([prev, cur], axis=2)

    qb = classes(q).reshape(b, nb, P, dil, H, D)
    kb = band(classes(k))
    vb = band(classes(v)).astype(jnp.float32)
    s = jnp.einsum('bnqrhd,bnkrhd->bnrhqk', qb, kb, preferred_element_type=jnp.float32) * ATT_SCALE
    iq = jnp.arange(P)[:, None]
    ik = jnp.arange(2 * P)[None, :]
    dist = P + iq - ik
    blk = jnp.arange(nb)[:, None, None]
    valid = (dist >= 0) & (dist <= ATT_KEYS) & (blk * P - P + ik >= 0)
    s = jnp.where(valid[None, :, None, None], s, -jnp.inf)
    m = jnp.max(s, axis=-1, keepdims=True)
    p = jnp.exp(s - m)
    den = jnp.sum(p, axis=-1, keepdims=True)
    o = jnp.einsum('bnrhqk,bnkrhd->bnqrhd', p, vb) / jnp.transpose(den, (0, 1, 4, 2, 3, 5))
    lse = jnp.transpose((m + jnp.log(den))[..., 0], (0, 1, 4, 2, 3))
    o = o.reshape(b, Mp, dil, H, D)[:, :M].reshape(b, L, H, D)
    lse = lse.reshape(b, Mp, dil, H)[:, :M].reshape(b, L, H)
    return o, lse

def dilated_attention_sample(q, k, v, buf, dil):
    wb, S = buf.shape[1], q.shape[1]
    keys = jnp.concatenate([buf[:, :, 0].astype(k.dtype), k], axis=1)
    vals = jnp.concatenate([buf[:, :, 1].astype(v.dtype), v], axis=1)
    idx = wb + jnp.arange(S)[:, None] - dil * jnp.arange(ATT_KEYS + 1)[None, :]
    valid = idx >= 0
    idx = jnp.maximum(idx, 0)
    kg = keys[:, idx]
    vg = vals[:, idx].astype(jnp.float32)
    s = jnp.einsum('bshd,bsjhd->bshj', q, kg, preferred_element_type=jnp.float32) * ATT_SCALE
    s = jnp.where(valid[None, :, None, :], s, -jnp.inf)
    m = jnp.max(s, axis=-1, keepdims=True)
    p = jnp.exp(s - m)
    den = jnp.sum(p, axis=-1, keepdims=True)
    o = jnp.einsum('bshj,bsjhd->bshd', p, vg) / den
    return o, (m + jnp.log(den))[..., 0]

def token_mixers(h, lb, w_in, hg_norm, conv_w, conv_b, dt_bias, a_log, d_skip, ssm_norm,
                 q_norm, k_norm, w_out_hg, w_out_ssm, w_out_att, w_o,
                 hg_s0, ssm_h0, conv_prefix, kv_bufs):
    b, L, _ = h.shape
    proj = h @ w_in

    hq, hf, hi, hg = jnp.split(proj[..., OFF_HG:OFF_SSM], 4, axis=-1)
    heads = lambda t: t.reshape(b, L, HG_HEADS, HG_DIM)
    fgate = lb + (1.0 - lb) * jax.nn.sigmoid(hf.astype(jnp.float32))
    o_hg, s_hg = hgrn2_recurrence(heads(jax.nn.silu(hq)), heads(1.0 - fgate),
                                  heads(jnp.log(fgate)), heads(hi), hg_s0)
    y_hg = (rms_norm(o_hg, hg_norm) * jax.nn.silu(heads(hg).astype(jnp.float32)))
    y_hg = y_hg.reshape(b, L, HG_WIDTH).astype(h.dtype)

    ssm = proj[..., OFF_SSM:OFF_ATT]
    z = ssm[..., :SSM_WIDTH]
    xbc = ssm[..., SSM_WIDTH:SSM_WIDTH + SSM_CONV_DIM]
    dt_raw = ssm[..., SSM_WIDTH + SSM_CONV_DIM:]
    xbc_c, conv_state = causal_dwconv(conv_prefix, xbc, conv_w, conv_b)
    xbc_c = jax.nn.silu(xbc_c)
    gn = SSM_GROUPS * SSM_STATE
    xs = xbc_c[..., :SSM_WIDTH].reshape(b, L, SSM_HEADS, SSM_HEAD_DIM)
    bm = xbc_c[..., SSM_WIDTH:SSM_WIDTH + gn].reshape(b, L, SSM_GROUPS, SSM_STATE)
    cm = xbc_c[..., SSM_WIDTH + gn:].reshape(b, L, SSM_GROUPS, SSM_STATE)
    dt = jax.nn.softplus(dt_raw.astype(jnp.float32) + dt_bias.astype(jnp.float32))
    a = -jnp.exp(a_log.astype(jnp.float32))
    y, s_ssm = ssd_recurrence(xs, dt, a, bm, cm, ssm_h0)
    y = y + d_skip.astype(jnp.float32)[:, None] * xs.astype(jnp.float32)
    y_ssm = rms_norm(y.reshape(b, L, SSM_WIDTH) * jax.nn.silu(z.astype(jnp.float32)), ssm_norm)
    y_ssm = y_ssm.astype(h.dtype)

    att = proj[..., OFF_ATT:OFF_GATE].reshape(b, L, ATT_N_GROUPS, 3, ATT_HEADS, ATT_HEAD_DIM)
    outs, lses, new_kv = [], [], []
    for g in range(ATT_N_GROUPS):
        qg = rms_norm(att[:, :, g, 0], q_norm[g])
        kg = rms_norm(att[:, :, g, 1], k_norm[g])
        vg = att[:, :, g, 2]
        if kv_bufs is None:
            o, lse = dilated_attention_prompt(qg, kg, vg, ATT_DILATIONS[g])
            keep = min(ATT_WINDOWS[g], L)
            new_kv.append(jnp.stack([kg, vg], axis=2)[:, L - keep:])
        else:
            o, lse = dilated_attention_sample(qg, kg, vg, kv_bufs[g], ATT_DILATIONS[g])
            new_kv.append(jnp.stack([kg, vg], axis=2))
        outs.append(o)
        lses.append(lse)
    wts = jax.nn.softmax(jnp.stack(lses), axis=0)
    y_att = jnp.sum(wts[..., None] * jnp.stack(outs), axis=0)
    y_att = y_att.reshape(b, L, ATT_WIDTH).astype(h.dtype)

    gates = jax.nn.sigmoid(proj[..., OFF_GATE:].astype(jnp.float32)).reshape(b, L, 3, D_MODEL)
    mixed = (gates[:, :, 0] * (y_hg @ w_out_hg)
             + gates[:, :, 1] * (y_ssm @ w_out_ssm)
             + gates[:, :, 2] * (y_att @ w_out_att))
    out = mixed.astype(h.dtype) @ w_o
    return out, (s_hg, s_ssm, conv_state, new_kv[0], new_kv[1], new_kv[2])

def swiglu(h, w_up, w_down):
    g, u = jnp.split(h @ w_up, 2, axis=-1)
    return (jax.nn.silu(g) * u) @ w_down

def moe_swiglu(h, w_router, w_up, w_down):
    logits = jnp.einsum('bld,de->ble', h, w_router, preferred_element_type=jnp.float32)
    top_v, top_i = lax.top_k(logits, TOP_K)
    top_w = jax.nn.softmax(top_v, axis=-1)
    combine = jnp.sum(top_w[..., None] * jax.nn.one_hot(top_i, N_EXPERTS, dtype=jnp.float32), axis=-2)
    out = jnp.zeros(h.shape, jnp.float32)
    for e in range(N_EXPERTS):
        out = out + combine[..., e:e + 1] * swiglu(h, w_up[e], w_down[e])
    return out.astype(h.dtype)

def setup_inputs(seed: int = 0) -> dict:
    key = jax.random.key(seed)
    ks = iter(jax.random.split(key, 40))
    f32 = jnp.float32
    nrm = lambda shape, scale: scale * jax.random.normal(next(ks), shape, f32)
    gain = lambda shape: 1.0 + 0.02 * jax.random.normal(next(ks), shape, f32)
    kv_shape = lambda w: (DEPTH, DEC_BATCH, min(w, PAST_LEN), 2, ATT_HEADS, ATT_HEAD_DIM)
    dt0 = jnp.exp(jax.random.uniform(next(ks), (DEPTH, SSM_HEADS), f32, math.log(1e-3), math.log(0.1)))
    dt_bias = dt0 + jnp.log(-jnp.expm1(-dt0))
    a_log = jnp.log(jax.random.uniform(next(ks), (DEPTH, SSM_HEADS), f32, 1.0, 16.0))
    return {
        'x_prompt': nrm((BATCH, SEQ, D_MODEL), 1.0),
        'x_sample': nrm((DEC_BATCH, DEC_SEQ, D_MODEL), 1.0),
        'state_hgrn': nrm((DEPTH, DEC_BATCH, HG_HEADS, HG_DIM, HG_DIM), 0.5),
        'state_ssm': nrm((DEPTH, DEC_BATCH, SSM_HEADS, SSM_HEAD_DIM, SSM_STATE), 0.3),
        'state_conv': nrm((DEPTH, DEC_BATCH, SSM_CONV - 1, SSM_CONV_DIM), 1.0),
        'cache_kv_w128': nrm(kv_shape(ATT_WINDOWS[0]), 1.0),
        'cache_kv_w512': nrm(kv_shape(ATT_WINDOWS[1]), 1.0),
        'cache_kv_w2048': nrm(kv_shape(ATT_WINDOWS[2]), 1.0),
        'w_in': nrm((DEPTH, D_MODEL, N_IN), D_MODEL ** -0.5),
        'mix_norm': gain((DEPTH, D_MODEL)),
        'hgrn_lb_logits': nrm((DEPTH, HG_WIDTH), 1.0),
        'hgrn_norm': gain((DEPTH, HG_DIM)),
        'ssm_conv_w': nrm((DEPTH, SSM_CONV, SSM_CONV_DIM), SSM_CONV ** -0.5),
        'ssm_conv_b': nrm((DEPTH, SSM_CONV_DIM), 0.02),
        'ssm_dt_bias': dt_bias,
        'ssm_a_log': a_log,
        'ssm_d': gain((DEPTH, SSM_HEADS)),
        'ssm_norm': gain((DEPTH, SSM_WIDTH)),
        'att_q_norm': gain((DEPTH, ATT_N_GROUPS, ATT_HEAD_DIM)),
        'att_k_norm': gain((DEPTH, ATT_N_GROUPS, ATT_HEAD_DIM)),
        'w_out_hgrn': nrm((DEPTH, HG_WIDTH, D_MODEL), HG_WIDTH ** -0.5),
        'w_out_ssm': nrm((DEPTH, SSM_WIDTH, D_MODEL), SSM_WIDTH ** -0.5),
        'w_out_att': nrm((DEPTH, ATT_WIDTH, D_MODEL), ATT_WIDTH ** -0.5),
        'w_o': nrm((DEPTH, D_MODEL, D_MODEL), D_MODEL ** -0.5),
        'ffn_norm': gain((DEPTH, D_MODEL)),
        'w_ffn_up': nrm((N_DENSE, D_MODEL, 2 * D_FF), D_MODEL ** -0.5),
        'w_ffn_down': nrm((N_DENSE, D_FF, D_MODEL), D_FF ** -0.5),
        'w_router': nrm((N_MOE, D_MODEL, N_EXPERTS), D_MODEL ** -0.5),
        'w_moe_up': nrm((N_MOE, N_EXPERTS, D_MODEL, 2 * D_FF_EXPERT), D_MODEL ** -0.5),
        'w_moe_down': nrm((N_MOE, N_EXPERTS, D_FF_EXPERT, D_MODEL), D_FF_EXPERT ** -0.5),
    }

def reference(x_prompt, x_sample, state_hgrn, state_ssm, state_conv, cache_kv_w128, cache_kv_w512,
              cache_kv_w2048, w_in, mix_norm, hgrn_lb_logits, hgrn_norm, ssm_conv_w, ssm_conv_b,
              ssm_dt_bias, ssm_a_log, ssm_d, ssm_norm, att_q_norm, att_k_norm, w_out_hgrn, w_out_ssm,
              w_out_att, w_o, ffn_norm, w_ffn_up, w_ffn_down, w_router, w_moe_up, w_moe_down):
    lb_soft = jax.nn.softmax(hgrn_lb_logits.astype(jnp.float32), axis=0)
    lb_table = jnp.cumsum(lb_soft, axis=0) - lb_soft[0]

    def run(x, layer_state):
        new_states = []
        for l in range(DEPTH):
            hg_s0, ssm_h0, conv_prefix, kv_bufs = layer_state(l, x.shape[0], x.dtype)
            h = rms_norm(x, mix_norm[l])
            mix_out, st = token_mixers(h, lb_table[l], w_in[l], hgrn_norm[l], ssm_conv_w[l], ssm_conv_b[l],
                                       ssm_dt_bias[l], ssm_a_log[l], ssm_d[l], ssm_norm[l],
                                       att_q_norm[l], att_k_norm[l], w_out_hgrn[l], w_out_ssm[l],
                                       w_out_att[l], w_o[l], hg_s0, ssm_h0, conv_prefix, kv_bufs)
            x = x + mix_out
            h = rms_norm(x, ffn_norm[l])
            if l % 2 == 0:
                x = x + swiglu(h, w_ffn_up[l // 2], w_ffn_down[l // 2])
            else:
                x = x + moe_swiglu(h, w_router[l // 2], w_moe_up[l // 2], w_moe_down[l // 2])
            new_states.append(st)
        return x, [jnp.stack(f) for f in zip(*new_states)]

    def fresh_state(l, b, dtype):
        return (jnp.zeros((b, HG_HEADS, HG_DIM, HG_DIM), jnp.float32),
                jnp.zeros((b, SSM_HEADS, SSM_HEAD_DIM, SSM_STATE), jnp.float32),
                jnp.zeros((b, SSM_CONV - 1, SSM_CONV_DIM), dtype),
                None)

    def cached_state(l, b, dtype):
        return (state_hgrn[l], state_ssm[l], state_conv[l],
                (cache_kv_w128[l], cache_kv_w512[l], cache_kv_w2048[l]))

    y_prompt, (p_hgrn, p_ssm, p_conv, p_kv128, p_kv512, p_kv2048) = run(x_prompt, fresh_state)
    y_sample, (s_hgrn, s_ssm, s_conv, s_kv128, s_kv512, s_kv2048) = run(x_sample, cached_state)
    return (y_prompt, y_sample, p_hgrn, p_ssm, p_conv, p_kv128, p_kv512, p_kv2048,
            s_hgrn, s_ssm, s_conv, s_kv128, s_kv512, s_kv2048)


_drawn_inputs = setup_inputs


def setup_inputs(seed=0):
    import zlib

    import numpy as np

    out = dict(_drawn_inputs(seed))
    spreads = {}
    factors = {'hgrn_norm': 2.814, 'ssm_d': 2.881, 'att_q_norm': 7.192, 'att_k_norm': 3.927}
    for name, (base, spread) in spreads.items():
        noise = np.random.default_rng([zlib.crc32(name.encode()), seed]).standard_normal(out[name].shape)
        drawn = base * np.exp(spread * noise) if base else spread * noise
        out[name] = __import__('jax').numpy.asarray(drawn.astype(out[name].dtype))
    for name, factor in factors.items():
        out[name] = (out[name] * factor).astype(out[name].dtype)
    return out
```

```python
from contextlib import ExitStack

import concourse.bass as bass
from concourse import mybir

F32 = mybir.dt.float32
I32 = mybir.dt.int32
U32 = mybir.dt.uint32
ALU = mybir.AluOpType
ACT = mybir.ActivationFunctionType
AX = mybir.AxisListType

P = 128
D = 1024
KT = D // P
TP, DB, DS = 256, 8, 4
TS = DB * DS
T = TP + TS
DEPTH = 2
HH, SH, AH = 4, 8, 4
AG = 3
CONV = 4
TAIL = CONV - 1
NEXP = 8
FF = 11 * D // 4
FE = 7 * D // 2
EPS = 1e-6
NEG = -1e30
LN_MIN = 1e-19
SCALE = 64 ** -0.5
OFF_SSM = 4 * HH * P
OFF_DT = OFF_SSM + 512 + 1024
OFF_ATT = OFF_DT + SH
N_IN = OFF_ATT + AG * 3 * 256 + 3 * D
BLK = [(0, 128), (128, 128), (256, 32)]
LEVELS = [1, 2, 4, 8, 16, 32, 64, 128]
PADW = TAIL + TP
PADT = PADW + DB * (TAIL + DS)
CW = PADT - TAIL
SLAB = 4096
RING = 3
MRING = 7
NCH = FE // 512
NDT = FF // P

V_MIX, V_FFN, V_CW, V_CB, V_SN, V_HN, V_LB, V_QN, V_KN, V_N = 0, 8, 16, 48, 56, 60, 61, 65, 68, 71

NS_HG, NS_SSM, NS_AG, NS_OUT, NS_WO = 4, 3, 11, 3, 2
NS_MIX = NS_HG + NS_SSM + NS_AG + NS_OUT + NS_WO
NS_DUP, NS_DDN = 11, 8
NS_DENSE = NS_DUP + NS_DDN

PER = dict(
    x_squared=2, rstd_ready=2, h_ready=2,
    hg_exp=3, hg_clamped=1, hg_log=1, hg_gated=1, hg_zeroed=1,
    lvl_dist=8, lvl_decay=8, lvl_q=8, lvl_k=8,
    kd_dist=1, kd_decay=1, kd_ready=1, hg_tail=1, qe_ready=1,
    vexp_ready=4, s0_scaled=4, hg_osq=1, hg_rstd=1, hg_done=1,
    conv_done=1, conv_exp=1, xs_ready=1, conv_tail=1, z_exp=1, z_gated=1,
    dt_neg=1, dt_log=1, dt_cum=1, dt_exp=1, dt_ready=1,
    w_exp=8, w_ready=8, bexp_ready=4, h0_scaled=4, ep_ready=4,
    ssm_y=1, ssm_ysq=1, ssm_rstd=1, ssm_done=1,
    qk_sq=3, qk_rstd=3, qk_ready=3, sc_neg=8, sc_exp=8, sc_ready=8,
    qx_ready=1, ss_neg=1, ss_exp=1, ss_ready=1, mixed_ready=8,
)


def hybrid_decoder(nc, x_prompt, x_sample, state_hgrn, state_ssm, state_conv, cache_kv_w128, cache_kv_w512,
                   cache_kv_w2048, w_in, mix_norm, hgrn_lb_logits, hgrn_norm, ssm_conv_w, ssm_conv_b,
                   ssm_dt_bias, ssm_a_log, ssm_d, ssm_norm, att_q_norm, att_k_norm, w_out_hgrn, w_out_ssm,
                   w_out_att, w_o, ffn_norm, w_ffn_up, w_ffn_down, w_router, w_moe_up, w_moe_down,
                   y_prompt, y_sample, p_hgrn, p_ssm, p_conv, p_kv128, p_kv512, p_kv2048,
                   s_hgrn, s_ssm, s_conv, s_kv128, s_kv512, s_kv2048):
    ctx = ExitStack()
    with ctx:
        def sb(name, shape, dt=F32):
            return ctx.enter_context(nc.sbuf_tensor(name, shape, dt))

        def sem(name):
            return ctx.enter_context(nc.semaphore(name))

        ring = sb("ring", [P, RING * SLAB])
        over = sb("over", [P, (MRING - RING) * SLAB])
        slot = [ring[:, i * SLAB:(i + 1) * SLAB] for i in range(RING)] + \
               [over[:, i * SLAB:(i + 1) * SLAB] for i in range(MRING - RING)]
        xT = sb("xT", [P, KT, T])
        hT = sb("hT", [P, KT, T])
        arena = sb("arena", [P, 14720])

        def view(base, at, *shape):
            n = 1
            for s in shape:
                n *= s
            v = base[:, at:at + n]
            if len(shape) == 2:
                v = v.rearrange("p (a b) -> p a b", a=shape[0])
            elif len(shape) == 3:
                v = v.rearrange("p (a b c) -> p a b c", a=shape[0], b=shape[1])
            return v

        att = view(over, 0, 18, T)
        gates = view(over, 18 * T, 24, T)
        hgp = view(over, 18 * T, 16, T)
        yall = view(over, 42 * T, 10, T)
        small = view(over, 52 * T, 1400)
        zT = view(arena, 0, 4, T)
        xpad = view(arena, 4 * T, 8, PADT)
        A0 = 4 * T + 8 * PADT
        G = view(arena, A0, 4, T)
        dist = view(arena, A0 + 4 * T, 4, T)
        qt = view(arena, A0 + 8 * T, 4, T)
        kt = view(arena, A0 + 12 * T, 4, T)
        S0 = [view(arena, A0 + 8 * T, DB, P), view(arena, A0 + 8 * T + 1024, DB, P)]
        A1 = A0 + 16 * T
        a00 = view(arena, A1, HH, P)
        a01 = view(arena, A1 + 512, HH, P)
        a11 = view(arena, A1 + 1024, HH, P)
        aS = view(arena, A1 + 1536, HH, TS)
        vtok = view(arena, A1 + 1664, 3, 512)
        kdtok = view(arena, A1 + 3200, 3, 512)
        vexp = view(arena, A1 + 4736, DB, P)
        assert A1 + 4736 + 1024 <= 14720
        taild = view(small, 1024, HH, DB, DS)
        qe = view(small, 1152, HH, TS)
        st_hg = view(arena, A0, HH, P)
        o_hg, osq, o_rstd = dist, view(arena, A1, HH, T), view(arena, A1 + 1664, HH, T)
        cv = view(arena, A0, 8, PADT)
        cve = view(arena, A0 + 8 * PADT, 8, PADT)
        xs = view(arena, A0 + 16 * PADT, 8, T)
        xdt = view(arena, A0, 3, 512)
        xw = view(arena, A0 + 1536, 3, 512)
        btok = view(arena, A0 + 3072, 3, 256)
        wb = [view(arena, A0 + 3840 + 416 * i, 416) for i in range(2)]
        A2 = A0 + 16 * PADT + 8 * T
        cbm = view(arena, A2, 2, 416)
        dts = view(arena, A2 + 832, 5, T)
        assert A2 + 832 + 5 * T <= 14720
        h0 = view(arena, 4 * T, DB, P)
        h0T = view(arena, 4 * T + 1024, DB, P)
        yT = view(arena, A2 + 832 + 5 * T, 4, T)
        zexp = view(arena, 4 * T, 4, T)
        cve4 = view(arena, A0 + 3840, 4, T)
        ff = view(arena, 0, NDT, T)
        ffe = [view(arena, NDT * T + 2 * T * i, 2, T) for i in range(2)]
        ssm_st = view(arena, A0, 512)
        bexp = view(small, 0, DB, P)
        crows = small[:, 0:1024]
        ctail = view(small, 1024, 8, 27)
        tokc = view(small, 1240, 3, 3, SH)
        kvtok = view(arena, 0, 3, AG, 512)
        kb = [view(arena, 4608 + 2304 * i, 9, 256) for i in range(2)]
        KTb = view(arena, 9216, 1792)
        kv_rows = view(arena, 11008, 416)
        sTs = view(arena, 11424, 3, P)
        sTn = view(arena, 11808, 3, P)
        qx = view(arena, 12192, AG, 2, 64)
        qsq = view(arena, 12576, 4, T)
        yrows = view(arena, 0, 3, D)
        htok = view(arena, 0, 3, D)
        Pm = view(arena, 3072, 3, P)
        Pc = view(arena, 3456, 3, P)
        Cm = arena[:, 3840:3840 + T]
        hg = view(arena, 4128, KT, P)
        ex = [arena[:, 5152 + 512 * i:5664 + 512 * i] for i in range(2)]
        hid = [arena[:, 6176 + 512 * i:6688 + 512 * i] for i in range(2)]
        hidT = [view(arena, 7200 + 512 * i, 4, P) for i in range(2)]
        yb = arena[:, 8224:9248]
        lg = view(arena, 9248, 3, NEXP)
        top = view(arena, 9272, 3, NEXP)
        topi = view(arena, 9296, 3, NEXP).bitcast(U32)
        topf = view(arena, 9320, 3, NEXP)
        pick = view(arena, 9344, 2, NEXP)
        chosen = view(arena, 9360, 3, NEXP)
        comb = view(arena, 9384, 3, NEXP)
        rank = view(arena, 9408, 3, NEXP)
        rw = view(arena, 9432, 3, 4)
        chosenT = arena[0:NEXP, 9444:9444 + T]
        placeT = arena[0:NEXP, 9732:9732 + T]
        rcount = arena[0:1, 10020:10024]
        rounds = arena[0:1, 10024:10025].bitcast(I32)
        wr = view(arena, 10032, KT, NEXP)
        assert 12576 + 4 * T <= 14720
        sc = [view(arena, 4608 + 768 * i, 2, 384) for i in range(2)]
        PT = [view(arena, 6144 + 768 * i, 2, 384) for i in range(2)]

        ident = sb("ident", [P, P])
        ones = sb("ones", [P, P])
        pairs = sb("pairs", [P, P])
        lmask = sb("lmask", [P, 7, P])
        causal = sb("causal", [P, P])
        scausal = sb("scausal", [TS, DB, DS])
        seqm = sb("seqm", [TS, DB])
        amask = sb("amask", [P, 2, 3 * P])
        smask = sb("smask", [P, 416])
        reset = sb("reset", [P, T])
        iota = sb("iota", [P, P])
        sel = sb("sel", [SH, SH, P])
        sel2 = sb("sel2", [SH, 4, P])
        vecs = sb("vecs", [P, DEPTH, V_N])
        lb = sb("lb", [P, DEPTH, 2, 4])
        hv = sb("hv", [SH, DEPTH, 3])
        wdt = sb("wdt", [P, KT, SH])
        dskip = sb("dskip", [P, DEPTH, 4])
        ep = sb("ep", [P, 4, TS])
        col = sb("col", [P, 40])
        eps = sb("eps", [P, 1])
        lbe = sb("lbe", [P, DEPTH, 4])
        rstd = arena[:, 14400:14400 + T]
        done = sb("done", [P, 1])
        bank = [ctx.enter_context(nc.psum_tensor(f"bank{i}", [P, 512], F32)) for i in range(8)]

        signals = {name: sem(name) for name in PER}
        raised = dict.fromkeys(PER, 0)

        def at(name, L, k=1):
            return signals[name], L * PER[name] + k

        def up(name):
            raised[name] += 1
            return signals[name], 1

        bank_filled = [sem(f"bank_filled{i}") for i in range(8)]
        bank_drained = [sem(f"bank_drained{i}") for i in range(8)]
        slab_in = [sem(f"slab_in{i}") for i in range(MRING)]
        st_out = sem("st_out")
        consts_ready, vecs_in, x_in = map(sem, ("consts_ready", "vecs_in", "x_in"))
        lb_ready, wdt_in, cstate_in, stored = map(sem, ("lb_ready", "wdt_in", "cstate_in", "stored"))
        s0_in = [sem(f"s0_in{i}") for i in range(2)]
        h0_in = sem("h0_in")
        v_used, up_exp, a_ready, lb_exp, masks_ready = map(
            sem, ("v_used", "up_exp", "a_ready", "lb_exp", "masks_ready"))
        stores = [0]
        k_in = [sem(f"k_in{i}") for i in range(2)]
        act_order, dve_order, pool_order = sem("act_order"), sem("dve_order"), sem("pool_order")

        jobs, fills = {}, [0] * 8

        def job(key, b):
            assert key not in jobs, key
            jobs[key] = (b, fills[b])
            fills[b] += 1

        acc_n = [0]

        def acc_job(key):
            job(key, 5 + acc_n[0] % 3)
            acc_n[0] += 1

        def level_banks(i):
            return (0, 1, 2) if i % 2 == 0 else (3, 4, 2)

        def level_end(L, i):
            return ("lvl", L, i, 0 if i == 7 else 2 if LEVELS[i] < DS else 1)

        def plan_mixer(L):
            job(("norm", L, 0), 0)
            for t in range(16):
                acc_job(("proj", L, t))
            for b in range(3):
                job(("vtok", L, b), 1 + b)
            job(("cstate", L), 4)
            for t in range(16, 28):
                acc_job(("proj", L, t))
            acc_job(("dt", L))
            for s in range(NS_AG):
                for t in range(4 * s, min(4 * s + 4, 42)):
                    acc_job(("proj", L, 28 + t))
                    if s < 4 and t % 2 == 1:
                        i = t // 2
                        b = level_banks(i)
                        if i < 7:
                            job(("lvl", L, i, 0), b[0])
                            job(("lvl", L, i, 1), b[1])
                            if LEVELS[i] < DS:
                                job(("lvl", L, i, 2), b[2])
                        else:
                            job(("lvl", L, i, 0), b[0])
                        if i == 0:
                            for k in range(3):
                                job(("lvl", L, "same", k), (3, 4, 2)[k])
                if s == 3:
                    for b in range(3):
                        job(("kdtok", L, b), b)
                    job(("hg_st", L), 3)
                    for h in range(HH):
                        job(("hg_o", L, h), h % 2)
                        job(("hg_s", L, h, 0), 2)
                        job(("hg_s", L, h, 1), 3)
                    for h in range(HH):
                        job(("hg_m", L, h), h)
                if s == 4:
                    job(("ctail", L, 0), 0)
                    job(("ctail", L, 1), 1)
                    job(("tokc", L), 2)
                    for b in range(3):
                        job(("xtok", L, b), 3 + b % 2)
                    for b in range(3):
                        job(("btok", L, b), b)
                    job(("cb", L, 0), 3)
                    job(("cb", L, 1), 4)
                if s in (5, 6):
                    for h in range(4 * (s - 5), 4 * (s - 5) + 4):
                        job(("wdecay", L, h), h % 2)
                        if h % 2:
                            job(("ssm_y", L, h // 2), 2 + h // 2 % 2)
                if s == 7:
                    job(("ssm_st", L), 0)
                    for j in range(4):
                        job(("h0T", L, j, 0), 1)
                        job(("h0T", L, j, 1), 2)
                        job(("inter", L, j), 3)
                        job(("ssm_s", L, j, 0), 4)
                        job(("ssm_s", L, j, 1), 0)
                    job(("ssm_m", L), 1)
                if s == 8:
                    for g in range(AG):
                        for k in range(4):
                            job(("qk_m", L, g, k), k)
                    for g in range(AG):
                        for b in range(3):
                            job(("kvtok", L, g, b), (3 * g + b) % 5)
                if s == 9:
                    for n in range(9):
                        if n < 8:
                            h, tb = n // 2, n % 2
                            for k in range(tb + 1):
                                job(("sc", L, n, k), k)
                        if n > 0:
                            m = n - 1
                            for k in range(m % 2 + 1):
                                job(("pt", L, m, k), 2 + k)
                            if m % 4 == 0:
                                job(("att_o", L, m // 4), 4)
            for b in range(DB):
                if b == 0:
                    job(("sS", L), 0)
                for k in range(4):
                    job(("kT", L, b, k), 1 + k)
            job(("sN", L), 1)
            job(("rows", L), 2)
            job(("pS", L), 3)
            job(("pN", L), 4)
            job(("oT", L), 0)
            for br in range(3):
                for m in range(KT):
                    acc_job(("out", L, br, m))
            for m in range(KT):
                acc_job(("wo", L, m))

        def plan_dense(L):
            job(("norm", L, 1), 0)
            for s in range(NS_DUP):
                for t in range(4):
                    acc_job(("up", L, s, t))
            for m in range(KT):
                acc_job(("down", L, m))

        for b in range(3):
            job(("xin", b, 0), 2 * b % 4)
            job(("xin", b, 1), 2 * b % 4 + 1)
        for L in range(DEPTH):
            job(("vecs", L), 4)
        for L in range(DEPTH):
            job(("dskip", L), 4)
        for L in range(DEPTH):
            plan_mixer(L)
            if L == 0:
                plan_dense(L)
        job(("norm", 1, 1), 0)
        for k in range(6):
            job(("htok", k // 2, k % 2), 1 + k % 4)
        job(("logits", 0), 5)
        job(("choice", 0), 6)
        job(("place", 0), 7)
        job(("count", 0), 5)
        for b in range(3):
            job(("y", b, 0), 2 * b % 4)
            job(("y", b, 1), 2 * b % 4 + 1)

        def filled(key):
            b, n = jobs[key]
            return bank_filled[b], n + 1

        def drained(key):
            b, n = jobs[key]
            return bank_drained[b], n + 1

        def psum(key):
            return bank[jobs[key][0]]

        slabs = []

        def rows_slab(w, r0, nr, c0, nc_):
            v = w[r0 * P:(r0 + nr) * P, c0:c0 + nc_].rearrange("(k p) n -> p k n", p=P)
            h = nr // 2
            return [(0, v[:, 0:h, :]), (h * nc_, v[:, h:nr, :])]

        last_use = []

        def plan_slabs(L):
            for s in range(7):
                slabs.append(rows_slab(w_in[L], 0, KT, 512 * s, 512))
                last_use.append(("proj", L, 4 * s + 3))
            for s in range(NS_AG):
                c = OFF_ATT + 512 * s
                slabs.append(rows_slab(w_in[L], 0, KT, c, min(512, N_IN - c)))
                last_use.append(("proj", L, min(28 + 4 * s + 3, 69)))
            slabs.append(rows_slab(w_out_hgrn[L], 0, 4, 0, D))
            slabs.append(rows_slab(w_out_ssm[L], 0, 4, 0, D))
            slabs.append(rows_slab(w_out_att[L], 0, 2, 0, D))
            last_use.extend(("out", L, br, KT - 1) for br in range(3))
            for s in range(2):
                slabs.append(rows_slab(w_o[L], 0, KT, 512 * s, 512))
                last_use.append(("wo", L, 4 * s + 3))
            if L == 0:
                for s in range(NS_DUP):
                    g = w_ffn_up[L].rearrange("(k p) n -> p k n", p=P)
                    slabs.append([(0, g[:, :, 256 * s:256 * s + 256]),
                                  (KT * 256, g[:, :, FF + 256 * s:FF + 256 * s + 256])])
                    last_use.append(("up", L, s, 3))
                for s in range(NS_DDN):
                    slabs.append(rows_slab(w_ffn_down[L], 0, NDT, P * s, P))
                    last_use.append(("down", L, s))

        for L in range(DEPTH):
            plan_slabs(L)
        first_slab = [0, NS_MIX + NS_DENSE]
        NSLAB = len(slabs)

        def slab(n, nr, w):
            return slot[n % RING][:, 0:nr * w].rearrange("p (k n) -> p k n", k=nr)

        def tail4(v):
            return v.rearrange("p (b i) -> p b i", i=DS)

        def load_rounds(eng):
            eng.wait_ge(rounds_ready, 1)
            return eng.value_load(rounds, min_val=1, max_val=-(-T // P))

        block = ctx.enter_context(nc.Block())

        LOOP = dict(m_sel=1, m_gathered=3, m_hg=2, m_weights=1, m_gu=14, m_exp=7, m_hid=7, m_turned=7, m_hidT=7,
                    m_down=7, m_y=2, m_scattered=8, m_added=8)
        loop_signals = {name: sem(name) for name in LOOP}
        loop_raised = dict.fromkeys(LOOP, 0)
        w_router_in, rounds_ready, rank_moved, dve_loop, chosen_exp, chosen_exped, chosen_ready, places_ready = map(
            sem, ("w_router_in", "rounds_ready", "rank_moved", "dve_loop", "chosen_exp", "chosen_exped",
                  "chosen_ready", "places_ready"))
        NDVE = 5 + 3 * NCH

        def lat(name, it, k):
            return loop_signals[name], (it + 1) * LOOP[name] + k

        def lup(name):
            loop_raised[name] += 1
            return loop_signals[name], 1

        def advance(eng, *names):
            for name in names:
                eng.sem_inc(loop_signals[name], LOOP[name])

        eslabs = []
        for c in range(NCH + 1):
            if c < NCH:
                eslabs += [("g", c), ("u", c)]
            if c > 0:
                eslabs.append(("d", c - 1))
        assert len(eslabs) % MRING == 0
        PERSLOT = len(eslabs) // MRING

        def eslot(n):
            return (n + RING) % MRING

        def eslab_in(it, n):
            q = eslot(n)
            before = len(range(q, NSLAB, RING)) if q < RING else 0
            return slab_in[q], 32 * (before + it * PERSLOT + n // MRING + 1)

        def eslab_used(it, n):
            kind, c = eslabs[n]
            if kind == "d":
                return lat("m_down", it, c + 1)
            return lat("m_gu", it, 2 * c + (1 if kind == "g" else 2))

        @block.sync
        def _(sp):
            for n, parts in enumerate(slabs):
                if n >= RING:
                    sp.wait_ge(*filled(last_use[n - RING]))
                for at_, src in parts:
                    k, w = src.shape[1], src.shape[2]
                    sp.dma_start(slot[n % RING][:, at_:at_ + k * w].rearrange("p (k n) -> p k n", k=k),
                                 src).then_inc(slab_in[n % RING], 16)

            up_v = w_moe_up[0].rearrange("e (k p) n -> p e k n", p=P)
            down_v = w_moe_down[0].rearrange("e (k p) n -> p e k n", p=P)
            nr = load_rounds(sp)
            with sp.Fori(0, nr) as r:
                with sp.Fori(0, NEXP) as e:
                    it = r * NEXP + e
                    for n, (kind, c) in enumerate(eslabs):
                        if n >= MRING:
                            sp.wait_ge(*eslab_used(it, n - MRING))
                        else:
                            sp.wait_ge(*eslab_used(it - 1, n - MRING + len(eslabs)))
                        q = slot[eslot(n)]
                        for h in range(2):
                            if kind == "d":
                                dst = q[:, 2 * h * D:(2 * h + 2) * D].rearrange("p (k n) -> p k n", k=2)
                                src = down_v[:, e, 4 * c + 2 * h:4 * c + 2 * h + 2, :]
                            else:
                                col0 = 512 * c + (FE if kind == "u" else 0)
                                dst = q[:, 2048 * h:2048 * h + 2048].rearrange("p (k n) -> p k n", k=4)
                                src = up_v[:, e, 4 * h:4 * h + 4, col0:col0 + 512]
                            sp.dma_start(dst, src).then_inc(slab_in[eslot(n)], 16)

        @block.gpsimd
        def _(pool):
            count = [0]

            def step(ins):
                count[0] += 1
                ins.then_inc(pool_order, 1)
                pool.wait_ge(pool_order, count[0])

            def say(ins, name, L, k=1):
                ins.then_inc(*up(name))
                pool.wait_ge(*at(name, L, k))

            gp = nc.gpsimd
            for b, (t0, n) in enumerate(BLK):
                src = x_prompt[0, t0:t0 + n, :] if t0 < TP else x_sample.rearrange("b i d -> (b i) d")
                pool.dma_start(arena[0:n, b * D:(b + 1) * D], src).then_inc(x_in, 16)
            for L in range(DEPTH):
                vr = arena[:, 3 * D + P * L:3 * D + P * L + P]
                rows = [(V_MIX, mix_norm[L].rearrange("(a p) -> a p", p=P)),
                        (V_FFN, ffn_norm[L].rearrange("(a p) -> a p", p=P)),
                        (V_CW, ssm_conv_w[L].rearrange("j (a p) -> (j a) p", p=P)),
                        (V_CB, ssm_conv_b[L].rearrange("(a p) -> a p", p=P)),
                        (V_SN, ssm_norm[L].rearrange("(a p) -> a p", p=P)),
                        (V_HN, hgrn_norm[L:L + 1, :]),
                        (V_LB, hgrn_lb_logits[L].rearrange("(a p) -> a p", p=P))]
                for r, src in rows:
                    pool.dma_start(vr[r:r + src.shape[0], :], src).then_inc(vecs_in, 16)
                for r, src in ((V_QN, att_q_norm[L]), (V_KN, att_k_norm[L])):
                    for e in range(2):
                        pool.dma_start(vr[r:r + AG, 64 * e:64 * e + 64], src).then_inc(vecs_in, 16)
                for k, src in enumerate((ssm_dt_bias, ssm_a_log, ssm_d)):
                    pool.dma_start(hv[:, L, k:k + 1], src[L].rearrange("(h a) -> h a", a=1)).then_inc(vecs_in, 16)

            step(gp.memset(ones[:, :], 1.0))
            step(gp.memset(ident[:, :], 0.0))
            step(gp.affine_select(out=ident[:, :], in_=ident[:, :], compare_op=ALU.not_equal, fill=1.0, base=0,
                                  pattern=[[-1, P]], channel_multiplier=1))
            step(gp.memset(eps[:, :], EPS))
            step(gp.memset(pairs[:, :], 0.0))
            step(gp.memset(pairs[0:64, 0:64], 1.0))
            step(gp.memset(pairs[64:128, 64:128], 1.0))
            step(gp.memset(lmask[:, :, :], 0.0))
            for i, h in enumerate(LEVELS[:7]):
                v = lmask[:, i, :].rearrange("p (n w) -> p n w", w=2 * h)[:, :, h:2 * h]
                step(gp.memset(v, 1.0))
                step(gp.affine_select(out=v, in_=v, compare_op=ALU.is_ge, fill=0.0, base=0,
                                      pattern=[[-2 * h, P // (2 * h)], [0, h]], channel_multiplier=1))
                step(gp.affine_select(out=v, in_=v, compare_op=ALU.is_ge, fill=0.0, base=h - 1,
                                      pattern=[[2 * h, P // (2 * h)], [0, h]], channel_multiplier=-1))
            step(gp.affine_select(out=causal[:, :], in_=ones[:, :], compare_op=ALU.is_ge, fill=0.0, base=0,
                                  pattern=[[1, P]], channel_multiplier=-1))
            step(gp.memset(seqm[:, :], 1.0))
            step(gp.affine_select(out=seqm[:, :], in_=seqm[:, :], compare_op=ALU.is_ge, fill=0.0, base=0,
                                  pattern=[[-DS, DB]], channel_multiplier=1))
            step(gp.affine_select(out=seqm[:, :], in_=seqm[:, :], compare_op=ALU.is_ge, fill=0.0, base=DS - 1,
                                  pattern=[[DS, DB]], channel_multiplier=-1))
            step(gp.tensor_tensor(scausal[:, :, :], causal[0:TS, 0:TS].rearrange("p (b i) -> p b i", i=DS),
                                  seqm[:, :].unsqueeze(2).to_broadcast([TS, DB, DS]), ALU.mult))
            step(gp.memset(reset[:, :], 1.0))
            step(gp.memset(reset[:, 0:1], 0.0))
            step(gp.memset(reset[:, TP:T:DS], 0.0))
            step(gp.iota(iota[:, :], pattern=[[1, P]], base=0, channel_multiplier=0,
                         allow_small_or_imprecise_dtypes=True))
            step(gp.memset(sel[:, :, :], 0.0))
            step(gp.affine_select(out=sel[:, :, :], in_=sel[:, :, :], compare_op=ALU.not_equal, fill=1.0, base=0,
                                  pattern=[[-1, SH], [0, P]], channel_multiplier=1))
            step(gp.memset(sel2[:, :, :], 0.0))
            v = sel2[:, :, :].rearrange("p j (e c) -> p j e c", e=2)
            step(gp.affine_select(out=v, in_=v, compare_op=ALU.not_equal, fill=1.0, base=0,
                                  pattern=[[-2, 4], [-1, 2], [0, 64]], channel_multiplier=1))
            dI = hT[:, 0:2, 0:P].bitcast(I32)
            step(gp.iota(dI, pattern=[[P, 2], [-1, P]], base=0, channel_multiplier=1))
            pI = hT[:, 2, 0:2].bitcast(I32)
            step(gp.iota(pI, pattern=[[0, 2]], base=0, channel_multiplier=1))
            cI = hT[:, 3, 0:TS].bitcast(I32)
            gp.iota(cI, pattern=[[1, TS]], base=0, channel_multiplier=0).then_inc(consts_ready, 1)

            def store(dst, src):
                pool.dma_start(dst, src).then_inc(stored, 16)
                stores[0] += 1

            def hst_store(dst, src):
                pool.dma_start(dst, src).then_inc(st_out, 16)

            for L in range(DEPTH):
                if L > 0:
                    pool.wait_ge(*at("dt_neg", L - 1))
                pool.dma_start(wdt[:, :, :], w_in[L].rearrange("(k p) n -> p k n", p=P)[:, :, OFF_DT:OFF_DT + SH]
                               ).then_inc(wdt_in, 16)
                if L > 0:
                    pool.wait_ge(*drained(("down", L - 1, KT - 1)))
                step(gp.memset(a00[:, :, :], 0.0))
                step(gp.memset(a11[:, :, :], 0.0))
                say(gp.memset(aS[0:TS, :, :], 0.0), "hg_zeroed", L)
                pool.dma_start(crows[0:DB * TAIL, :], state_conv[L].rearrange("b j c -> (b j) c")
                               ).then_inc(cstate_in, 16)
                pool.wait_ge(*at("hg_gated", L))
                for i in range(8):
                    pool.wait_ge(*at("lvl_decay", L, i + 1))
                    if i > 0:
                        pool.wait_ge(*filled(level_end(L, i - 1)))
                    if LEVELS[i] <= 16:
                        say(gp.tensor_tensor(kt[:, :, :], hgp[:, 4:8, :], dist[:, :, :], ALU.mult), "lvl_k", L, i + 1)
                    else:
                        say(gp.tensor_tensor(kt[:, :, 0:TP], hgp[:, 4:8, 0:TP], dist[:, :, 0:TP], ALU.mult),
                            "lvl_k", L, i + 1)
                pool.wait_ge(*at("kd_decay", L))
                pool.wait_ge(*filled(("lvl", L, 7, 0)))
                say(gp.tensor_tensor(kt[:, :, :], hgp[:, 4:8, :], dist[:, :, :], ALU.mult), "kd_ready", L)
                for h in range(2):
                    pool.wait_ge(*filled(("kdtok", L, 2)))
                    pool.dma_start(S0[h], state_hgrn[L, :, h].rearrange("b d v -> d b v")).then_inc(s0_in[h], 16)
                for h in range(HH):
                    pool.wait_ge(*filled(("hg_o", L, h)))
                    pool.wait_ge(s0_in[h % 2], 16 * (2 * 2 * L + 2 * (h // 2) + 1))
                    say(gp.tensor_tensor(S0[h % 2], S0[h % 2],
                                         taild[:, h, :, DS - 1:DS].to_broadcast([P, DB, P]), ALU.mult),
                        "s0_scaled", L, h + 1)
                    pool.wait_ge(*drained(("hg_s", L, h, 1)))
                    pool.dma_start(s_hgrn[L, :, h].rearrange("b d v -> d b v"), S0[h % 2]).then_inc(s0_in[h % 2], 16)
                    if h + 2 < HH:
                        pool.wait_ge(s0_in[h % 2], 16 * (2 * 2 * L + 2 * (h // 2) + 2))
                        pool.dma_start(S0[h % 2], state_hgrn[L, :, h + 2].rearrange("b d v -> d b v")
                                       ).then_inc(s0_in[h % 2], 16)
                    if h == 0:
                        pool.wait_ge(*drained(("hg_st", L)))
                        hst_store(p_hgrn[L, 0].rearrange("h d v -> d h v"), st_hg)
                for h in range(2):
                    pool.wait_ge(s0_in[h], 16 * (2 * 2 * L + 4))
                pool.wait_ge(*drained(("ctail", L, 0)))
                pool.wait_ge(*drained(("ctail", L, 1)))
                store(p_conv[L, 0], crows[0:3, :])
                store(s_conv[L].rearrange("b j c -> (b j) c"), crows[32:32 + DB * TAIL, :])
                pool.wait_ge(stored, 16 * stores[0])
                for h in range(SH):
                    if h % 4 == 0:
                        pool.wait_ge(*drained(("cb", L, h // 4)))
                    pool.wait_ge(*at("w_exp", L, h + 1))
                    step(gp.tensor_tensor(wb[h % 2][:, 0:384], wb[h % 2][:, 0:384], cbm[:, h // 4, 0:384], ALU.mult))
                    say(gp.tensor_tensor(wb[h % 2][0:TS, 384:416], wb[h % 2][0:TS, 384:416],
                                         cbm[0:TS, h // 4, 384:416], ALU.mult), "w_ready", L, h + 1)
                for j in range(4):
                    if j > 0:
                        pool.wait_ge(h0_in, 16 * (8 * L + 2 * j))
                    else:
                        pool.wait_ge(*at("z_gated", L))
                    pool.dma_start(h0, state_ssm[L, :, 2 * j:2 * j + 2].rearrange("b h p n -> (h p) b n")
                                   ).then_inc(h0_in, 16)
                    if j == 0:
                        pool.wait_ge(*drained(("btok", L, 2)))
                    if j > 0:
                        pool.wait_ge(*filled(("ssm_s", L, j - 1, 1)))
                    say(gp.tensor_tensor(bexp[0:TS], btok[0:TS, 2, (j // 2) * P:(j // 2) * P + P].unsqueeze(1)
                                         .to_broadcast([TS, DB, P]),
                                         seqm[:, :].unsqueeze(2).to_broadcast([TS, DB, P]), ALU.mult),
                        "bexp_ready", L, j + 1)
                    pool.wait_ge(*filled(("h0T", L, j, 1)))
                    pool.wait_ge(*at("ep_ready", L, j + 1))
                    say(gp.tensor_tensor(h0, h0, tail4(ep[:, j, :])[:, :, DS - 1:DS].to_broadcast([P, DB, P]),
                                         ALU.mult), "h0_scaled", L, j + 1)
                    pool.wait_ge(*drained(("ssm_s", L, j, 1)))
                    pool.dma_start(s_ssm[L, :, 2 * j:2 * j + 2].rearrange("b h p n -> (h p) b n"), h0
                                   ).then_inc(h0_in, 16)
                    if j == 0:
                        pool.wait_ge(*drained(("ssm_st", L)))
                        hst_store(p_ssm[L, 0].rearrange("(j e) p n -> (e p) j n", e=2),
                              ssm_st.rearrange("p (j n) -> p j n", j=4))
                pool.wait_ge(h0_in, 16 * (8 * L + 8))
                for i in range(4, 9):
                    pool.wait_ge(*drained(("kvtok", L, i // 3, i % 3)))
                for g, dst in enumerate((p_kv128, p_kv512, p_kv2048)):
                    for b in range(2):
                        if g == 0 and b == 0:
                            continue
                        r = dst[L, 0].rearrange("w two h d -> w (two h d)")
                        store(r[(b * P if g else 0):(b * P if g else 0) + P, :], kvtok[:, b, g, :])
                for g, dst in enumerate((s_kv128, s_kv512, s_kv2048)):
                    store(dst[L].rearrange("b i two h d -> (b i) (two h d)"), kvtok[0:TS, 2, g, :])
                for which in range(2):
                    for b in range(DB):
                        n = which * DB + b
                        if n == 0:
                            pool.wait_ge(*drained(("att_o", L, 1)))
                        if DB > b >= 2 and which == 0:
                            pool.wait_ge(*filled(("kT", L, b - 2, 3)))
                        if which == 1 and b < 2:
                            pool.wait_ge(*filled(("kT", L, 6 + b, 3)))
                        if which == 1 and b >= 2:
                            pool.wait_ge(v_used, L * DB + b - 1)
                        dst = kb[b % 2]
                        c128 = cache_kv_w128[L, b].rearrange("w two h d -> w two (h d)")
                        c512 = cache_kv_w512[L, b].rearrange("(m r) two h d -> m r two (h d)", r=4)
                        c2048 = cache_kv_w2048[L, b].rearrange("(m r) two h d -> m r two (h d)", r=16)
                        pool.dma_start(dst[:, 0, :], c128[:, which, :]).then_inc(k_in[b % 2], 16)
                        pool.dma_start(dst[:, 1:5, :], c512[:, :, which, :]).then_inc(k_in[b % 2], 16)
                        pool.dma_start(dst[0:64, 5:9, :], c2048[:, 0:4, which, :]).then_inc(k_in[b % 2], 16)
                for m in range(KT):
                    pool.wait_ge(*drained(("out", L, 2, m)))
                    step(gp.tensor_tensor(gates[:, m, :], gates[:, m, :], gates[:, 8 + m, :], ALU.add))
                    say(gp.tensor_tensor(gates[:, m, :], gates[:, m, :], gates[:, 16 + m, :], ALU.add),
                        "mixed_ready", L, m + 1)
            pool.wait_ge(*drained(("wo", 1, KT - 1)))
            pool.dma_start(wr, w_router[0].rearrange("(k p) e -> p k e", p=P)).then_inc(w_router_in, 16)
            for b, (t0, n) in enumerate(BLK):
                dst = y_prompt[0, t0:t0 + n, :] if t0 < TP else y_sample.rearrange("b i d -> (b i) d")
                for k in range(2):
                    pool.wait_ge(*drained(("y", b, k)))
                store(dst, yrows[0:n, b, :])
            pool.wait_ge(stored, 16 * stores[0])

        @block.tensor
        def _(pe):
            mm = nc.tensor.matmul
            opened = [0] * 8
            n_slab = [0]

            def open_bank(key):
                b, n = jobs[key]
                assert opened[b] == n, key
                opened[b] += 1
                if n > 0:
                    pe.wait_ge(bank_drained[b], n)
                return bank[b]

            def close_bank(ins, key):
                ins.then_inc(bank_filled[jobs[key][0]], 1)

            def put(out, lhsT, rhs, start=True, stop=True):
                return mm(out, lhsT, rhs, start=start, stop=stop, skip_group_check=True)

            def turn(out, in_):
                k, m = in_.shape
                if m == P:
                    return nc.tensor.transpose(out, in_, ident[0:k, 0:k])
                return put(out, in_, ident[0:k, 0:k])

            def take_slab(nr, w):
                n = n_slab[0]
                pe.wait_ge(slab_in[n % RING], 32 * (n // RING + 1))
                return slab(n, nr, w)

            def contract(key, w, c0, nk, src, width=P):
                acc = open_bank(key)
                for k in range(nk):
                    ins = put(acc[0:width, 0:T], w[:, k, c0:c0 + width], src[:, k, :], k == 0, k == nk - 1)
                return ins

            def proj_slab(L, keys, between=None, nk=KT, src=None):
                w = take_slab(nk, P * len(keys))
                for i, key in enumerate(keys):
                    ins = contract(key, w, P * i, nk, hT if src is None else src)
                    close_bank(ins, key)
                    if between is not None and i < len(keys) - 1:
                        between(i)
                n_slab[0] += 1
                if between is not None:
                    between(len(keys) - 1)

            def mean_over_features(L, which):
                acc = open_bank(("norm", L, which))
                pe.wait_ge(*at("x_squared", L, which + 1))
                for k in range(KT):
                    ins = put(acc[:, 0:T], ones[:, :], hT[:, k, :], k == 0, k == KT - 1)
                close_bank(ins, ("norm", L, which))

            def token_rows(key, src, blk, tiles):
                t0, n = BLK[blk]
                acc = open_bank(key)
                for i, m in enumerate(tiles):
                    ins = turn(acc[0:n, P * i:P * i + P], src[:, m, t0:t0 + n])
                close_bank(ins, key)

            def level(L, i):
                if i == "same":
                    kk, qq = hgp[:, 4:8], hgp[:, 0:4]
                    pe.wait_ge(*at("hg_gated", L))
                else:
                    kk, qq = kt, qt
                    pe.wait_ge(*at("lvl_q", L, i + 1))
                    pe.wait_ge(*at("lvl_k", L, i + 1))
                if i == 7:
                    acc = open_bank(("lvl", L, i, 0))
                    for h in range(HH):
                        ins = put(acc[:, P * h:P * h + P], kk[:, h, 0:P], qq[:, h, P:TP])
                    close_bank(ins, ("lvl", L, i, 0))
                    return
                for b in range(2):
                    acc = open_bank(("lvl", L, i, b))
                    for h in range(HH):
                        ins = put(acc[:, P * h:P * h + P], kk[:, h, P * b:P * b + P], qq[:, h, P * b:P * b + P])
                    if b == 0 or ("lvl", L, i, 2) in jobs:
                        close_bank(ins, ("lvl", L, i, b))
                if ("lvl", L, i, 2) in jobs:
                    acc = open_bank(("lvl", L, i, 2))
                    for h in range(HH):
                        ins = put(acc[0:TS, TS * h:TS * h + TS], kk[:, h, TP:T], qq[:, h, TP:T])
                    close_bank(ins, ("lvl", L, i, 2))
                else:
                    close_bank(ins, ("lvl", L, i, 1))

            def hgrn_out(L):
                pe.wait_ge(*at("kd_ready", L))
                for b in range(3):
                    token_rows(("kdtok", L, b), kt, b, range(HH))
                acc = open_bank(("hg_st", L))
                pe.wait_ge(*drained(("kdtok", L, 2)))
                pe.wait_ge(*drained(("kdtok", L, 1)))
                pe.wait_ge(*drained(("kdtok", L, 0)))
                for h in range(HH):
                    for b in range(2):
                        ins = put(acc[:, P * h:P * h + P], kdtok[:, b, P * h:P * h + P], vtok[:, b, P * h:P * h + P],
                                  b == 0, b == 1)
                close_bank(ins, ("hg_st", L))
                pe.wait_ge(*drained(("lvl", L, 7, 0)))
                pe.wait_ge(*drained(("lvl", L, 6, 1)))
                pe.wait_ge(*drained(("lvl", L, 6, 0)))
                pe.wait_ge(*at("qe_ready", L))
                for h in range(HH):
                    acc = open_bank(("hg_o", L, h))
                    v = vtok[:, :, P * h:P * h + P]
                    put(acc[:, 0:P], v[:, 0, :], a00[:, h, :], True, False)
                    put(acc[:, P:TP], v[:, 0, :], a01[:, h, :], False, False)
                    put(acc[:, P:TP], v[:, 1, :], a11[:, h, :], False, False)
                    put(acc[:, TP:T], v[0:TS, 2, :], aS[0:TS, h, :], False, False)
                    pe.wait_ge(s0_in[h % 2], 16 * (4 * L + 2 * (h // 2) + 1))
                    for b in range(DB):
                        ins = put(acc[:, TP + DS * b:TP + DS * b + DS], S0[h % 2][:, b, :],
                                  qe[:, h, DS * b:DS * b + DS], False, b == DB - 1)
                    close_bank(ins, ("hg_o", L, h))
                    pe.wait_ge(*at("vexp_ready", L, h + 1))
                    for k in range(2):
                        acc = open_bank(("hg_s", L, h, k))
                        ins = put(acc[:, :], kdtok[0:TS, 2, P * h:P * h + P],
                                  vexp[0:TS, 4 * k:4 * k + 4, :].rearrange("p b v -> p (b v)"))
                        close_bank(ins, ("hg_s", L, h, k))
                pe.wait_ge(*at("hg_osq", L))
                for h in range(HH):
                    acc = open_bank(("hg_m", L, h))
                    close_bank(put(acc[:, 0:T], ones[:, :], osq[:, h, :]), ("hg_m", L, h))

            def ssd_rows(L):
                for k in range(2):
                    acc = open_bank(("ctail", L, k))
                    if k == 0:
                        pe.wait_ge(*at("conv_tail", L))
                    for i in range(4):
                        m = 4 * k + i
                        put(acc[0:3, P * i:P * i + P], ctail[:, m, 0:3], ident[:, :])
                        ins = put(acc[32:56, P * i:P * i + P], ctail[:, m, 3:27], ident[:, :])
                    close_bank(ins, ("ctail", L, k))
                acc = open_bank(("tokc", L))
                pe.wait_ge(*at("dt_ready", L))
                for b, (t0, n) in enumerate(BLK):
                    for i, r in enumerate((2, 0, 4)):
                        c = 24 * b + 8 * i
                        ins = turn(acc[0:n, c:c + 8], dts[0:SH, r, t0:t0 + n])
                close_bank(ins, ("tokc", L))
                pe.wait_ge(*at("xs_ready", L))
                for b in range(3):
                    token_rows(("xtok", L, b), xs, b, range(4))
                for b in range(3):
                    token_rows(("btok", L, b), xs, b, (4, 5))
                for g in range(2):
                    acc = open_bank(("cb", L, g))
                    B, C = xs[:, 4 + g, :], xs[:, 6 + g, :]
                    put(acc[:, 0:TP], B[:, 0:P], C[:, 0:TP])
                    put(acc[:, TP:TP + P], B[:, P:TP], C[:, P:TP])
                    close_bank(put(acc[0:TS, 384:416], B[:, TP:T], C[:, TP:T]), ("cb", L, g))

            def ssd_head(L, h):
                acc = open_bank(("wdecay", L, h))
                close_bank(put(acc[:, 0:T], sel[:, h, :], dts[0:SH, 2, :]), ("wdecay", L, h))

            def ssd_y(L, h):
                key = ("ssm_y", L, h // 2)
                acc = open_bank(key) if h % 2 == 0 else psum(key)
                if h == 0:
                    for b in range(3):
                        pe.wait_ge(*drained(("xtok", L, b)))
                pe.wait_ge(*at("w_ready", L, h + 1))
                w, r = wb[h % 2], 64 * (h % 2)
                x = xdt[:, :, 64 * h:64 * h + 64]
                put(acc[r:r + 64, 0:TP], x[:, 0, :], w[:, 0:TP], True, False)
                put(acc[r:r + 64, P:TP], x[:, 1, :], w[:, TP:384], False, False)
                ins = put(acc[r:r + 64, TP:T], x[0:TS, 2, :], w[0:TS, 384:416], False, True)
                if h % 2:
                    close_bank(ins, key)

            def ssd_states(L):
                acc = open_bank(("ssm_st", L))
                for b in range(3):
                    pe.wait_ge(*drained(("btok", L, b)))
                for j in range(4):
                    for b in range(2):
                        ins = put(acc[:, P * j:P * j + P], xw[:, b, P * j:P * j + P],
                                  btok[:, b, (j // 2) * P:(j // 2) * P + P], b == 0, b == 1)
                close_bank(ins, ("ssm_st", L))
                for j in range(4):
                    pe.wait_ge(h0_in, 16 * (8 * L + 2 * j + 1))
                    for k in range(2):
                        acc = open_bank(("h0T", L, j, k))
                        for b in range(4):
                            ins = turn(acc[:, P * b:P * b + P], h0[:, 4 * k + b, :])
                        close_bank(ins, ("h0T", L, j, k))
                    acc = open_bank(("inter", L, j))
                    put(acc[:, TS:2 * TS], sel2[:, j, :], dts[0:SH, 3, TP:T])
                    for k in range(2):
                        pe.wait_ge(*drained(("h0T", L, j, k)))
                    for b in range(DB):
                        ins = put(acc[:, DS * b:DS * b + DS], h0T[:, b, :],
                                  xs[:, 6 + j // 2, TP + DS * b:TP + DS * b + DS])
                    close_bank(ins, ("inter", L, j))
                    pe.wait_ge(*at("bexp_ready", L, j + 1))
                    for k in range(2):
                        acc = open_bank(("ssm_s", L, j, k))
                        ins = put(acc[:, :], xw[0:TS, 2, P * j:P * j + P],
                                  bexp[0:TS, 4 * k:4 * k + 4, :].rearrange("p b v -> p (b v)"))
                        close_bank(ins, ("ssm_s", L, j, k))
                acc = open_bank(("ssm_m", L))
                pe.wait_ge(*at("ssm_ysq", L))
                for j in range(4):
                    ins = put(acc[:, 0:T], ones[:, :], cve4[:, j, :], j == 0, j == 3)
                close_bank(ins, ("ssm_m", L))

            def qk_norms(L):
                for g in range(AG):
                    for k in range(4):
                        acc = open_bank(("qk_m", L, g, k))
                        if k == 0:
                            pe.wait_ge(*at("qk_sq", L, g + 1))
                        close_bank(put(acc[:, 0:T], pairs[:, :], qsq[:, k, :]), ("qk_m", L, g, k))
                for g in range(AG):
                    pe.wait_ge(*at("qk_ready", L, g + 1))
                    for b in range(3):
                        token_rows(("kvtok", L, g, b), att, b, range(6 * g + 2, 6 * g + 6))

            def scores(L, n):
                h, tb = n // 2, n % 2
                j, r = h // 2, 64 * (h % 2)
                for k in range(tb + 1):
                    acc = open_bank(("sc", L, n, k))
                    for g in range(AG):
                        ins = put(acc[:, P * g:P * g + P], att[r:r + 64, 6 * g + j, P * tb:P * tb + P],
                                  att[r:r + 64, 6 * g + 2 + j, P * k:P * k + P])
                    close_bank(ins, ("sc", L, n, k))

            def weigh(L, n):
                h, tb = n // 2, n % 2
                j, r = h // 2, 64 * (h % 2)
                pe.wait_ge(*at("sc_ready", L, n + 1))
                for k in range(tb + 1):
                    acc = open_bank(("pt", L, n, k))
                    for g in range(AG):
                        ins = turn(acc[:, P * g:P * g + P], sc[n % 2][:, k, P * g:P * g + P])
                    close_bank(ins, ("pt", L, n, k))
                key = ("att_o", L, j)
                acc = open_bank(key) if n % 4 == 0 else psum(key)
                for k in range(tb + 1):
                    pe.wait_ge(*drained(("pt", L, n, k)))
                    if n == 0 and k == 0:
                        for i in range(4, 9):
                            pe.wait_ge(*drained(("kvtok", L, i // 3, i % 3)))
                    for g in range(AG):
                        ins = put(acc[r:r + 64, P * tb:P * tb + P], kvtok[:, k, g, 256 + 64 * h:256 + 64 * h + 64],
                                  PT[n % 2][:, k, P * g:P * g + P], k == 0 and g == 0, k == tb and g == 2)
                if n % 4 == 3:
                    close_bank(ins, key)

            def sample_keys(L):
                sS = open_bank(("sS", L))
                pe.wait_ge(*at("qx_ready", L))
                for b in range(DB):
                    kk = kb[b % 2]
                    pe.wait_ge(k_in[b % 2], 48 * (8 * L + b // 2 + 1))
                    for k in range(4):
                        acc = open_bank(("kT", L, b, k))
                        if k == 0:
                            for p in range(2):
                                ins = turn(acc[:, P * p:P * p + P], kk[:, 0, P * p:P * p + P])
                        elif k < 3:
                            for i in range(4):
                                r, p = 2 * (k - 1) + i // 2, i % 2
                                ins = turn(acc[:, P * i:P * i + P], kk[:, 1 + r, P * p:P * p + P])
                        else:
                            for i in range(8):
                                ins = turn(acc[:, 64 * i:64 * i + 64], kk[0:64, 5 + i // 2, P * (i % 2):P * (i % 2) + P])
                        close_bank(ins, ("kT", L, b, k))
                    for k in range(4):
                        pe.wait_ge(*drained(("kT", L, b, k)))
                    for p in range(2):
                        q = qx[:, :, p, 8 * b:8 * b + 8]
                        c = 16 * b + 8 * p
                        put(sS[:, c:c + 8], KTb[:, P * p:P * p + P], q[:, 0, :])
                        for r in range(4):
                            k0 = 256 + (2 * r + p) * P
                            put(sS[:, P + c + r:P + c + 8:4], KTb[:, k0:k0 + P], q[:, 1, r:8:4])
                            k0 = 1280 + (2 * r + p) * 64
                            ins = put(sS[0:64, 2 * P + c + r:2 * P + c + 8:4], KTb[:, k0:k0 + 64], q[:, 2, r:8:4])
                    if b == DB - 1:
                        close_bank(ins, ("sS", L))
                acc = open_bank(("sN", L))
                for g in range(AG):
                    for p in range(2):
                        o = acc[0:TS, P * g:P * g + P].rearrange("t (b c) -> t b c", b=DB)[:, :, 8 * p:8 * p + 8]
                        ins = put(o, att[:, 6 * g + 2 + p, TP:T], qx[:, g, p, :])
                close_bank(ins, ("sN", L))
                acc = open_bank(("rows", L))
                pe.wait_ge(*drained(("sS", L)))
                pe.wait_ge(*drained(("sN", L)))
                turn(acc[:, 0:P], sTs[:, 0, :])
                turn(acc[:, P:2 * P], sTs[:, 1, :])
                turn(acc[:, 2 * P:2 * P + 64], sTs[0:64, 2, :])
                for g in range(AG):
                    ins = turn(acc[:, 320 + TS * g:320 + TS * g + TS], sTn[0:TS, g, :])
                close_bank(ins, ("rows", L))

            def sample_values(L):
                acc = open_bank(("pS", L))
                pe.wait_ge(*at("ss_ready", L))
                turn(acc[:, 0:P], kv_rows[:, 0:P])
                turn(acc[:, P:2 * P], kv_rows[:, P:2 * P])
                close_bank(turn(acc[0:64, 2 * P:3 * P], kv_rows[:, 2 * P:2 * P + 64]), ("pS", L))
                acc = open_bank(("pN", L))
                for g in range(AG):
                    ins = turn(acc[0:TS, P * g:P * g + P], kv_rows[:, 320 + TS * g:320 + TS * g + TS])
                close_bank(ins, ("pN", L))
                oT = open_bank(("oT", L))
                pe.wait_ge(*drained(("pS", L)))
                pe.wait_ge(*drained(("pN", L)))
                for g in range(AG):
                    for p in range(2):
                        pr = sTn[0:TS, g, :].rearrange("t (b c) -> t b c", b=DB)[:, :, 8 * p:8 * p + 8]
                        o = oT[:, 0:P].rearrange("t (b c) -> t b c", b=DB)[:, :, 8 * p:8 * p + 8]
                        put(o, kvtok[0:TS, 2, g, 256 + P * p:256 + P * p + P], pr, g == 0 and p == 0, False)
                for b in range(DB):
                    vv = kb[b % 2]
                    pe.wait_ge(k_in[b % 2], 48 * (8 * L + 4 + b // 2 + 1))
                    for p in range(2):
                        c = 16 * b + 8 * p
                        put(oT[:, c:c + 8], vv[:, 0, P * p:P * p + P], sTs[:, 0, c:c + 8], False, False)
                        for r in range(4):
                            put(oT[:, c + r:c + 8:4], vv[:, 1 + r, P * p:P * p + P], sTs[:, 1, c + r:c + 8:4],
                                False, False)
                            ins = put(oT[:, c + r:c + 8:4], vv[0:64, 5 + r, P * p:P * p + P],
                                      sTs[0:64, 2, c + r:c + 8:4], False, False)
                    if b == DB - 1:
                        close_bank(ins, ("oT", L))
                    else:
                        ins.then_inc(v_used, 1)

            def mixer(L):
                mean_over_features(L, 0)
                pe.wait_ge(*at("h_ready", L, 1))
                for s in range(NS_HG):
                    proj_slab(L, [("proj", L, 4 * s + i) for i in range(4)])
                for b in range(3):
                    if b == 0:
                        pe.wait_ge(*drained(("proj", L, 11)))
                        pe.wait_ge(*drained(("proj", L, 10)))
                        pe.wait_ge(*drained(("proj", L, 9)))
                    token_rows(("vtok", L, b), hgp, b, range(8, 12))
                acc = open_bank(("cstate", L))
                pe.wait_ge(cstate_in, 16 * (L + 1))
                for m in range(KT):
                    ins = turn(acc[:, 24 * m:24 * m + 24], crows[0:24, P * m:P * m + P])
                close_bank(ins, ("cstate", L))
                for s in range(NS_HG, NS_HG + NS_SSM):
                    proj_slab(L, [("proj", L, 4 * s + i) for i in range(4)])
                pe.wait_ge(wdt_in, 16 * (L + 1))
                close_bank(contract(("dt", L), wdt, 0, KT, hT, SH), ("dt", L))
                for s in range(NS_AG):
                    n = min(4, 42 - 4 * s)

                    def between(i):
                        if s < 4 and i % 2 == 1:
                            level(L, 2 * s + i // 2)
                            if 2 * s + i // 2 == 0:
                                level(L, "same")
                    proj_slab(L, [("proj", L, 28 + 4 * s + i) for i in range(n)], between)
                    if s == 3:
                        hgrn_out(L)
                    if s == 4:
                        ssd_rows(L)
                    if s in (5, 6):
                        h0_ = 4 * (s - 5)
                        for h in range(h0_, h0_ + 5):
                            if h < h0_ + 4:
                                ssd_head(L, h)
                            if h > h0_:
                                ssd_y(L, h - 1)
                    if s == 7:
                        ssd_states(L)
                    if s == 8:
                        qk_norms(L)
                    if s == 9:
                        for n_ in range(9):
                            if n_ < 8:
                                scores(L, n_)
                            if n_ > 0:
                                weigh(L, n_ - 1)
                sample_keys(L)
                sample_values(L)
                for br, (nk, y0) in enumerate(((4, 0), (4, 4), (2, 8))):
                    if br == 0:
                        pe.wait_ge(*at("hg_done", L))
                        pe.wait_ge(*at("ssm_done", L))
                        pe.wait_ge(*drained(("att_o", L, 1)))
                        pe.wait_ge(*drained(("oT", L)))
                    proj_slab(L, [("out", L, br, m) for m in range(KT)], None, nk, yall[:, y0:y0 + nk, :])
                for s in range(2):
                    w = take_slab(KT, 512)
                    for i in range(4):
                        key = ("wo", L, 4 * s + i)
                        acc = open_bank(key)
                        for k in range(KT):
                            if s == 0 and i == 0:
                                pe.wait_ge(*at("mixed_ready", L, k + 1))
                            ins = put(acc[:, 0:T], w[:, k, P * i:P * i + P], gates[:, k, :], k == 0, k == KT - 1)
                        close_bank(ins, key)
                    n_slab[0] += 1

            def dense(L):
                mean_over_features(L, 1)
                pe.wait_ge(*at("h_ready", L, 2))
                for s in range(NS_DUP):
                    w = take_slab(2 * KT, 256)
                    for t in range(4):
                        key = ("up", L, s, t)
                        close_bank(contract(key, w[:, KT * (t // 2):KT * (t // 2) + KT, :], P * (t % 2), KT, hT), key)
                    n_slab[0] += 1
                for s in range(NS_DDN):
                    w = take_slab(NDT, P)
                    acc = open_bank(("down", L, s))
                    for k in range(NDT):
                        if s == 0:
                            pe.wait_ge(*drained(("up", L, k // 2, 2 + k % 2)))
                        ins = put(acc[:, 0:T], w[:, k, :], ff[:, k, :], k == 0, k == NDT - 1)
                    close_bank(ins, ("down", L, s))
                    n_slab[0] += 1

            pe.wait_ge(consts_ready, 1)
            pe.wait_ge(x_in, 48)
            for b, (t0, n) in enumerate(BLK):
                for k in range(2):
                    acc = open_bank(("xin", b, k))
                    for i in range(4):
                        m = 4 * k + i
                        ins = turn(acc[:, P * i:P * i + n], arena[0:n, b * D + P * m:b * D + P * m + P])
                    close_bank(ins, ("xin", b, k))
            pe.wait_ge(vecs_in, 16 * 14 * DEPTH)
            for L in range(DEPTH):
                acc = open_bank(("vecs", L))
                ins = turn(acc[:, 0:V_N], arena[0:V_N, 3 * D + P * L:3 * D + P * L + P])
                close_bank(ins, ("vecs", L))
            for L in range(DEPTH):
                acc = open_bank(("dskip", L))
                for j in range(4):
                    ins = put(acc[:, j:j + 1], sel2[:, j, :], hv[:, L, 2:3])
                close_bank(ins, ("dskip", L))
            for L in range(DEPTH):
                mixer(L)
                if L == 0:
                    dense(L)
            mean_over_features(1, 1)
            pe.wait_ge(*at("h_ready", 1, 2))
            for k in range(6):
                token_rows(("htok", k // 2, k % 2), hT, k // 2, range(4 * (k % 2), 4 * (k % 2) + 4))
            pe.wait_ge(w_router_in, 16)
            acc = open_bank(("logits", 0))
            for b, (t0, n) in enumerate(BLK):
                for k in range(KT):
                    ins = put(acc[0:n, 8 * b:8 * b + 8], hT[:, k, t0:t0 + n], wr[:, k, :], k == 0, k == KT - 1)
            close_bank(ins, ("logits", 0))
            acc = open_bank(("choice", 0))
            pe.wait_ge(chosen_ready, 1)
            for b, (t0, n) in enumerate(BLK):
                ins = put(acc[0:NEXP, t0:t0 + n], chosen[0:n, b, :], ident[0:n, 0:n])
            close_bank(ins, ("choice", 0))
            acc = open_bank(("place", 0))
            pe.wait_ge(places_ready, 1)
            for b, (t0, n) in enumerate(BLK):
                ins = put(acc[0:n, 8 * b:8 * b + 8], placeT[:, t0:t0 + n], ident[0:NEXP, 0:NEXP])
            close_bank(ins, ("place", 0))
            acc = open_bank(("count", 0))
            close_bank(put(acc[0:1, 0:NEXP], chosenT[:, T - 1:T], ident[0:NEXP, 0:NEXP]), ("count", 0))
            pe.wait_ge(*drained(("wo", 1, KT - 1)))
            for k in range(6):
                pe.wait_ge(*drained(("htok", k // 2, k % 2)))
            pe.wait_ge(*drained(("place", 0)))
            pe.wait_ge(*drained(("count", 0)))
            advance(pe, "m_gathered", "m_gu", "m_turned", "m_down", "m_scattered")
            G_, U_, T_, Y_ = (bank[0], bank[1]), (bank[2], bank[3]), bank[4], (bank[5], bank[6])
            sbanks = (7, 4, 0, 1, 2, 3, 7, 4)
            nr = load_rounds(pe)
            with pe.Fori(0, nr) as r:
                with pe.Fori(0, NEXP) as e:
                    it = r * NEXP + e
                    pe.wait_ge(*lat("m_added", it, 0))
                    pe.wait_ge(*lat("m_sel", it, 1))
                    for half in range(2):
                        for i in range(4):
                            m = 4 * half + i
                            for b, (t0, n) in enumerate(BLK):
                                ins = put(bank[half][:, P * i:P * i + P], htok[0:n, b, P * m:P * m + P], Pm[0:n, b, :],
                                          b == 0, b == 2)
                        ins.then_inc(*lup("m_gathered"))
                    for b, (t0, n) in enumerate(BLK):
                        ins = turn(bank[2][:, t0:t0 + n], Pc[0:n, b, :])
                    ins.then_inc(*lup("m_gathered"))
                    for c in range(NCH + 1):
                        if c < NCH:
                            if c == 0:
                                pe.wait_ge(*lat("m_hg", it, 2))
                                pe.wait_ge(*lat("m_weights", it, 1))
                            if c >= 2:
                                pe.wait_ge(*lat("m_hid", it, c - 1))
                            for which, bb in (("g", G_), ("u", U_)):
                                n = eslabs.index((which, c))
                                pe.wait_ge(*eslab_in(it, n))
                                w = slot[eslot(n)].rearrange("p (k n) -> p k n", k=KT)
                                for k in range(KT):
                                    ins = put(bb[c % 2][:, :], hg[:, k, :], w[:, k, :], k == 0, k == KT - 1)
                                ins.then_inc(*lup("m_gu"))
                        if c > 0:
                            d = c - 1
                            pe.wait_ge(*lat("m_hid", it, d + 1))
                            if d > 0:
                                pe.wait_ge(*lat("m_hidT", it, d))
                            for i in range(4):
                                ins = turn(T_[:, P * i:P * i + P], hid[d % 2][:, P * i:P * i + P])
                            ins.then_inc(*lup("m_turned"))
                            n = eslabs.index(("d", d))
                            pe.wait_ge(*eslab_in(it, n))
                            pe.wait_ge(*lat("m_hidT", it, d + 1))
                            w = slot[eslot(n)].rearrange("p (k n) -> p k n", k=4)
                            for i in range(4):
                                for half in range(2):
                                    ins = put(Y_[half][:, :], hidT[d % 2][:, i, :], w[:, i, 512 * half:512 * half + 512],
                                              d == 0 and i == 0, d == NCH - 1 and i == 3)
                            ins.then_inc(*lup("m_down"))
                    pe.wait_ge(*lat("m_y", it, 2))
                    for m, q in enumerate(sbanks):
                        if m >= 6:
                            pe.wait_ge(*lat("m_added", it, m - 5))
                        put(bank[q][:, 0:T], yb[:, P * m:P * m + P], Cm).then_inc(*lup("m_scattered"))
            pe.wait_ge(*lat("m_added", (nr - 1) * NEXP + NEXP - 1, 8))
            for b in range(3):
                for k in range(2):
                    token_rows(("y", b, k), xT, b, range(4 * k, 4 * k + 4))

        @block.scalar
        def _(act):
            count = [0]

            def step(ins):
                count[0] += 1
                ins.then_inc(act_order, 1)
                act.wait_ge(act_order, count[0])

            def say(ins, name, L, k=1):
                ins.then_inc(*up(name))
                act.wait_ge(*at(name, L, k))

            def empty(ins, key):
                ins.then_inc(bank_drained[jobs[key][0]], 1)
                act.wait_ge(*drained(key))

            def fn(out, in_, f, **kw):
                return nc.scalar.activation(out, in_, f, **kw)

            def copy_out(out, key, src):
                act.wait_ge(*filled(key))
                empty(fn(out, src, ACT.Copy), key)

            def features_mean(L, which):
                if L > 0 and which == 0:
                    act.wait_ge(*drained(("down", L - 1, KT - 1)))
                if which == 1:
                    act.wait_ge(*drained(("wo", L, KT - 1)))
                    act.wait_ge(*filled(("proj", L, 69)))
                if L == 0 and which == 0:
                    act.wait_ge(masks_ready, 1)
                say(fn(hT[:, :, :], xT[:, :, :], ACT.Square), "x_squared", L, which + 1)
                key = ("norm", L, which)
                act.wait_ge(*filled(key))
                empty(fn(rstd, psum(key)[:, 0:T], ACT.Ln, scale=1.0 / D, bias=eps[:, :]), key)
                say(fn(rstd, rstd, ACT.Exp, scale=-0.5), "rstd_ready", L, which + 1)

            def level_decay(L, i):
                act.wait_ge(*at("lvl_dist", L, i + 1))
                w = T if LEVELS[i] <= 16 else TP
                say(fn(dist[:, :, 0:w], dist[:, :, 0:w], ACT.Exp), "lvl_decay", L, i + 1)

            def hgrn_tail(L):
                act.wait_ge(*at("lvl_q", L, 8))
                act.wait_ge(*at("lvl_k", L, 8))
                for h in range(HH):
                    step(fn(dist[:, h, 0:TP], G[:, h, 0:TP], ACT.Exp, scale=-1.0, bias=G[:, h, TP - 1:TP]))
                act.wait_ge(*at("kd_dist", L))
                say(fn(dist[:, :, TP:T], dist[:, :, TP:T], ACT.Exp, scale=-1.0), "kd_decay", L)
                say(fn(taild.rearrange("p h b i -> p h (b i)"), G[:, :, TP:T], ACT.Exp), "hg_tail", L)
                for b, (t0, n) in enumerate(BLK):
                    key = ("kdtok", L, b)
                    copy_out(kdtok[0:n, b, :], key, psum(key)[0:n, :])
                key = ("hg_st", L)
                act.wait_ge(*at("qe_ready", L))
                copy_out(st_hg.rearrange("p h v -> p (h v)"), key, psum(key)[:, :])
                act.wait_ge(*drained(("hg_o", L, 2)))
                act.wait_ge(*drained(("hg_o", L, 3)))
                say(fn(osq, o_hg, ACT.Square), "hg_osq", L)
                for h in range(HH):
                    key = ("hg_m", L, h)
                    act.wait_ge(*filled(key))
                    empty(fn(o_rstd[:, h, :], psum(key)[:, 0:T], ACT.Ln, scale=1.0 / P, bias=eps[:, :]), key)
                say(fn(o_rstd, o_rstd, ACT.Exp, scale=-0.5), "hg_rstd", L)

            def ssd_inputs(L):
                act.wait_ge(*at("conv_done", L))
                say(fn(cve[:, :, 0:CW], cv[:, :, 0:CW], ACT.Exp, scale=-1.0), "conv_exp", L)
                act.wait_ge(*at("conv_tail", L))
                say(fn(zexp, zT, ACT.Exp, scale=-1.0), "z_exp", L)
                act.wait_ge(*at("dt_neg", L))
                step(fn(dts[0:SH, 1, :], dts[0:SH, 1, :], ACT.Exp))
                say(fn(dts[0:SH, 1, :], dts[0:SH, 1, :], ACT.Ln, bias=ones[0:SH, 0:1]), "dt_log", L)
                act.wait_ge(*at("dt_cum", L))
                step(fn(dts[0:SH, 3, :], dts[0:SH, 2, :], ACT.Exp))
                say(fn(dts[0:SH, 4, :], dts[0:SH, 4, :], ACT.Exp, scale=-1.0), "dt_exp", L)
                for k in range(2):
                    key = ("ctail", L, k)
                    act.wait_ge(*filled(key))
                    step(fn(crows[0:3, 512 * k:512 * k + 512], psum(key)[0:3, :], ACT.Copy))
                    empty(fn(crows[32:56, 512 * k:512 * k + 512], psum(key)[32:56, :], ACT.Copy), key)
                key = ("tokc", L)
                act.wait_ge(*filled(key))
                flat = tokc.rearrange("p a b c -> p (a b c)")
                step(fn(flat[:, 0:48], psum(key)[:, 0:48], ACT.Copy))
                empty(fn(flat[0:TS, 48:72], psum(key)[0:TS, 48:72], ACT.Copy), key)
                for b, (t0, n) in enumerate(BLK):
                    key = ("btok", L, b)
                    copy_out(btok[0:n, b, :], key, psum(key)[0:n, 0:256])

            def ssd_decays(L, h):
                act.wait_ge(*drained(("wdecay", L, h)))
                w = wb[h % 2]
                step(fn(w[:, 0:384], w[:, 0:384], ACT.Exp))
                say(fn(w[0:TS, 384:416], w[0:TS, 384:416], ACT.Exp), "w_exp", L, h + 1)

            def ssd_out(L):
                key = ("ssm_st", L)
                copy_out(ssm_st, key, psum(key)[:, :])
                for j in range(4):
                    for k in range(2):
                        key = ("h0T", L, j, k)
                        copy_out(h0T[:, 4 * k:4 * k + 4, :].rearrange("n b p -> n (b p)"), key, psum(key)[:, :])
                act.wait_ge(*at("ssm_y", L))
                say(fn(cve4, yT, ACT.Square), "ssm_ysq", L)
                key = ("ssm_m", L)
                act.wait_ge(*filled(key))
                empty(fn(zT[:, 0, :], psum(key)[:, 0:T], ACT.Ln, scale=1.0 / 512, bias=eps[:, :]), key)
                say(fn(zT[:, 0, :], zT[:, 0, :], ACT.Exp, scale=-0.5), "ssm_rstd", L)

            def qk_out(L):
                act.wait_ge(*at("ssm_done", L))
                act.wait_ge(h0_in, 16 * (8 * L + 8))
                act.wait_ge(st_out, 32 * (L + 1))
                for g in range(AG):
                    if g > 0:
                        act.wait_ge(*at("qk_ready", L, g))
                    say(fn(qsq, att[:, 6 * g:6 * g + 4, :], ACT.Square), "qk_sq", L, g + 1)
                    for k in range(4):
                        key = ("qk_m", L, g, k)
                        act.wait_ge(*filled(key))
                        if k == 0:
                            for kk in range(1, 4):
                                act.wait_ge(*filled(("qk_m", L, g, kk)))
                        empty(fn(qsq[:, k, :], psum(key)[:, 0:T], ACT.Ln, scale=1.0 / 64, bias=eps[:, :]), key)
                    say(fn(qsq, qsq, ACT.Exp, scale=-0.5), "qk_rstd", L, g + 1)
                for g in range(AG):
                    for b, (t0, n) in enumerate(BLK):
                        key = ("kvtok", L, g, b)
                        copy_out(kvtok[0:n, b, g, :], key, psum(key)[0:n, :])

            def prompt_attention(L):
                for n in range(9):
                    if n < 8:
                        w = n % 2 + 1
                        act.wait_ge(*at("sc_neg", L, n + 1))
                        s = sc[n % 2].rearrange("p k c -> p (k c)")[:, 0:384 * w]
                        c = 4 * (n % 2)
                        say(fn(s, s, ACT.Exp, bias=col[:, c + 1:c + 2], accum_out=col[:, c + 2:c + 3]),
                            "sc_exp", L, n + 1)
                    if n > 0:
                        m = n - 1
                        for k in range(m % 2 + 1):
                            key = ("pt", L, m, k)
                            copy_out(PT[m % 2][:, k, :], key, psum(key)[:, 0:384])
                        if m % 4 == 3:
                            key = ("att_o", L, m // 4)
                            copy_out(yall[:, 8 + m // 4, 0:TP], key, psum(key)[:, 0:TP])

            def sample_attention(L):
                for b in range(DB):
                    for k in (2, 3):
                        key = ("kT", L, b, k)
                        copy_out(KTb[:, 256 + 512 * (k - 1):256 + 512 * k], key, psum(key)[:, :])
                key = ("sS", L)
                act.wait_ge(*filled(key))
                step(fn(sTs[:, 0:2, :].rearrange("p a r -> p (a r)"), psum(key)[:, 0:256], ACT.Copy))
                empty(fn(sTs[0:64, 2, :], psum(key)[0:64, 256:384], ACT.Copy), key)
                key = ("sN", L)
                copy_out(sTn[0:TS].rearrange("p a r -> p (a r)"), key, psum(key)[0:TS, 0:384])
                act.wait_ge(*at("ss_neg", L))
                say(fn(kv_rows, kv_rows, ACT.Exp, bias=col[:, 9:10], accum_out=col[:, 10:11]), "ss_exp", L)
                key = ("pS", L)
                act.wait_ge(*filled(key))
                step(fn(sTs[:, 0:2, :].rearrange("p a r -> p (a r)"), psum(key)[:, 0:256], ACT.Copy))
                empty(fn(sTs[0:64, 2, :], psum(key)[0:64, 256:384], ACT.Copy), key)
                key = ("pN", L)
                copy_out(sTn[0:TS].rearrange("p a r -> p (a r)"), key, psum(key)[0:TS, 0:384])

            def mixer(L):
                features_mean(L, 0)
                if L > 0:
                    act.wait_ge(*at("mixed_ready", L - 1, KT))
                for t in range(16):
                    key = ("proj", L, t)
                    copy_out(hgp[:, t, :], key, psum(key)[:, 0:T])
                    if t == 3:
                        say(fn(qt, hgp[:, 0:4, :], ACT.Exp, scale=-1.0), "hg_exp", L, 1)
                    if t == 7:
                        say(fn(dist, hgp[:, 4:8, :], ACT.Exp, scale=-1.0), "hg_exp", L, 2)
                    if t == 15:
                        say(fn(kt, hgp[:, 12:16, :], ACT.Exp, scale=-1.0), "hg_exp", L, 3)
                act.wait_ge(*at("hg_clamped", L))
                say(fn(G, G, ACT.Ln), "hg_log", L)
                for b, (t0, n) in enumerate(BLK):
                    key = ("vtok", L, b)
                    copy_out(vtok[0:n, b, :], key, psum(key)[0:n, :])
                for t in range(16, 28):
                    key = ("proj", L, t)
                    if t < 20:
                        copy_out(zT[:, t - 16, :], key, psum(key)[:, 0:T])
                    else:
                        act.wait_ge(*filled(key))
                        step(fn(xpad[:, t - 20, TAIL:PADW], psum(key)[:, 0:TP], ACT.Copy))
                        s = xpad[:, t - 20, PADW:PADT].rearrange("p (b c) -> p b c", b=DB)[:, :, TAIL:TAIL + DS]
                        empty(fn(s, tail4(psum(key)[:, TP:T]), ACT.Copy), key)
                key = ("dt", L)
                copy_out(yall[0:SH, 9, :], key, psum(key)[0:SH, 0:T])
                level_decay(L, 0)
                for s in range(NS_AG):
                    if s == 4:
                        act.wait_ge(*at("hg_done", L))
                    for t in range(4 * s, min(4 * s + 4, 42)):
                        key = ("proj", L, 28 + t)
                        if t < 18:
                            copy_out(att[:, t, :], key, psum(key)[:, 0:T])
                        else:
                            act.wait_ge(*filled(key))
                            empty(fn(gates[:, t - 18, :], psum(key)[:, 0:T], ACT.Exp, scale=-1.0), key)
                        if t % 2 == 1 and t < 14:
                            level_decay(L, t // 2 + 1)
                    if s == 3:
                        hgrn_tail(L)
                    if s == 4:
                        ssd_inputs(L)
                    if s in (5, 6):
                        for h in range(4 * (s - 5), 4 * (s - 5) + 4):
                            ssd_decays(L, h)
                    if s == 7:
                        ssd_out(L)
                    if s == 8:
                        qk_out(L)
                    if s == 9:
                        prompt_attention(L)
                sample_attention(L)

            def dense(L):
                features_mean(L, 1)
                for s in range(NS_DUP):
                    for t in range(2):
                        key = ("up", L, s, t)
                        if s >= 2:
                            act.wait_ge(*drained(("up", L, s - 2, 2 + t)))
                        act.wait_ge(*filled(key))
                        ins = fn(ffe[s % 2][:, t, :], psum(key)[:, 0:T], ACT.Exp, scale=-1.0)
                        ins.then_inc(up_exp, 1)
                        act.wait_ge(up_exp, 2 * s + t + 1)

            for b, (t0, n) in enumerate(BLK):
                for k in range(2):
                    key = ("xin", b, k)
                    act.wait_ge(*filled(key))
                    empty(fn(xT[:, 4 * k:4 * k + 4, t0:t0 + n],
                             psum(key)[:, :].rearrange("p (m t) -> p m t", m=4)[:, :, 0:n], ACT.Copy), key)
            for L in range(DEPTH):
                key = ("vecs", L)
                copy_out(vecs[:, L, :], key, psum(key)[:, 0:V_N])
            for L in range(DEPTH):
                key = ("dskip", L)
                copy_out(dskip[:, L, :], key, psum(key)[:, 0:4])
            for L in range(DEPTH):
                ins = fn(hv[:, L, 1:2], hv[:, L, 1:2], ACT.Exp)
                ins.then_inc(a_ready, 1)
                act.wait_ge(a_ready, L + 1)
            act.wait_ge(lb_ready, 1)
            ins = fn(lbe[:, :, :], lbe[:, :, :], ACT.Exp)
            ins.then_inc(lb_exp, 1)
            act.wait_ge(lb_exp, 1)
            for L in range(DEPTH):
                mixer(L)
                if L == 0:
                    dense(L)
            features_mean(1, 1)
            for k in range(6):
                b, half = k // 2, k % 2
                n = BLK[b][1]
                copy_out(htok[0:n, b, 512 * half:512 * half + 512], ("htok", b, half), psum(("htok", b, half))[0:n, :])
            for b, (t0, n) in enumerate(BLK):
                act.wait_ge(chosen_exp, b + 1)
                ins = fn(rw[0:n, b, 0:1], rw[0:n, b, 0:1], ACT.Exp)
                ins.then_inc(chosen_exped, 1)
                act.wait_ge(chosen_exped, b + 1)
            advance(act, "m_hg", "m_exp", "m_hidT", "m_y")
            nr = load_rounds(act)
            with act.Fori(0, nr) as r:
                with act.Fori(0, NEXP) as e:
                    it = r * NEXP + e
                    act.wait_ge(*lat("m_gu", it, 0))
                    for half in range(2):
                        act.wait_ge(*lat("m_gathered", it, half + 1))
                        fn(hg[:, 4 * half:4 * half + 4, :].rearrange("p a b -> p (a b)"), bank[half][:, :],
                           ACT.Copy).then_inc(*lup("m_hg"))
                    for c in range(NCH + 1):
                        if c < NCH:
                            act.wait_ge(*lat("m_hid", it, max(c - 1, 0)))
                            act.wait_ge(*lat("m_gu", it, 2 * c + 1))
                            fn(ex[c % 2], bank[c % 2][:, :], ACT.Exp, scale=-1.0).then_inc(*lup("m_exp"))
                        if c > 0:
                            d = c - 1
                            act.wait_ge(*lat("m_turned", it, d + 1))
                            act.wait_ge(*lat("m_down", it, max(d - 1, 0)))
                            fn(hidT[d % 2].rearrange("p a b -> p (a b)"), bank[4][:, :], ACT.Copy
                               ).then_inc(*lup("m_hidT"))
                    act.wait_ge(*lat("m_scattered", it, 0))
                    act.wait_ge(*lat("m_down", it, NCH))
                    for half in range(2):
                        fn(yb[:, 512 * half:512 * half + 512], bank[5 + half][:, :], ACT.Copy).then_inc(*lup("m_y"))
            for b, (t0, n) in enumerate(BLK):
                for k in range(2):
                    key = ("y", b, k)
                    copy_out(yrows[0:n, b, 512 * k:512 * k + 512], key, psum(key)[0:n, :])

        @block.vector
        def _(dve):
            count = [0]
            ve = nc.vector

            def step(ins):
                count[0] += 1
                ins.then_inc(dve_order, 1)
                dve.wait_ge(dve_order, count[0])

            def say(ins, name, L, k=1):
                ins.then_inc(*up(name))
                dve.wait_ge(*at(name, L, k))

            def empty(ins, key):
                ins.then_inc(bank_drained[jobs[key][0]], 1)
                dve.wait_ge(*drained(key))

            def tt(out, a, b, op):
                return ve.tensor_tensor(out, a, b, op)

            def sigmoid_of_exp(v):
                step(ve.tensor_scalar(v, v, 1.0, None, ALU.add))
                step(ve.reciprocal(v, v))

            def normalise(L, which):
                dve.wait_ge(*at("rstd_ready", L, which + 1))
                v = V_MIX if which == 0 else V_FFN
                for m in range(KT):
                    ins = ve.scalar_tensor_tensor(hT[:, m, :], xT[:, m, :], vecs[:, L, v + m:v + m + 1], rstd,
                                                  ALU.mult, ALU.mult)
                    if m < KT - 1:
                        step(ins)
                    else:
                        say(ins, "h_ready", L, which + 1)

            def hgrn_inputs(L):
                dve.wait_ge(*at("hg_exp", L, 1))
                sigmoid_of_exp(qt)
                step(tt(hgp[:, 0:4, :], hgp[:, 0:4, :], qt, ALU.mult))
                dve.wait_ge(*at("hg_exp", L, 2))
                sigmoid_of_exp(dist)
                for h in range(HH):
                    step(ve.tensor_scalar(dist[:, h, :], dist[:, h, :], lb[:, L, 1, h:h + 1], lb[:, L, 0, h:h + 1],
                                          ALU.mult, ALU.add))
                say(ve.tensor_scalar(G, dist, LN_MIN, None, ALU.max), "hg_clamped", L)
                step(ve.tensor_scalar(hgp[:, 4:8, :], dist, -1.0, 1.0, ALU.mult, ALU.add))
                dve.wait_ge(*at("hg_log", L))
                for h in range(HH):
                    step(ve.tensor_tensor_scan(G[:, h, :], reset[:, :], G[:, h, :], 0.0, ALU.mult, ALU.add))
                level_dist(L, 0)
                dve.wait_ge(*at("hg_exp", L, 3))
                sigmoid_of_exp(kt)
                say(tt(hgp[:, 12:16, :], hgp[:, 12:16, :], kt, ALU.mult), "hg_gated", L)
                step(ve.memset(xpad[:, :, 0:TAIL], 0.0))
                key = ("cstate", L)
                dve.wait_ge(*filled(key))
                dst = xpad[:, :, PADW:PADT].rearrange("p m (b c) -> p m b c", b=DB)[:, :, :, 0:TAIL]
                src = psum(key)[:, 0:192].rearrange("p (m b c) -> p m b c", m=KT, b=DB)
                empty(ve.tensor_copy(dst, src), key)

            def level_dist(L, i):
                h = LEVELS[i]
                if i > 0:
                    dve.wait_ge(*at("lvl_k", L, i))
                if h <= 16:
                    g = G.rearrange("p h t -> p (h t)").rearrange("p (n w) -> p n w", w=2 * h)
                    d = dist.rearrange("p h t -> p (h t)").rearrange("p (n w) -> p n w", w=2 * h)
                    step(tt(d, g, g[:, :, h - 1:h].to_broadcast([P, HH * T // (2 * h), 2 * h]), ALU.subtract))
                    d = dist
                else:
                    g = G[:, :, 0:TP].rearrange("p h (n w) -> p h n w", w=2 * h)
                    d = dist[:, :, 0:TP].rearrange("p h (n w) -> p h n w", w=2 * h)
                    step(tt(d, g, g[:, :, :, h - 1:h].to_broadcast([P, HH, TP // (2 * h), 2 * h]), ALU.subtract))
                    d = dist[:, :, 0:TP]
                say(ve.scalar_tensor_tensor(d, d, -1.0, d, ALU.mult, ALU.min), "lvl_dist", L, i + 1)

            def level_mask(L, i):
                if i == 7:
                    key = ("lvl", L, 7, 0)
                    dve.wait_ge(*filled(key))
                    empty(ve.tensor_copy(a01.rearrange("p h t -> p (h t)"), psum(key)[:, :]), key)
                    return
                m = ident[:, :] if i == "same" else lmask[:, i, :]
                for b, a in enumerate((a00, a11, aS)):
                    key = ("lvl", L, i, b)
                    if key not in jobs:
                        continue
                    n = P if b < 2 else TS
                    dve.wait_ge(*filled(key))
                    mk = m[0:n, 0:n].unsqueeze(1).to_broadcast([n, HH, n]).bitcast(U32)
                    src = psum(key)[0:n, 0:HH * n].rearrange("p (h t) -> p h t", h=HH)
                    empty(ve.copy_predicated(a[0:n], mk, src), key)

            def hgrn_levels(L):
                dve.wait_ge(*at("hg_zeroed", L))
                for i in range(8):
                    dve.wait_ge(*at("lvl_decay", L, i + 1))
                    if i > 0:
                        dve.wait_ge(*filled(level_end(L, i - 1)))
                    w = T if LEVELS[i] <= 16 else TP
                    say(tt(qt[:, :, 0:w], hgp[:, 0:4, 0:w], dist[:, :, 0:w], ALU.mult), "lvl_q", L, i + 1)
                    if i < 7:
                        level_dist(L, i + 1)
                    else:
                        dve.wait_ge(*at("lvl_k", L, 8))
                        s = G[:, :, TP:T].rearrange("p h (b i) -> p h b i", i=DS)
                        d = dist[:, :, TP:T].rearrange("p h (b i) -> p h b i", i=DS)
                        say(tt(d, s, s[:, :, :, DS - 1:DS].to_broadcast([P, HH, DB, DS]), ALU.subtract), "kd_dist", L)
                    level_mask(L, i)
                    if i == 0:
                        level_mask(L, "same")

            def hgrn_out(L):
                dve.wait_ge(*at("hg_tail", L))
                say(tt(qe, hgp[:, 0:4, TP:T], taild.rearrange("p h b i -> p h (b i)"), ALU.mult), "qe_ready", L)
                dve.wait_ge(*at("kd_ready", L))
                for h in range(HH):
                    if h > 0:
                        dve.wait_ge(*filled(("hg_s", L, h - 1, 1)))
                    say(tt(vexp[0:TS], vtok[0:TS, 2, P * h:P * h + P].unsqueeze(1).to_broadcast([TS, DB, P]),
                           seqm[:, :].unsqueeze(2).to_broadcast([TS, DB, P]), ALU.mult), "vexp_ready", L, h + 1)
                    key = ("hg_o", L, h)
                    dve.wait_ge(*filled(key))
                    empty(ve.tensor_copy(o_hg[:, h, :], psum(key)[:, 0:T]), key)
                    dve.wait_ge(*at("s0_scaled", L, h + 1))
                    for k in range(2):
                        key = ("hg_s", L, h, k)
                        s = S0[h % 2][:, 4 * k:4 * k + 4, :].rearrange("p b v -> p (b v)")
                        dve.wait_ge(*filled(key))
                        empty(tt(s, s, psum(key)[:, :], ALU.add), key)
                dve.wait_ge(*at("hg_rstd", L))
                step(ve.scalar_tensor_tensor(o_hg, o_hg, vecs[:, L, V_HN:V_HN + 1], o_rstd, ALU.mult, ALU.mult))
                say(tt(yall[:, 0:4, :], o_hg, hgp[:, 12:16, :], ALU.mult), "hg_done", L)

            def gate_tiles(L, s):
                a, b = max(4 * s, 18), min(4 * s + 4, 42)
                dve.wait_ge(*drained(("proj", L, 28 + b - 1)))
                for t in range(b - a):
                    dve.wait_ge(*drained(("proj", L, 28 + a + t)))
                sigmoid_of_exp(gates[:, a - 18:b - 18, :])

            def ssd_inputs(L):
                for t in range(20, 28):
                    dve.wait_ge(*drained(("proj", L, t)))
                for i in range(2):
                    dve.wait_ge(s0_in[i], 16 * (4 * L + 4))
                dve.wait_ge(st_out, 16 * (2 * L + 1))
                for m in range(8):
                    w = [vecs[:, L, V_CW + 8 * j + m:V_CW + 8 * j + m + 1] for j in range(CONV)]
                    step(ve.tensor_scalar(cv[:, m, 0:CW], xpad[:, m, 0:CW], w[0],
                                          vecs[:, L, V_CB + m:V_CB + m + 1], ALU.mult, ALU.add))
                    for j in range(1, CONV):
                        ins = ve.scalar_tensor_tensor(cv[:, m, 0:CW], xpad[:, m, j:j + CW], w[j], cv[:, m, 0:CW],
                                                      ALU.mult, ALU.add)
                        if m == 7 and j == CONV - 1:
                            say(ins, "conv_done", L)
                        else:
                            step(ins)
                step(ve.tensor_copy(ctail[:, :, 0:TAIL], xpad[:, :, PADW - TAIL:PADW]))
                for m in range(KT):
                    s = xpad[:, m, PADW:PADT].rearrange("p (b c) -> p b c", b=DB)[:, :, DS:DS + TAIL]
                    ins = ve.tensor_copy(ctail[:, m, TAIL:27].rearrange("p (b c) -> p b c", b=DB), s)
                    if m < KT - 1:
                        step(ins)
                    else:
                        say(ins, "conv_tail", L)
                dve.wait_ge(*drained(("dt", L)))
                u, tmp, cum, wl = (dts[0:SH, i, :] for i in (0, 1, 2, 4))
                step(ve.tensor_scalar(u, yall[0:SH, 9, :], hv[:, L, 0:1], None, ALU.add))
                say(ve.scalar_tensor_tensor(tmp, u, -1.0, u, ALU.mult, ALU.min), "dt_neg", L)
                dve.wait_ge(*at("conv_exp", L))
                sigmoid_of_exp(cve[:, :, 0:CW])
                step(tt(xs[:, :, 0:TP], cv[:, :, 0:TP], cve[:, :, 0:TP], ALU.mult))
                for m in range(KT):
                    a, b = (v[:, m, PADW:PADT].rearrange("p (b c) -> p b c", b=DB)[:, :, 0:DS] for v in (cv, cve))
                    ins = tt(tail4(xs[:, m, TP:T]), a, b, ALU.mult)
                    if m < KT - 1:
                        step(ins)
                    else:
                        say(ins, "xs_ready", L)
                dve.wait_ge(*at("dt_log", L))
                dve.wait_ge(a_ready, L + 1)
                step(ve.scalar_tensor_tensor(u, u, 0.0, tmp, ALU.max, ALU.add))
                step(ve.tensor_scalar(cum, u, hv[:, L, 1:2], -1.0, ALU.mult, ALU.mult))
                step(ve.tensor_tensor_scan(cum, reset[0:SH, :], cum, 0.0, ALU.mult, ALU.add))
                step(ve.tensor_scalar(wl[:, 0:TP], cum[:, 0:TP], cum[:, TP - 1:TP], None, ALU.subtract))
                c4 = tail4(cum[:, TP:T])
                say(tt(tail4(wl[:, TP:T]), c4, c4[:, :, DS - 1:DS].to_broadcast([SH, DB, DS]), ALU.subtract),
                    "dt_cum", L)
                dve.wait_ge(*at("dt_exp", L))
                say(tt(wl, wl, u, ALU.mult), "dt_ready", L)
                dve.wait_ge(*at("z_exp", L))
                sigmoid_of_exp(zexp)
                say(tt(zT, zT, zexp, ALU.mult), "z_gated", L)
                for b, (t0, n) in enumerate(BLK):
                    key = ("xtok", L, b)
                    dve.wait_ge(*filled(key))
                    dve.wait_ge(*drained(("tokc", L)))
                    src = psum(key)[0:n, :].rearrange("p (h c) -> p h c", h=SH)
                    for i, dst in ((1, xdt), (2, xw)):
                        ins = tt(dst[0:n, b, :].rearrange("p (h c) -> p h c", h=SH), src,
                                 tokc[0:n, b, i, :].unsqueeze(2).to_broadcast([n, SH, 64]), ALU.mult)
                        step(ins) if i == 1 else empty(ins, key)
                for g in range(2):
                    key = ("cb", L, g)
                    dve.wait_ge(*filled(key))
                    a, c = psum(key), cbm[:, g, :]
                    step(tt(c[:, 0:P], a[:, 0:P], causal[:, :], ALU.mult))
                    step(ve.tensor_copy(c[:, P:TP], a[:, P:TP]))
                    step(tt(c[:, TP:384], a[:, TP:384], causal[:, :], ALU.mult))
                    empty(tt(c[0:TS, 384:416], a[0:TS, 384:416], scausal[:, :, :].rearrange("p b i -> p (b i)"),
                             ALU.mult), key)

            def ssd_head(L, h):
                key = ("wdecay", L, h)
                dve.wait_ge(*filled(key))
                w, a = wb[h % 2], psum(key)
                if h == 0:
                    dve.wait_ge(*drained(("tokc", L)))
                step(ve.tensor_scalar(w[:, 0:TP], a[:, 0:TP], tokc[:, 0, 0, h:h + 1], 0.0, ALU.subtract, ALU.min))
                step(ve.tensor_scalar(w[:, TP:384], a[:, P:TP], tokc[:, 1, 0, h:h + 1], 0.0, ALU.subtract, ALU.min))
                empty(ve.tensor_scalar(w[0:TS, 384:416], a[0:TS, TP:T], tokc[0:TS, 2, 0, h:h + 1], 0.0,
                                       ALU.subtract, ALU.min), key)

            def ssd_y(L, j):
                key = ("ssm_y", L, j)
                dve.wait_ge(*filled(key))
                empty(ve.scalar_tensor_tensor(yT[:, j, :], xs[:, j, :], dskip[:, L, j:j + 1], psum(key)[:, 0:T],
                                              ALU.mult, ALU.add), key)

            def ssd_out(L):
                for j in range(4):
                    key = ("inter", L, j)
                    dve.wait_ge(*filled(key))
                    say(ve.tensor_copy(ep[:, j, :], psum(key)[:, TS:2 * TS]), "ep_ready", L, j + 1)
                    empty(tt(col[:, 8:40], psum(key)[:, 0:TS], ep[:, j, :], ALU.mult), key)
                    step(tt(yT[:, j, TP:T], yT[:, j, TP:T], col[:, 8:40], ALU.add))
                    dve.wait_ge(*at("h0_scaled", L, j + 1))
                    for k in range(2):
                        key = ("ssm_s", L, j, k)
                        s = h0[:, 4 * k:4 * k + 4, :].rearrange("p b v -> p (b v)")
                        dve.wait_ge(*filled(key))
                        empty(tt(s, s, psum(key)[:, :], ALU.add), key)
                say(tt(yT, yT, zT, ALU.mult), "ssm_y", L)
                dve.wait_ge(*at("ssm_rstd", L))
                for j in range(4):
                    ins = ve.scalar_tensor_tensor(yall[:, 4 + j, :], yT[:, j, :], vecs[:, L, V_SN + j:V_SN + j + 1],
                                                  zT[:, 0, :], ALU.mult, ALU.mult)
                    step(ins) if j < 3 else say(ins, "ssm_done", L)

            def qk_out(L):
                for g in range(AG):
                    dve.wait_ge(*at("qk_rstd", L, g + 1))
                    for k in range(4):
                        v = (V_QN if k < 2 else V_KN) + g
                        a = att[:, 6 * g + k, :]
                        ins = ve.scalar_tensor_tensor(a, a, vecs[:, L, v:v + 1], qsq[:, k, :], ALU.mult, ALU.mult)
                        step(ins) if k < 3 else say(ins, "qk_ready", L, g + 1)
                step(ve.memset(qx, 0.0))
                for p in range(2):
                    for e in range(2):
                        r = slice(64 * e, 64 * e + 64)
                        for g in range(AG):
                            dst = qx[r, g, p, :].rearrange("p (b c) -> p b c", b=DB)[:, :, DS * e:DS * e + DS]
                            ins = ve.tensor_copy(dst, tail4(att[r, 6 * g + p, TP:T]))
                            step(ins) if (p, e, g) != (1, 1, 2) else say(ins, "qx_ready", L)

            def prompt_attention(L):
                for n in range(9):
                    if n < 8:
                        w = n % 2 + 1
                        c = 4 * (n % 2)
                        for k in range(w):
                            key = ("sc", L, n, k)
                            dve.wait_ge(*filled(key))
                            if n >= 2 and k == 0:
                                for kk in range(w):
                                    dve.wait_ge(*filled(("pt", L, n - 2, kk)))
                            empty(ve.scalar_tensor_tensor(sc[n % 2][:, k, :], psum(key)[:, 0:384], SCALE,
                                                          amask[:, w - 1 - k, :], ALU.mult, ALU.add), key)
                        s = sc[n % 2].rearrange("p k c -> p (k c)")[:, 0:384 * w]
                        step(ve.tensor_reduce(col[:, c:c + 1], s, AX.X, ALU.max))
                        say(ve.tensor_scalar(col[:, c + 1:c + 2], col[:, c:c + 1], -1.0, None, ALU.mult),
                            "sc_neg", L, n + 1)
                    if n > 0:
                        m = n - 1
                        c = 4 * (m % 2)
                        s = sc[m % 2].rearrange("p k c -> p (k c)")[:, 0:384 * (m % 2 + 1)]
                        dve.wait_ge(*at("sc_exp", L, m + 1))
                        step(ve.reciprocal(col[:, c + 3:c + 4], col[:, c + 2:c + 3]))
                        say(ve.tensor_scalar(s, s, col[:, c + 3:c + 4], None, ALU.mult), "sc_ready", L, m + 1)

            def sample_attention(L):
                for b in range(DB):
                    for k in (0, 1):
                        key = ("kT", L, b, k)
                        dve.wait_ge(*filled(key))
                        if k == 0:
                            empty(ve.tensor_copy(KTb[:, 0:256], psum(key)[:, 0:256]), key)
                        else:
                            empty(ve.tensor_copy(KTb[:, 256:768], psum(key)[:, :]), key)
                key = ("rows", L)
                dve.wait_ge(*filled(key))
                empty(ve.scalar_tensor_tensor(kv_rows, psum(key)[:, 0:416], SCALE, smask[:, :], ALU.mult, ALU.add), key)
                step(ve.tensor_reduce(col[:, 8:9], kv_rows, AX.X, ALU.max))
                say(ve.tensor_scalar(col[:, 9:10], col[:, 8:9], -1.0, None, ALU.mult), "ss_neg", L)
                dve.wait_ge(*at("ss_exp", L))
                step(ve.reciprocal(col[:, 11:12], col[:, 10:11]))
                say(ve.tensor_scalar(kv_rows, kv_rows, col[:, 11:12], None, ALU.mult), "ss_ready", L)
                key = ("oT", L)
                dve.wait_ge(*filled(key))
                for p in range(2):
                    for e in range(2):
                        r = slice(64 * e, 64 * e + 64)
                        c = 8 * p + DS * e
                        src = psum(key)[r, 0:P].rearrange("p (b c) -> p b c", b=DB)[:, :, c:c + DS]
                        ins = ve.tensor_copy(tail4(yall[r, 8 + p, TP:T]), src)
                        step(ins) if p + e < 2 else empty(ins, key)

            def mixer(L):
                normalise(L, 0)
                hgrn_inputs(L)
                hgrn_levels(L)
                hgrn_out(L)
                ssd_inputs(L)
                gate_tiles(L, 4)
                for h in range(SH):
                    ssd_head(L, h)
                    if h % 4 and h % 2 == 0:
                        ssd_y(L, h // 2 - 1)
                    if h % 4 == 3:
                        ssd_y(L, h // 2)
                        gate_tiles(L, 5 + h // 4)
                ssd_out(L)
                gate_tiles(L, 7)
                qk_out(L)
                gate_tiles(L, 8)
                prompt_attention(L)
                gate_tiles(L, 9)
                sample_attention(L)
                gate_tiles(L, 10)
                for br in range(3):
                    for m in range(KT):
                        key = ("out", L, br, m)
                        g = gates[:, 8 * br + m, :]
                        dve.wait_ge(*filled(key))
                        empty(tt(g, g, psum(key)[:, 0:T], ALU.mult), key)
                for m in range(KT):
                    key = ("wo", L, m)
                    dve.wait_ge(*filled(key))
                    empty(tt(xT[:, m, :], xT[:, m, :], psum(key)[:, 0:T], ALU.add), key)

            def dense(L):
                normalise(L, 1)
                for s in range(NS_DUP):
                    for t in range(4):
                        key = ("up", L, s, t)
                        e = ffe[s % 2][:, t % 2, :]
                        if t < 2:
                            dve.wait_ge(up_exp, 2 * s + t + 1)
                            sigmoid_of_exp(e)
                            empty(tt(e, e, psum(key)[:, 0:T], ALU.mult), key)
                        else:
                            dve.wait_ge(*filled(key))
                            empty(tt(ff[:, 2 * s + t - 2, :], e, psum(key)[:, 0:T], ALU.mult), key)
                for m in range(KT):
                    key = ("down", L, m)
                    dve.wait_ge(*filled(key))
                    empty(tt(xT[:, m, :], xT[:, m, :], psum(key)[:, 0:T], ALU.add), key)

            for L in range(DEPTH):
                dve.wait_ge(*drained(("vecs", L)))
            l0, l1 = (vecs[:, L, V_LB:V_LB + 4] for L in range(DEPTH))
            m4, s4 = col[:, 0:4], col[:, 4:8]
            step(tt(m4, l0, l1, ALU.max))
            step(tt(lbe[:, 0, :], l0, m4, ALU.subtract))
            ins = tt(lbe[:, 1, :], l1, m4, ALU.subtract)
            ins.then_inc(lb_ready, 1)
            dve.wait_ge(lb_ready, 1)
            dve.wait_ge(lb_exp, 1)
            step(tt(s4, lbe[:, 0, :], lbe[:, 1, :], ALU.add))
            step(ve.reciprocal(s4, s4))
            for L in range(DEPTH):
                step(tt(lbe[:, L, :], lbe[:, L, :], s4, ALU.mult))
            step(tt(s4, lbe[:, 0, :], lbe[:, 1, :], ALU.add))
            step(tt(lb[:, 0, 0, :], lbe[:, 0, :], lbe[:, 0, :], ALU.subtract))
            step(tt(lb[:, 1, 0, :], s4, lbe[:, 0, :], ALU.subtract))
            step(ve.tensor_scalar(lb[:, :, 1, :], lb[:, :, 0, :], -1.0, 1.0, ALU.mult, ALU.add))
            dve.wait_ge(consts_ready, 1)
            dI = hT[:, 0:2, 0:P].bitcast(I32)
            tI = hT[:, 4:6, 0:P].bitcast(I32)
            tF = hT[:, 6:8, 0:P]
            nearF = hT[:, 2, 4:4 + P]
            for g, dil in enumerate((1, 4, 16)):
                out = amask[:, :, P * g:P * g + P]
                step(ve.tensor_scalar(tI, dI, dil - 1, None, ALU.bitwise_and))
                step(ve.tensor_copy(tF, tI))
                step(ve.tensor_scalar(tF, tF, 0.0, None, ALU.is_equal))
                step(ve.tensor_copy(out, dI))
                if g == 0:
                    step(ve.tensor_scalar(nearF, out[:, 1, :], 128.0, None, ALU.is_le))
                step(ve.tensor_scalar(out, out, 0.0, None, ALU.is_ge))
                step(tt(out, out, tF, ALU.mult))
                if g == 0:
                    step(tt(out[:, 1, :], out[:, 1, :], nearF, ALU.mult))
                step(ve.tensor_scalar(out, out, 1.0, -NEG, ALU.subtract, ALU.mult))
            pI, cI = hT[:, 2, 0:2].bitcast(I32), hT[:, 3, 0:TS].bitcast(I32)
            qI = hT[:, 3, 32:64].bitcast(I32)
            rI = hT[:, 2, 140:142].bitcast(I32)
            tok_p, seq_p = hT[:, 2, 142:143], hT[:, 2, 143:144]
            tok_c, seq_c = hT[:, 3, 64:96], hT[:, 3, 96:128]
            step(ve.tensor_scalar(rI[:, 0:1], pI[:, 0:1], 3, None, ALU.bitwise_and))
            step(ve.tensor_scalar(rI[:, 1:2], pI[:, 1:2], 4, None, ALU.logical_shift_right))
            step(ve.tensor_copy(hT[:, 2, 142:144], rI))
            step(ve.tensor_scalar(qI, cI, 3, None, ALU.bitwise_and))
            step(ve.tensor_copy(tok_c, qI))
            step(ve.tensor_scalar(cI, cI, 2, None, ALU.logical_shift_right))
            step(ve.tensor_copy(seq_c, cI))
            step(ve.memset(smask[:, :], 1.0))
            step(ve.tensor_scalar(smask[:, 0:P], iota[:, :], tok_p, None, ALU.is_ge))
            step(ve.tensor_scalar(seq_c, seq_c, seq_p, None, ALU.is_equal))
            for g in range(AG):
                o = smask[:, 320 + TS * g:352 + TS * g]
                step(ve.tensor_scalar(o, tok_c, tok_p, None, ALU.is_le if g == 0 else ALU.is_equal))
                step(tt(o, o, seq_c, ALU.mult))
            step(ve.tensor_scalar(smask[:, :], smask[:, :], 1.0, -NEG, ALU.subtract, ALU.mult))
            ins = ve.memset(done[:, :], 0.0)
            ins.then_inc(masks_ready, 1)
            dve.wait_ge(masks_ready, 1)
            for L in range(DEPTH):
                mixer(L)
                if L == 0:
                    dense(L)
            normalise(1, 1)
            key = ("logits", 0)
            dve.wait_ge(*filled(key))
            step(ve.tensor_copy(lg[:, 0:2, :].rearrange("p b e -> p (b e)"), psum(key)[:, 0:16]))
            empty(ve.tensor_copy(lg[0:TS, 2, :], psum(key)[0:TS, 16:24]), key)
            for b, (t0, n) in enumerate(BLK):
                step(ve.max(top[0:n, b, :], lg[0:n, b, :]))
                step(ve.max_index(topi[0:n, b, :], top[0:n, b, :], lg[0:n, b, :]))
                step(ve.tensor_copy(topf[0:n, b, :], topi[0:n, b, :]))
                ins = tt(rw[0:n, b, 0:1], top[0:n, b, 1:2], top[0:n, b, 0:1], ALU.subtract)
                ins.then_inc(chosen_exp, 1)
                dve.wait_ge(chosen_exp, b + 1)
                dve.wait_ge(chosen_exped, b + 1)
                e1, den, p1, p2 = (rw[0:n, b, i:i + 1] for i in range(4))
                step(ve.tensor_scalar(den, e1, 1.0, None, ALU.add))
                step(ve.reciprocal(p1, den))
                step(tt(p2, p1, e1, ALU.mult))
                for i in range(2):
                    step(ve.tensor_scalar(pick[0:n, i, :], iota[0:n, 0:NEXP], topf[0:n, b, i:i + 1], None, ALU.is_equal))
                step(tt(chosen[0:n, b, :], pick[0:n, 0, :], pick[0:n, 1, :], ALU.add))
                step(ve.tensor_scalar(comb[0:n, b, :], pick[0:n, 0, :], p1, None, ALU.mult))
                ins = ve.scalar_tensor_tensor(comb[0:n, b, :], pick[0:n, 1, :], p2, comb[0:n, b, :], ALU.mult, ALU.add)
                if b < 2:
                    step(ins)
                else:
                    ins.then_inc(chosen_ready, 1)
                    dve.wait_ge(chosen_ready, 1)
            key = ("choice", 0)
            dve.wait_ge(*filled(key))
            empty(ve.tensor_copy(placeT, psum(key)[0:NEXP, 0:T]), key)
            step(ve.tensor_tensor_scan(chosenT, placeT, placeT, 0.0, ALU.add, ALU.max))
            step(tt(placeT, placeT, chosenT, ALU.mult))
            ins = ve.tensor_scalar(placeT, placeT, -1.0, None, ALU.add)
            ins.then_inc(places_ready, 1)
            dve.wait_ge(places_ready, 1)
            key = ("place", 0)
            dve.wait_ge(*filled(key))
            step(ve.tensor_copy(rank[:, 0:2, :].rearrange("p b e -> p (b e)"), psum(key)[:, 0:16]))
            empty(ve.tensor_copy(rank[0:TS, 2, :], psum(key)[0:TS, 16:24]), key)
            key = ("count", 0)
            dve.wait_ge(*filled(key))
            empty(ve.tensor_reduce(rcount[:, 0:1], psum(key)[0:1, 0:NEXP], AX.X, ALU.max), key)
            step(ve.tensor_scalar(rcount[:, 1:2], rcount[:, 0:1], float(P), 1.0, ALU.is_gt, ALU.add))
            step(ve.tensor_scalar(rcount[:, 2:3], rcount[:, 0:1], 2.0 * P, None, ALU.is_gt))
            step(tt(rcount[:, 3:4], rcount[:, 1:2], rcount[:, 2:3], ALU.add))
            ins = ve.tensor_copy(rounds, rcount[:, 3:4])
            ins.then_inc(rounds_ready, 1)
            dve.wait_ge(rounds_ready, 1)
            advance(dve, "m_sel", "m_weights", "m_hid", "m_added")
            dve.sem_inc(dve_loop, NDVE)
            nr = load_rounds(dve)
            with dve.Fori(0, nr) as r:
                with dve.Fori(0, NEXP) as e:
                    it = r * NEXP + e
                    order = [0]

                    def lstep(ins):
                        order[0] += 1
                        ins.then_inc(dve_loop, 1)
                        dve.wait_ge(dve_loop, (it + 1) * NDVE + order[0])

                    dve.wait_ge(*lat("m_gathered", it, 0))
                    for b, (t0, n) in enumerate(BLK):
                        lstep(ve.tensor_scalar(Pm[0:n, b, :], iota[0:n, :], rank[0:n, b, bass.ds(e, 1)], None,
                                               ALU.is_equal))
                    for b, (t0, n) in enumerate(BLK):
                        ins = ve.tensor_scalar(Pc[0:n, b, :], Pm[0:n, b, :], comb[0:n, b, bass.ds(e, 1)], None, ALU.mult)
                        if b < 2:
                            lstep(ins)
                        else:
                            ins.then_inc(*lup("m_sel"))
                            dve.wait_ge(*lat("m_sel", it, 1))
                    dve.wait_ge(*lat("m_scattered", it, 0))
                    dve.wait_ge(*lat("m_gathered", it, 3))
                    ve.tensor_copy(Cm, bank[2][:, 0:T]).then_inc(*lup("m_weights"))
                    for c in range(NCH):
                        x = ex[c % 2]
                        dve.wait_ge(*lat("m_exp", it, c + 1))
                        lstep(ve.tensor_scalar(x, x, 1.0, None, ALU.add))
                        lstep(ve.reciprocal(x, x))
                        lstep(tt(x, x, bank[c % 2][:, :], ALU.mult))
                        dve.wait_ge(*lat("m_turned", it, max(c - 1, 0)))
                        dve.wait_ge(*lat("m_gu", it, 2 * c + 2))
                        tt(hid[c % 2], x, bank[2 + c % 2][:, :], ALU.mult).then_inc(*lup("m_hid"))
                    for m, q in enumerate((7, 4, 0, 1, 2, 3, 7, 4)):
                        dve.wait_ge(*lat("m_scattered", it, m + 1))
                        tt(xT[:, m, :], xT[:, m, :], bank[q][:, 0:T], ALU.add).then_inc(*lup("m_added"))
                    assert order[0] == NDVE, order
                dve.wait_ge(*lat("m_added", r * NEXP + NEXP - 1, 8))
                for b, (t0, n) in enumerate(BLK):
                    ve.tensor_scalar(rank[0:n, b, :], rank[0:n, b, :], float(-P), None, ALU.add
                                     ).then_inc(rank_moved, 1)
                dve.wait_ge(rank_moved, r * 3 + 3)

        assert raised == {k: DEPTH * v for k, v in PER.items()}, {k: v for k, v in raised.items() if v != DEPTH * PER[k]}
        assert loop_raised == LOOP, loop_raised


_INS = ['x_prompt', 'x_sample', 'state_hgrn', 'state_ssm', 'state_conv', 'cache_kv_w128', 'cache_kv_w512',
        'cache_kv_w2048', 'w_in', 'mix_norm', 'hgrn_lb_logits', 'hgrn_norm', 'ssm_conv_w', 'ssm_conv_b',
        'ssm_dt_bias', 'ssm_a_log', 'ssm_d', 'ssm_norm', 'att_q_norm', 'att_k_norm', 'w_out_hgrn', 'w_out_ssm',
        'w_out_att', 'w_o', 'ffn_norm', 'w_ffn_up', 'w_ffn_down', 'w_router', 'w_moe_up', 'w_moe_down']
_OUTS = [(1, 256, 1024), (8, 4, 1024), (2, 1, 4, 128, 128), (2, 1, 8, 64, 128), (2, 1, 3, 1024),
         (2, 1, 128, 2, 4, 64), (2, 1, 256, 2, 4, 64), (2, 1, 256, 2, 4, 64),
         (2, 8, 4, 128, 128), (2, 8, 8, 64, 128), (2, 8, 3, 1024),
         (2, 8, 4, 2, 4, 64), (2, 8, 4, 2, 4, 64), (2, 8, 4, 2, 4, 64)]


def kernel(**inputs):
    import numpy as _np
    import concourse.bacc as _bacc
    from concourse import mybir as _mybir
    from concourse.bass_utils import run_bass_kernel_spmd as _run

    nc = _bacc.Bacc("TRN2", target_bir_lowering=False, num_devices=1)
    arrays, args = {}, []
    for name in _INS:
        a = _np.ascontiguousarray(inputs[name])
        arrays[f"in_{name}_dram"] = a
        args.append(nc.dram_tensor(f"in_{name}_dram", a.shape, _mybir.dt.from_np(a.dtype), kind="ExternalInput").ap())
    for i, shape in enumerate(_OUTS):
        args.append(nc.dram_tensor(f"out_{i}_dram", shape, _mybir.dt.float32, kind="ExternalOutput").ap())
    hybrid_decoder(nc, *args)
    r = _run(nc, [arrays], core_ids=[0])
    return tuple(r.results[0][f"out_{i}_dram"] for i in range(len(_OUTS)))
```

```python
from contextlib import ExitStack

import concourse.bass as bass
from concourse import mybir

F32 = mybir.dt.float32
I32 = mybir.dt.int32
U32 = mybir.dt.uint32
ALU = mybir.AluOpType
ACT = mybir.ActivationFunctionType
AX = mybir.AxisListType

P = 128
D = 1024
KT = D // P
TP, DB, DS = 256, 8, 4
TS = DB * DS
T = TP + TS
DEPTH = 2
HH, SH, AH = 4, 8, 4
AG = 3
CONV = 4
TAIL = CONV - 1
NEXP = 8
FF = 11 * D // 4
FE = 7 * D // 2
NDT = FF // P
EPS = 1e-6
NEG = -1e30
LN_MIN = 1e-19
SCALE = 64 ** -0.5
OFF_SSM = 4 * HH * P
OFF_DT = OFF_SSM + 512 + 1024
OFF_ATT = OFF_DT + SH
N_IN = OFF_ATT + AG * 3 * 256 + 3 * D
BLK = [(0, 128), (128, 128), (256, 32)]
LEVELS = [1, 2, 4, 8, 16, 32, 64, 128]
PADW = TAIL + TP
PADT = PADW + DB * (TAIL + DS)
CW = PADT - TAIL
SLAB = 2048
RING = 4
ESLAB = 4096
MRING = 7
CAP = P
NCH = FE // 512

V_MIX, V_FFN, V_CW, V_CB, V_SN, V_HN, V_LB, V_QN, V_KN, V_N = 0, 8, 16, 48, 56, 60, 61, 65, 68, 71

NS_HG, NS_SSM, NS_AG, NS_OUT, NS_WO = 8, 6, 21, 5, 4
NS_MIX = NS_HG + NS_SSM + NS_AG + NS_OUT + NS_WO
NS_DUP, NS_DDN = NDT, 2 * KT
NS_DENSE = NS_DUP + NS_DDN
SIG_MAX = 2.0 ** 62

PER = dict(
    x_squared=4, rstd_ready=2, h_ready=16,
    hg_exp=3, hg_plus=3, hg_sig=3, hg_clamped=1, hg_log=1, hg_gated=1, hg_zeroed=1,
    lvl_dist=8, lvl_decay=8, lvl_q=8, lvl_k=8,
    kd_dist=1, kd_decay=1, kd_ready=1, hg_tail=1, qe_ready=1,
    vexp_ready=4, s0_scaled=4, hg_osq=1, hg_rstd=1, hg_done=1,
    conv_done=1, conv_exp=1, conv_plus=1, conv_sig=1, z_plus=1, z_sig=1, gate_plus=12, gate_sig=12, xs_ready=1, conv_tail=1, z_exp=1, z_gated=1,
    dt_neg=1, dt_log=1, dt_cum=1, dt_exp=1, dt_ready=1,
    w_exp=8, w_ready=8, bexp_ready=2, h0_scaled=4, ep_ready=4,
    ssm_y=1, ssm_ysq=1, ssm_rstd=1, ssm_done=1,
    qk_sq=3, qk_rstd=3, qk_ready=3, sc_neg=8, sc_exp=8, sc_ready=8,
    qx_ready=1, ss_neg=1, ss_exp=1, ss_ready=1, mixed_ready=8,
)


def hybrid_decoder(nc, x_prompt, x_sample, state_hgrn, state_ssm, state_conv, cache_kv_w128, cache_kv_w512,
                   cache_kv_w2048, w_in, mix_norm, hgrn_lb_logits, hgrn_norm, ssm_conv_w, ssm_conv_b,
                   ssm_dt_bias, ssm_a_log, ssm_d, ssm_norm, att_q_norm, att_k_norm, w_out_hgrn, w_out_ssm,
                   w_out_att, w_o, ffn_norm, w_ffn_up, w_ffn_down, w_router, w_moe_up, w_moe_down,
                   y_prompt, y_sample, p_hgrn, p_ssm, p_conv, p_kv128, p_kv512, p_kv2048,
                   s_hgrn, s_ssm, s_conv, s_kv128, s_kv512, s_kv2048):
    ctx = ExitStack()
    with ctx:
        def sb(name, shape, dt=F32):
            return ctx.enter_context(nc.sbuf_tensor(name, shape, dt))

        def sem(name):
            return ctx.enter_context(nc.semaphore(name))

        ring = sb("ring", [P, RING * SLAB])
        over = sb("over", [P, 4 * ESLAB])
        slot = [ring[:, i * SLAB:(i + 1) * SLAB] for i in range(RING)]
        xT = sb("xT", [P, KT, T])
        hT = sb("hT", [P, KT, T])
        arena = sb("arena", [P, 14720 + ESLAB])
        eslot = [over[:, i * ESLAB:(i + 1) * ESLAB] for i in range(4)] + [arena[:, 14720:14720 + ESLAB]] + \
                [ring[:, i * ESLAB:(i + 1) * ESLAB] for i in range(2)]

        def view(base, at, *shape):
            n = 1
            for s in shape:
                n *= s
            v = base[:, at:at + n]
            if len(shape) == 2:
                v = v.rearrange("p (a b) -> p a b", a=shape[0])
            elif len(shape) == 3:
                v = v.rearrange("p (a b c) -> p a b c", a=shape[0], b=shape[1])
            return v

        att = view(over, 0, 18, T)
        gates = view(over, 18 * T, 24, T)
        hgp = view(over, 18 * T, 16, T)
        yall = view(over, 42 * T, 10, T)
        small = view(over, 52 * T, 1400)
        zT = view(arena, 0, 4, T)
        xpad = view(arena, 4 * T, 8, PADT)
        A0 = 4 * T + 8 * PADT
        G = view(arena, A0, 4, T)
        dist = view(arena, A0 + 4 * T, 4, T)
        qt = view(arena, A0 + 8 * T, 4, T)
        kt = view(arena, A0 + 12 * T, 4, T)
        S0 = [view(arena, A0 + 8 * T, DB, P), view(arena, A0 + 8 * T + 1024, DB, P)]
        A1 = A0 + 16 * T
        a00 = view(arena, A1, HH, P)
        a01 = view(arena, A1 + 512, HH, P)
        a11 = view(arena, A1 + 1024, HH, P)
        aS = view(arena, A1 + 1536, HH, TS)
        vtok = view(arena, A1 + 1664, 3, 512)
        kdtok = view(arena, A1 + 3200, 3, 512)
        vexp = view(arena, A1 + 4736, DB, P)
        assert A1 + 4736 + 1024 <= 14720
        taild = view(arena, 18520, HH, DB, DS)
        qe = view(arena, 18392, HH, TS)
        st_hg = view(arena, A0, HH, P)
        o_hg, osq, o_rstd = dist, view(arena, A1, HH, T), view(arena, A1 + 1664, HH, T)
        cv = view(arena, 14720, 8, PADT)
        zexp = view(arena, 14720 + 8 * PADT, 4, T)
        cve = view(over, 42 * T, 8, PADT)
        xs = view(arena, 4 * T, 8, T)
        xdt = view(arena, A0, 3, 512)
        xw = view(arena, A0 + 1536, 3, 512)
        btok = view(arena, A0 + 3072, 3, 256)
        wb = [view(arena, A0 + 3840 + 416 * i, 416) for i in range(2)]
        A2 = A0 + 3840 + 1152
        cbm = view(arena, A2, 2, 416)
        dts = view(arena, A2 + 832, 5, T)
        yT = view(arena, A2 + 832 + 5 * T, 4, T)
        h0 = [view(arena, A2 + 832 + 9 * T + 1024 * i, DB, P) for i in range(2)]
        A3 = A2 + 832 + 9 * T + 2048
        assert A3 <= 14720
        h0T = [view(arena, 14720 + 1024 * i, DB, P) for i in range(2)]
        ssm_st = view(arena, 14720 + 2048, 512)
        bexp = [view(small, 0, DB, P), view(arena, 14720 + 2560, DB, P)]
        crows = small[:, 0:1024]
        ctail = view(small, 1024, 8, 27)
        tokc = view(small, 1312, 3, 3, SH)
        cve4 = view(arena, A0 + 3840, 4, T)
        ff = view(arena, 0, NDT, T)
        ffe = [view(arena, (NDT + i) * T, T) for i in range(4)]
        kvtok = view(arena, 0, 3, AG, 512)
        kb = [view(arena, 4608 + 2304 * i, 9, 256) for i in range(2)]
        KTb = view(arena, 9216, 1792)
        kv_rows = view(arena, 11008, 416)
        sTs = view(arena, 11424, 3, P)
        sTn = view(arena, 11808, 3, P)
        qx = view(arena, 12192, AG, 2, 64)
        qsq = yall[:, 4:8, :]
        yrows = view(arena, 0, 3, D)
        htok = view(arena, 0, 3, D)
        Pm = view(arena, 3072, 3, CAP)
        Pc = view(arena, 3456, 3, CAP)
        Cm = arena[0:CAP, 3840:3840 + T]
        hg = view(arena, 4128, KT, CAP)
        ex = [arena[0:CAP, 5152 + 512 * i:5664 + 512 * i] for i in range(2)]
        hid = [arena[0:CAP, 6176 + 512 * i:6688 + 512 * i] for i in range(2)]
        hidT = [view(arena, 7200 + 512 * i, 4, CAP) for i in range(2)]
        yb = arena[0:CAP, 8224:9248]
        lg = view(arena, 9248, 3, NEXP)
        top = view(arena, 9272, 3, NEXP)
        topi = view(arena, 9296, 3, NEXP).bitcast(U32)
        topf = view(arena, 9320, 3, NEXP)
        pick = view(arena, 9344, 2, NEXP)
        chosen = view(arena, 9360, 3, NEXP)
        comb = view(arena, 9384, 3, NEXP + 1)
        rank = view(arena, 9412, 3, NEXP + 1)
        rw = view(arena, 9440, 3, 4)
        chosenT = arena[0:NEXP, 9452:9452 + T]
        placeT = arena[0:NEXP, 9740:9740 + T]
        rcount = arena[0:1, 10028:10032]
        rounds = arena[0:1, 10096:10097].bitcast(I32)
        wr = view(arena, 10032, KT, NEXP)
        sc = [view(arena, 12576 + 768 * i, 2, 384) for i in range(2)]
        PT = [view(arena, 14112 + 768 * i, 2, 384) for i in range(2)]

        ident = sb("ident", [P, P])
        ones = sb("ones", [P, P])
        pairs = sb("pairs", [P, P])
        lmask = sb("lmask", [P, 7, P])
        causal = sb("causal", [P, P])
        scausal = sb("scausal", [TS, DB, DS])
        seqm = sb("seqm", [TS, DB])
        amask = sb("amask", [P, 2, 3 * P])
        smask = sb("smask", [P, 416])
        reset = sb("reset", [P, T])
        iota = sb("iota", [P, P])
        sel = sb("sel", [SH, SH, P])
        sel2 = sb("sel2", [SH, 4, P])
        vecs = sb("vecs", [P, DEPTH, V_N])
        lb = sb("lb", [P, DEPTH, 2, 4])
        hv = sb("hv", [SH, DEPTH, 3])
        wdt = sb("wdt", [P, KT, SH])
        dskip = sb("dskip", [P, DEPTH, 4])
        ep = sb("ep", [P, 4, TS])
        col = sb("col", [P, 40])
        eps = sb("eps", [P, 1])
        lbe = sb("lbe", [P, DEPTH, 4])
        rstd = arena[:, 14400:14400 + T]
        bank = [ctx.enter_context(nc.psum_tensor(f"bank{i}", [P, 512], F32)) for i in range(8)]

        signals = {name: sem(name) for name in PER}
        raised = dict.fromkeys(PER, 0)

        def at(name, L, k=1):
            return signals[name], L * PER[name] + k

        def up(name):
            raised[name] += 1
            return signals[name], 1

        bank_filled = [sem(f"bank_filled{i}") for i in range(8)]
        bank_drained = [sem(f"bank_drained{i}") for i in range(8)]
        slab_in = [sem(f"slab_in{i}") for i in range(RING)]
        st_out = sem("st_out")
        ident_ready, consts_ready, vecs_in, x_in = map(sem, ("ident_ready", "consts_ready", "vecs_in", "x_in"))
        lb_ready, wdt_in, cstate_in, stored = map(sem, ("lb_ready", "wdt_in", "cstate_in", "stored"))
        s0_in = [sem(f"s0_in{i}") for i in range(2)]
        h0_in = [sem(f"h0_in{i}") for i in range(2)]
        conv_out = [0] * DEPTH
        v_used, up_exp, up_plus, up_sig, a_ready, lb_exp = map(
            sem, ("v_used", "up_exp", "up_plus", "up_sig", "a_ready", "lb_exp"))
        stores = [0]
        k_in = [sem(f"k_in{i}") for i in range(2)]
        act_order, dve_order, pool_order = sem("act_order"), sem("dve_order"), sem("pool_order")

        jobs, fills = {}, [0] * 8

        def job(key, b):
            assert key not in jobs, key
            jobs[key] = (b, fills[b])
            fills[b] += 1

        acc_n = [0]

        def acc_job(key):
            job(key, 5 + acc_n[0] % 3)
            acc_n[0] += 1

        def level_banks(i):
            return (0, 1, 2) if i % 2 == 0 else (3, 4, 2)

        def level_end(L, i):
            return ("lvl", L, i, 0 if i == 7 else 2 if LEVELS[i] < DS else 1)

        def plan_mixer(L):
            job(("norm", L, 0), 0)
            for t in range(16):
                acc_job(("proj", L, t))
            for b in range(3):
                job(("vtok", L, b), 1 + b)
            job(("cstate", L), 4)
            for t in range(16, 28):
                acc_job(("proj", L, t))
            acc_job(("dt", L))
            for s in range(NS_AG):
                for i in range(2):
                    acc_job(("proj", L, 28 + 2 * s + i))
                    h = 2 * (s - 14) + i
                    if 0 <= h < SH:
                        job(("wdecay", L, h), h % 2)
                    if 0 < h <= SH and (h - 1) % 2 == 0:
                        job(("ssm_y", L, (h - 1) // 2), 2 + (h - 1) // 2 % 2)
                if s < 8:
                    b = level_banks(s)
                    job(("lvl", L, s, 0), b[0])
                    if s < 7:
                        job(("lvl", L, s, 1), b[1])
                    if LEVELS[s] < DS:
                        job(("lvl", L, s, 2), b[2])
                if s == 0:
                    for k in range(3):
                        job(("lvl", L, "same", k), (3, 4, 2)[k])
                if s == 7:
                    for b in range(3):
                        job(("kdtok", L, b), b)
                    job(("hg_st", L), 3)
                if 8 <= s < 12:
                    h = s - 8
                    job(("hg_o", L, h), h % 2)
                    job(("hg_s", L, h, 0), 2)
                    job(("hg_s", L, h, 1), 3)
                if 9 <= s < 12:
                    for k in range(4):
                        job(("qk_m", L, s - 9, k), (4, 0, 4, 1)[k])
                if s == 12:
                    for h in range(HH):
                        job(("hg_m", L, h), h)
                    job(("ctail", L, 0), 4)
                    job(("ctail", L, 1), 0)
                if s == 13:
                    job(("tokc", L), 2)
                    for b in range(3):
                        job(("xtok", L, b), 3 + b % 2)
                    for b in range(3):
                        job(("btok", L, b), b)
                    job(("cb", L, 0), 3)
                    job(("cb", L, 1), 4)
                if s == 18:
                    job(("ssm_st", L), 0)
                if s >= 19:
                    for j in ((0, 1) if s == 19 else (2, 3)):
                        job(("h0T", L, j, 0), 1)
                        job(("h0T", L, j, 1), 2)
                        job(("inter", L, j), 3)
                        job(("ssm_s", L, j, 0), 4)
                        job(("ssm_s", L, j, 1), 0)
            job(("ssm_m", L), 1)
            for g in range(AG):
                for b in range(3):
                    job(("kvtok", L, g, b), (3 * g + b) % 5)
            for n in range(9):
                if n < 8:
                    for k in range(n % 2 + 1):
                        job(("sc", L, n, k), k)
                    if n == 0:
                        job(("sS", L), 7)
                    for k in range(4):
                        job(("kT", L, n, k), 5 + k % 2)
                if n > 0:
                    for k in range((n - 1) % 2 + 1):
                        job(("pt", L, n - 1, k), 2 + k)
                    if (n - 1) % 4 == 0:
                        job(("att_o", L, (n - 1) // 4), 4)
            job(("sN", L), 1)
            job(("rows", L), 2)
            for m in range(4):
                acc_job(("out", L, 0, m))
            job(("pS", L), 3)
            job(("pN", L), 4)
            for m in range(4, 8):
                acc_job(("out", L, 0, m))
            job(("oT", L), 0)
            for br in (1, 2):
                for m in range(KT):
                    acc_job(("out", L, br, m))
            for m in range(KT):
                acc_job(("wo", L, m))

        def plan_dense(L):
            job(("norm", L, 1), 0)
            for s in range(NS_DUP):
                for t in range(2):
                    acc_job(("up", L, s, t))
            for m in range(KT):
                acc_job(("down", L, m))

        for b in range(3):
            job(("xin", b, 0), 2 * b % 4)
            job(("xin", b, 1), 2 * b % 4 + 1)
        for L in range(DEPTH):
            job(("vecs", L), 4)
        for L in range(DEPTH):
            job(("dskip", L), 4)
        for L in range(DEPTH):
            plan_mixer(L)
            if L == 0:
                plan_dense(L)
        job(("norm", 1, 1), 0)
        for k in range(6):
            job(("htok", k // 2, k % 2), 1 + k % 4)
        job(("logits", 0), 5)
        job(("choice", 0), 6)
        job(("place", 0), 7)
        job(("count", 0), 5)
        for b in range(3):
            job(("y", b, 0), 2 * b % 4)
            job(("y", b, 1), 2 * b % 4 + 1)

        def filled(key):
            b, n = jobs[key]
            return bank_filled[b], n + 1

        def drained(key):
            b, n = jobs[key]
            return bank_drained[b], n + 1

        def psum(key):
            return bank[jobs[key][0]]

        slabs = []
        last_use = []
        slab_dmas, in_slot = [], [0] * RING

        def rows_of(w, r0, nr, c0, nc_):
            return w[r0 * P:(r0 + nr) * P, c0:c0 + nc_].rearrange("(k p) n -> p k n", p=P)

        def add_slab(last, *parts):
            in_slot[len(slabs) % RING] += len(parts)
            slab_dmas.append(in_slot[len(slabs) % RING])
            slabs.append(parts)
            last_use.append(last)

        def plan_slabs(L):
            for s in range(NS_HG + NS_SSM):
                add_slab(("proj", L, 2 * s + 1), (0, rows_of(w_in[L], 0, KT, 256 * s, 256)))
            for s in range(NS_AG):
                add_slab(("proj", L, 29 + 2 * s), (0, rows_of(w_in[L], 0, KT, OFF_ATT + 256 * s, 256)))
            for br, w in enumerate((w_out_hgrn, w_out_ssm)):
                for s in range(2):
                    add_slab(("out", L, br, 4 * s + 3), (0, rows_of(w[L], 0, 4, 512 * s, 512)))
            add_slab(("out", L, 2, KT - 1), (0, rows_of(w_out_att[L], 0, 2, 0, D)))
            for s in range(NS_WO):
                add_slab(("wo", L, 2 * s + 1), (0, rows_of(w_o[L], 0, KT, 256 * s, 256)))
            if L == 0:
                for s in range(NS_DUP):
                    add_slab(("up", L, s, 1), (0, rows_of(w_ffn_up[L], 0, KT, P * s, P)),
                             (KT * P, rows_of(w_ffn_up[L], 0, KT, FF + P * s, P)))
                for s in range(NS_DDN):
                    h = NDT // 2
                    add_slab(("down", L, s // 2), (0, rows_of(w_ffn_down[L], h * (s % 2), h, P * (s // 2), P)))

        for L in range(DEPTH):
            plan_slabs(L)
        first_slab = [0, NS_MIX + NS_DENSE]

        def slab(n, nr, w):
            return slot[n % RING][:, 0:nr * w].rearrange("p (k n) -> p k n", k=nr)

        def tail4(v):
            return v.rearrange("p (b i) -> p b i", i=DS)

        def load_rounds(eng):
            eng.wait_ge(rounds_ready, 1)
            return eng.value_load(rounds, min_val=1, max_val=-(-T // CAP))

        block = ctx.enter_context(nc.Block())

        LOOP = dict(m_sel=1, m_gathered=2, m_hg=2, m_turned=1, m_weights=1, m_scattered=8, m_added=8,
                    m_gu=14, m_exp=7, m_hid=7, m_hidden=7, m_hidT=7, m_down=7, m_y=2)
        loop_signals = {name: sem(name) for name in LOOP}
        loop_raised = dict.fromkeys(LOOP, 0)
        w_router_in, rounds_ready, rank_moved, dve_loop, chosen_exp, chosen_exped, chosen_ready, places_ready = map(
            sem, ("w_router_in", "rounds_ready", "rank_moved", "dve_loop", "chosen_exp", "chosen_exped",
                  "chosen_ready", "places_ready"))
        NSEL = 5
        NDVE = NSEL + 3 * NCH

        def lat(name, it, k):
            return loop_signals[name], (it + 1) * LOOP[name] + k

        def lup(name):
            loop_raised[name] += 1
            return loop_signals[name], 1

        def advance(eng, *names):
            for name in names:
                eng.sem_inc(loop_signals[name], LOOP[name])

        eslabs = []
        for c in range(NCH + 1):
            if c < NCH:
                eslabs += [("g", c), ("u", c)]
            if c > 0:
                eslabs.append(("d", c - 1))
        assert len(eslabs) % MRING == 0
        PERSLOT = len(eslabs) // MRING
        slab_here = [sem(f"slab_here{i}") for i in range(MRING)]

        def eslab_in(it, n):
            return slab_here[n % MRING], 32 * (it * PERSLOT + n // MRING + 1)

        def eslab_used(it, n):
            kind, c = eslabs[n]
            if kind == "d":
                return lat("m_down", it, c + 1)
            return lat("m_gu", it, 2 * c + (1 if kind == "g" else 2))

        @block.sync
        def _(sp):
            issued = [0]

            def weights_until(n_end):
                for n in range(issued[0], n_end):
                    if n >= RING:
                        sp.wait_ge(*filled(last_use[n - RING]))
                    for c0, src in slabs[n]:
                        k, w = src.shape[1], src.shape[2]
                        sp.dma_start(slot[n % RING][:, c0:c0 + k * w].rearrange("p (k n) -> p k n", k=k),
                                     src).then_inc(slab_in[n % RING], 16)
                issued[0] = max(issued[0], n_end)

            def store(dst, src):
                sp.dma_start(dst, src).then_inc(stored, 16)
                stores[0] += 1

            def load_s0(L, h):
                sp.dma_start(S0[h % 2], state_hgrn[L, :, h].rearrange("b d v -> d b v")).then_inc(s0_in[h % 2], 16)

            def load_h0(L, j):
                sp.dma_start(h0[j % 2], state_ssm[L, :, 2 * j:2 * j + 2].rearrange("b h p n -> (h p) b n")
                             ).then_inc(h0_in[j % 2], 16)

            def load_cache(L, which, b):
                dst = kb[b % 2]
                c128 = cache_kv_w128[L, b].rearrange("w two h d -> w two (h d)")
                c512 = cache_kv_w512[L, b].rearrange("(m r) two h d -> m r two (h d)", r=4)
                c2048 = cache_kv_w2048[L, b].rearrange("(m r) two h d -> m r two (h d)", r=16)
                sp.dma_start(dst[:, 0, :], c128[:, which, :]).then_inc(k_in[b % 2], 16)
                sp.dma_start(dst[:, 1:5, :], c512[:, :, which, :]).then_inc(k_in[b % 2], 16)
                sp.dma_start(dst[0:64, 5:9, :], c2048[:, 0:4, which, :]).then_inc(k_in[b % 2], 16)

            for b, (t0, n) in enumerate(BLK):
                src = x_prompt[0, t0:t0 + n, :] if t0 < TP else x_sample.rearrange("b i d -> (b i) d")
                sp.dma_start(arena[0:n, b * D:(b + 1) * D], src).then_inc(x_in, 16)
            for L in range(DEPTH):
                vr = arena[:, 3 * D + P * L:3 * D + P * L + P]
                rows = [(V_MIX, mix_norm[L].rearrange("(a p) -> a p", p=P)),
                        (V_FFN, ffn_norm[L].rearrange("(a p) -> a p", p=P)),
                        (V_CW, ssm_conv_w[L].rearrange("j (a p) -> (j a) p", p=P)),
                        (V_CB, ssm_conv_b[L].rearrange("(a p) -> a p", p=P)),
                        (V_SN, ssm_norm[L].rearrange("(a p) -> a p", p=P)),
                        (V_HN, hgrn_norm[L:L + 1, :]),
                        (V_LB, hgrn_lb_logits[L].rearrange("(a p) -> a p", p=P))]
                for r, src in rows:
                    sp.dma_start(vr[r:r + src.shape[0], :], src).then_inc(vecs_in, 16)
                for r, src in ((V_QN, att_q_norm[L]), (V_KN, att_k_norm[L])):
                    for e in range(2):
                        sp.dma_start(vr[r:r + AG, 64 * e:64 * e + 64], src).then_inc(vecs_in, 16)
                for k, src in enumerate((ssm_dt_bias, ssm_a_log, ssm_d)):
                    sp.dma_start(hv[:, L, k:k + 1], src[L].rearrange("(h a) -> h a", a=1)).then_inc(vecs_in, 16)

            for L in range(DEPTH):
                ag = first_slab[L] + NS_HG + NS_SSM
                weights_until(first_slab[L] + RING)
                if L > 0:
                    sp.wait_ge(*filled(("dt", L - 1)))
                    sp.wait_ge(stored, 16 * stores[0])
                    sp.wait_ge(*filled(("ssm_s", L - 1, 3, 1)))
                sp.dma_start(wdt[:, :, :], w_in[L].rearrange("(k p) n -> p k n", p=P)[:, :, OFF_DT:OFF_DT + SH]
                             ).then_inc(wdt_in, 16)
                sp.dma_start(crows[0:DB * TAIL, :], state_conv[L].rearrange("b j c -> (b j) c")
                             ).then_inc(cstate_in, 16)
                weights_until(ag + 7 + RING + 1)
                sp.wait_ge(*filled(("kdtok", L, 2)))
                load_s0(L, 0)
                load_s0(L, 1)
                for h in range(HH):
                    weights_until(ag + 8 + h + RING + 1)
                    sp.wait_ge(*drained(("hg_s", L, h, 1)))
                    sp.dma_start(s_hgrn[L, :, h].rearrange("b d v -> d b v"), S0[h % 2]).then_inc(s0_in[h % 2], 16)
                    if h + 2 < HH:
                        sp.wait_ge(s0_in[h % 2], 16 * (4 * L + 2))
                        load_s0(L, h + 2)
                sp.wait_ge(*drained(("hg_st", L)))
                sp.dma_start(p_hgrn[L, 0].rearrange("h d v -> d h v"), st_hg).then_inc(st_out, 16)
                weights_until(ag + 13 + RING + 1)
                sp.wait_ge(*drained(("ctail", L, 0)))
                sp.wait_ge(*drained(("ctail", L, 1)))
                store(p_conv[L, 0], crows[0:3, :])
                store(s_conv[L].rearrange("b j c -> (b j) c"), crows[32:32 + DB * TAIL, :])
                conv_out[L] = stores[0]
                sp.wait_ge(*at("hg_done", L))
                for i in range(2):
                    sp.wait_ge(s0_in[i], 16 * (4 * L + 4))
                load_h0(L, 0)
                load_h0(L, 1)
                weights_until(ag + 18 + RING + 1)
                sp.wait_ge(*drained(("ssm_st", L)))
                sp.dma_start(p_ssm[L, 0].rearrange("(j e) p n -> (e p) j n", e=2),
                             ssm_st.rearrange("p (j n) -> p j n", j=4)).then_inc(st_out, 16)
                for j in range(4):
                    weights_until(ag + 19 + j // 2 + RING + 1)
                    sp.wait_ge(*drained(("ssm_s", L, j, 1)))
                    sp.dma_start(s_ssm[L, :, 2 * j:2 * j + 2].rearrange("b h p n -> (h p) b n"), h0[j % 2]
                                 ).then_inc(h0_in[j % 2], 16)
                    if j + 2 < 4:
                        sp.wait_ge(h0_in[j % 2], 16 * (4 * L + 2))
                        load_h0(L, j + 2)
                sp.wait_ge(*at("ssm_done", L))
                for i in range(2):
                    sp.wait_ge(h0_in[i], 16 * (4 * L + 4))
                for b in range(DB):
                    if b >= 2:
                        sp.wait_ge(*filled(("kT", L, b - 2, 3)))
                    load_cache(L, 0, b)
                for b in range(2):
                    sp.wait_ge(*filled(("kT", L, 6 + b, 3)))
                    load_cache(L, 1, b)
                for i in range(4, 9):
                    sp.wait_ge(*drained(("kvtok", L, i // 3, i % 3)))
                for g, dst in enumerate((p_kv128, p_kv512, p_kv2048)):
                    for b in range(2):
                        if g == 0 and b == 0:
                            continue
                        r = dst[L, 0].rearrange("w two h d -> w (two h d)")
                        store(r[(b * P if g else 0):(b * P if g else 0) + P, :], kvtok[:, b, g, :])
                for g, dst in enumerate((s_kv128, s_kv512, s_kv2048)):
                    store(dst[L].rearrange("b i two h d -> (b i) (two h d)"), kvtok[0:TS, 2, g, :])
                out0 = ag + NS_AG
                for b in range(2, DB):
                    weights_until(out0 + RING + min(2 + (b > 3) + (b > 6), 4))
                    sp.wait_ge(v_used, L * (DB - 1) + b - 1)
                    load_cache(L, 1, b)
            weights_until(len(slabs))
            sp.wait_ge(*filled(("wo", 1, KT - 1)))
            sp.dma_start(wr, w_router[0].rearrange("(k p) e -> p k e", p=P)).then_inc(w_router_in, 16)
            up_v = w_moe_up[0].rearrange("e (k p) n -> p e k n", p=P)
            down_v = w_moe_down[0].rearrange("e (k p) n -> p e k n", p=P)
            nr = load_rounds(sp)
            with sp.Fori(0, nr) as r:
                with sp.Fori(0, NEXP) as e:
                    it = r * NEXP + e
                    for n, (kind, c) in enumerate(eslabs):
                        if n >= MRING:
                            sp.wait_ge(*eslab_used(it, n - MRING))
                        else:
                            sp.wait_ge(*eslab_used(it - 1, n - MRING + len(eslabs)))
                        q = eslot[n % MRING]
                        for h in range(2):
                            if kind == "d":
                                dst = q[:, 2 * h * D:(2 * h + 2) * D].rearrange("p (k n) -> p k n", k=2)
                                src = down_v[:, e, 4 * c + 2 * h:4 * c + 2 * h + 2, :]
                            else:
                                col0 = 512 * c + (FE if kind == "u" else 0)
                                dst = q[:, 2048 * h:2048 * h + 2048].rearrange("p (k n) -> p k n", k=4)
                                src = up_v[:, e, 4 * h:4 * h + 4, col0:col0 + 512]
                            sp.dma_start(dst, src).then_inc(slab_here[n % MRING], 16)

            for b, (t0, n) in enumerate(BLK):
                dst = y_prompt[0, t0:t0 + n, :] if t0 < TP else y_sample.rearrange("b i d -> (b i) d")
                for k in range(2):
                    sp.wait_ge(*drained(("y", b, k)))
                store(dst, yrows[0:n, b, :])
            sp.wait_ge(stored, 16 * stores[0])
            sp.wait_ge(st_out, 16 * 2 * DEPTH)
            for i in range(2):
                sp.wait_ge(s0_in[i], 16 * 4 * DEPTH)
                sp.wait_ge(h0_in[i], 16 * 4 * DEPTH)

        @block.gpsimd
        def _(pool):
            count = [0]

            def step(ins):
                count[0] += 1
                ins.then_inc(pool_order, 1)
                pool.wait_ge(pool_order, count[0])

            def say(ins, name, L, k=1):
                ins.then_inc(*up(name))
                pool.wait_ge(*at(name, L, k))

            gp = nc.gpsimd
            step(gp.memset(ident[:, :], 0.0))
            gp.affine_select(out=ident[:, :], in_=ident[:, :], compare_op=ALU.not_equal, fill=1.0, base=0,
                             pattern=[[-1, P]], channel_multiplier=1).then_inc(ident_ready, 1)
            pool.wait_ge(ident_ready, 1)
            step(gp.memset(ones[:, :], 1.0))
            step(gp.memset(eps[:, :], EPS))
            step(gp.memset(pairs[:, :], 0.0))
            step(gp.memset(pairs[0:64, 0:64], 1.0))
            step(gp.memset(pairs[64:128, 64:128], 1.0))
            step(gp.memset(lmask[:, :, :], 0.0))
            for i, h in enumerate(LEVELS[:7]):
                v = lmask[:, i, :].rearrange("p (n w) -> p n w", w=2 * h)[:, :, h:2 * h]
                step(gp.memset(v, 1.0))
                step(gp.affine_select(out=v, in_=v, compare_op=ALU.is_ge, fill=0.0, base=0,
                                      pattern=[[-2 * h, P // (2 * h)], [0, h]], channel_multiplier=1))
                step(gp.affine_select(out=v, in_=v, compare_op=ALU.is_ge, fill=0.0, base=h - 1,
                                      pattern=[[2 * h, P // (2 * h)], [0, h]], channel_multiplier=-1))
            step(gp.affine_select(out=causal[:, :], in_=ones[:, :], compare_op=ALU.is_ge, fill=0.0, base=0,
                                  pattern=[[1, P]], channel_multiplier=-1))
            step(gp.memset(seqm[:, :], 1.0))
            step(gp.affine_select(out=seqm[:, :], in_=seqm[:, :], compare_op=ALU.is_ge, fill=0.0, base=0,
                                  pattern=[[-DS, DB]], channel_multiplier=1))
            step(gp.affine_select(out=seqm[:, :], in_=seqm[:, :], compare_op=ALU.is_ge, fill=0.0, base=DS - 1,
                                  pattern=[[DS, DB]], channel_multiplier=-1))
            step(gp.tensor_tensor(scausal[:, :, :], causal[0:TS, 0:TS].rearrange("p (b i) -> p b i", i=DS),
                                  seqm[:, :].unsqueeze(2).to_broadcast([TS, DB, DS]), ALU.mult))
            step(gp.memset(reset[:, :], 1.0))
            step(gp.memset(reset[:, 0:1], 0.0))
            step(gp.memset(reset[:, TP:T:DS], 0.0))
            step(gp.iota(iota[:, :], pattern=[[1, P]], base=0, channel_multiplier=0,
                         allow_small_or_imprecise_dtypes=True))
            step(gp.memset(sel[:, :, :], 0.0))
            step(gp.affine_select(out=sel[:, :, :], in_=sel[:, :, :], compare_op=ALU.not_equal, fill=1.0, base=0,
                                  pattern=[[-1, SH], [0, P]], channel_multiplier=1))
            step(gp.memset(sel2[:, :, :], 0.0))
            v = sel2[:, :, :].rearrange("p j (e c) -> p j e c", e=2)
            step(gp.affine_select(out=v, in_=v, compare_op=ALU.not_equal, fill=1.0, base=0,
                                  pattern=[[-2, 4], [-1, 2], [0, 64]], channel_multiplier=1))
            dI = yall[:, 0:2, 0:P].bitcast(I32)
            step(gp.iota(dI, pattern=[[P, 2], [-1, P]], base=0, channel_multiplier=1))
            pI = yall[:, 2, 0:2].bitcast(I32)
            step(gp.iota(pI, pattern=[[0, 2]], base=0, channel_multiplier=1))
            cI = yall[:, 3, 0:TS].bitcast(I32)
            gp.iota(cI, pattern=[[1, TS]], base=0, channel_multiplier=0).then_inc(consts_ready, 1)

            for L in range(DEPTH):
                if L > 0:
                    pool.wait_ge(*drained(("down", L - 1, KT - 1)))
                else:
                    pool.wait_ge(*filled(("vecs", 1)))
                step(gp.memset(a00[:, :, :], 0.0))
                step(gp.memset(a11[:, :, :], 0.0))
                say(gp.memset(aS[0:TS, :, :], 0.0), "hg_zeroed", L)
                pool.wait_ge(*at("hg_gated", L))
                for i in range(8):
                    pool.wait_ge(*at("lvl_decay", L, i + 1))
                    if i > 0:
                        pool.wait_ge(*filled(level_end(L, i - 1)))
                    w = T if LEVELS[i] <= 16 else TP
                    say(gp.tensor_tensor(kt[:, :, 0:w], hgp[:, 4:8, 0:w], dist[:, :, 0:w], ALU.mult),
                        "lvl_k", L, i + 1)
                pool.wait_ge(*at("kd_decay", L))
                pool.wait_ge(*filled(("lvl", L, 7, 0)))
                say(gp.tensor_tensor(kt[:, :, :], hgp[:, 4:8, :], dist[:, :, :], ALU.mult), "kd_ready", L)
                for h in range(HH):
                    pool.wait_ge(*at("hg_tail", L))
                    pool.wait_ge(*filled(("hg_o", L, h)))
                    pool.wait_ge(s0_in[h % 2], 16 * (4 * L + 2 * (h // 2) + 1))
                    say(gp.tensor_tensor(S0[h % 2], S0[h % 2],
                                         taild[:, h, :, DS - 1:DS].to_broadcast([P, DB, P]), ALU.mult),
                        "s0_scaled", L, h + 1)
                for b in range(3):
                    pool.wait_ge(*drained(("btok", L, b)))
                pool.wait_ge(stored, 16 * conv_out[L])
                pool.wait_ge(*at("conv_sig", L))
                for g in range(2):
                    say(gp.tensor_tensor(bexp[g][0:TS], btok[0:TS, 2, g * P:g * P + P].unsqueeze(1)
                                         .to_broadcast([TS, DB, P]),
                                         seqm[:, :].unsqueeze(2).to_broadcast([TS, DB, P]), ALU.mult),
                        "bexp_ready", L, g + 1)
                for h in range(SH):
                    if h % 4 == 0:
                        pool.wait_ge(*drained(("cb", L, h // 4)))
                    pool.wait_ge(*at("w_exp", L, h + 1))
                    step(gp.tensor_tensor(wb[h % 2][:, 0:384], wb[h % 2][:, 0:384], cbm[:, h // 4, 0:384], ALU.mult))
                    say(gp.tensor_tensor(wb[h % 2][0:TS, 384:416], wb[h % 2][0:TS, 384:416],
                                         cbm[0:TS, h // 4, 384:416], ALU.mult), "w_ready", L, h + 1)
                for j in range(4):
                    pool.wait_ge(*filled(("h0T", L, j, 1)))
                    pool.wait_ge(*at("ep_ready", L, j + 1))
                    say(gp.tensor_tensor(h0[j % 2], h0[j % 2],
                                         tail4(ep[:, j, :])[:, :, DS - 1:DS].to_broadcast([P, DB, P]),
                                         ALU.mult), "h0_scaled", L, j + 1)
                for m in range(KT):
                    for br in range(3):
                        pool.wait_ge(*drained(("out", L, br, m)))
                    step(gp.tensor_tensor(gates[:, m, :], gates[:, m, :], gates[:, 8 + m, :], ALU.add))
                    say(gp.tensor_tensor(gates[:, m, :], gates[:, m, :], gates[:, 16 + m, :], ALU.add),
                        "mixed_ready", L, m + 1)

        @block.tensor
        def _(pe):
            mm = nc.tensor.matmul
            opened = [0] * 8
            n_slab = [0]
            new_h = [None]

            def open_bank(key):
                b, n = jobs[key]
                assert opened[b] == n, key
                opened[b] += 1
                if n > 0:
                    pe.wait_ge(bank_drained[b], n)
                return bank[b]

            def close_bank(ins, key):
                ins.then_inc(bank_filled[jobs[key][0]], 1)

            def put(out, lhsT, rhs, start=True, stop=True):
                return mm(out, lhsT, rhs, start=start, stop=stop, skip_group_check=True)

            def turn(out, in_):
                k, m = in_.shape
                if m == P:
                    return nc.tensor.transpose(out, in_, ident[0:k, 0:k])
                return put(out, in_, ident[0:k, 0:k])

            def take_slab(nr, w):
                n = n_slab[0]
                pe.wait_ge(slab_in[n % RING], 16 * slab_dmas[n])
                return slab(n, nr, w)

            def contract(key, w, c0, nk, src, width=P):
                acc = open_bank(key)
                wait_for_h, new_h[0] = new_h[0], None
                for k in range(nk):
                    if wait_for_h:
                        L, before = wait_for_h
                        pe.wait_ge(*at("h_ready", L, before + k + 1))
                    ins = put(acc[0:width, 0:T], w[:, k, c0:c0 + width], src[:, k, :], k == 0, k == nk - 1)
                return ins

            def proj_slab(L, keys, between=None, nk=KT, src=None):
                w = take_slab(nk, P * len(keys))
                for i, key in enumerate(keys):
                    ins = contract(key, w, P * i, nk, hT if src is None else src)
                    close_bank(ins, key)
                    if between is not None and i < len(keys) - 1:
                        between(i)
                n_slab[0] += 1
                if between is not None:
                    between(len(keys) - 1)

            def mean_over_features(L, which):
                acc = open_bank(("norm", L, which))
                for k in range(KT):
                    if k % 4 == 0:
                        pe.wait_ge(*at("x_squared", L, 2 * which + k // 4 + 1))
                    ins = put(acc[:, 0:T], ones[:, :], hT[:, k, :], k == 0, k == KT - 1)
                close_bank(ins, ("norm", L, which))

            def token_rows(key, src, blk, tiles):
                t0, n = BLK[blk]
                acc = open_bank(key)
                for i, m in enumerate(tiles):
                    ins = turn(acc[0:n, P * i:P * i + P], src[:, m, t0:t0 + n])
                close_bank(ins, key)

            def level(L, i):
                if i == "same":
                    kk, qq = hgp[:, 4:8], hgp[:, 0:4]
                    pe.wait_ge(*at("hg_gated", L))
                else:
                    kk, qq = kt, qt
                    pe.wait_ge(*at("lvl_q", L, i + 1))
                    pe.wait_ge(*at("lvl_k", L, i + 1))
                if i == 7:
                    acc = open_bank(("lvl", L, i, 0))
                    for h in range(HH):
                        ins = put(acc[:, P * h:P * h + P], kk[:, h, 0:P], qq[:, h, P:TP])
                    close_bank(ins, ("lvl", L, i, 0))
                    return
                for b in range(2):
                    acc = open_bank(("lvl", L, i, b))
                    for h in range(HH):
                        ins = put(acc[:, P * h:P * h + P], kk[:, h, P * b:P * b + P], qq[:, h, P * b:P * b + P])
                    if b == 0 or ("lvl", L, i, 2) in jobs:
                        close_bank(ins, ("lvl", L, i, b))
                if ("lvl", L, i, 2) in jobs:
                    acc = open_bank(("lvl", L, i, 2))
                    for h in range(HH):
                        ins = put(acc[0:TS, TS * h:TS * h + TS], kk[:, h, TP:T], qq[:, h, TP:T])
                    close_bank(ins, ("lvl", L, i, 2))
                else:
                    close_bank(ins, ("lvl", L, i, 1))

            def hgrn_tail(L):
                pe.wait_ge(*at("kd_ready", L))
                for b in range(3):
                    token_rows(("kdtok", L, b), kt, b, range(HH))
                acc = open_bank(("hg_st", L))
                for b in range(3):
                    pe.wait_ge(*drained(("kdtok", L, b)))
                for h in range(HH):
                    for b in range(2):
                        ins = put(acc[:, P * h:P * h + P], kdtok[:, b, P * h:P * h + P], vtok[:, b, P * h:P * h + P],
                                  b == 0, b == 1)
                close_bank(ins, ("hg_st", L))

            def hgrn_head(L, h):
                if h == 0:
                    pe.wait_ge(*drained(("lvl", L, 7, 0)))
                    pe.wait_ge(*drained(("lvl", L, 6, 1)))
                    pe.wait_ge(*drained(("lvl", L, 6, 0)))
                    pe.wait_ge(*at("qe_ready", L))
                acc = open_bank(("hg_o", L, h))
                v = vtok[:, :, P * h:P * h + P]
                put(acc[:, 0:P], v[:, 0, :], a00[:, h, :], True, False)
                put(acc[:, P:TP], v[:, 0, :], a01[:, h, :], False, False)
                put(acc[:, P:TP], v[:, 1, :], a11[:, h, :], False, False)
                put(acc[:, TP:T], v[0:TS, 2, :], aS[0:TS, h, :], False, False)
                pe.wait_ge(s0_in[h % 2], 16 * (4 * L + 2 * (h // 2) + 1))
                for b in range(DB):
                    ins = put(acc[:, TP + DS * b:TP + DS * b + DS], S0[h % 2][:, b, :],
                              qe[:, h, DS * b:DS * b + DS], False, b == DB - 1)
                close_bank(ins, ("hg_o", L, h))
                pe.wait_ge(*at("vexp_ready", L, h + 1))
                for k in range(2):
                    acc = open_bank(("hg_s", L, h, k))
                    ins = put(acc[:, :], kdtok[0:TS, 2, P * h:P * h + P],
                              vexp[0:TS, 4 * k:4 * k + 4, :].rearrange("p b v -> p (b v)"))
                    close_bank(ins, ("hg_s", L, h, k))

            def hgrn_means(L):
                pe.wait_ge(*at("hg_osq", L))
                for h in range(HH):
                    acc = open_bank(("hg_m", L, h))
                    close_bank(put(acc[:, 0:T], ones[:, :], osq[:, h, :]), ("hg_m", L, h))

            def conv_tails(L):
                for k in range(2):
                    acc = open_bank(("ctail", L, k))
                    if k == 0:
                        pe.wait_ge(*at("conv_tail", L))
                    for i in range(4):
                        m = 4 * k + i
                        put(acc[0:3, P * i:P * i + P], ctail[:, m, 0:3], ident[:, :])
                        ins = put(acc[32:56, P * i:P * i + P], ctail[:, m, 3:27], ident[:, :])
                    close_bank(ins, ("ctail", L, k))

            def ssd_rows(L):
                acc = open_bank(("tokc", L))
                pe.wait_ge(*at("dt_ready", L))
                for b, (t0, n) in enumerate(BLK):
                    for i, r in enumerate((2, 0, 4)):
                        c = 24 * b + 8 * i
                        ins = turn(acc[0:n, c:c + 8], dts[0:SH, r, t0:t0 + n])
                close_bank(ins, ("tokc", L))
                pe.wait_ge(*at("xs_ready", L))
                for b in range(3):
                    token_rows(("xtok", L, b), xs, b, range(4))
                for b in range(3):
                    token_rows(("btok", L, b), xs, b, (4, 5))
                for g in range(2):
                    acc = open_bank(("cb", L, g))
                    B, C = xs[:, 4 + g, :], xs[:, 6 + g, :]
                    put(acc[:, 0:TP], B[:, 0:P], C[:, 0:TP])
                    put(acc[:, TP:TP + P], B[:, P:TP], C[:, P:TP])
                    close_bank(put(acc[0:TS, 384:416], B[:, TP:T], C[:, TP:T]), ("cb", L, g))

            def ssd_head(L, h):
                acc = open_bank(("wdecay", L, h))
                close_bank(put(acc[:, 0:T], sel[:, h, :], dts[0:SH, 2, :]), ("wdecay", L, h))

            def ssd_y(L, h):
                key = ("ssm_y", L, h // 2)
                acc = open_bank(key) if h % 2 == 0 else psum(key)
                if h == 0:
                    for b in range(3):
                        pe.wait_ge(*drained(("xtok", L, b)))
                pe.wait_ge(*at("w_ready", L, h + 1))
                w, r = wb[h % 2], 64 * (h % 2)
                x = xdt[:, :, 64 * h:64 * h + 64]
                put(acc[r:r + 64, 0:TP], x[:, 0, :], w[:, 0:TP], True, False)
                put(acc[r:r + 64, P:TP], x[:, 1, :], w[:, TP:384], False, False)
                ins = put(acc[r:r + 64, TP:T], x[0:TS, 2, :], w[0:TS, 384:416], False, True)
                if h % 2:
                    close_bank(ins, key)

            def ssd_prompt_state(L):
                acc = open_bank(("ssm_st", L))
                for b in range(3):
                    pe.wait_ge(*drained(("btok", L, b)))
                for j in range(4):
                    for b in range(2):
                        ins = put(acc[:, P * j:P * j + P], xw[:, b, P * j:P * j + P],
                                  btok[:, b, (j // 2) * P:(j // 2) * P + P], b == 0, b == 1)
                close_bank(ins, ("ssm_st", L))

            def ssd_state(L, j):
                pe.wait_ge(h0_in[j % 2], 16 * (4 * L + 2 * (j // 2) + 1))
                for k in range(2):
                    acc = open_bank(("h0T", L, j, k))
                    for b in range(4):
                        ins = turn(acc[:, P * b:P * b + P], h0[j % 2][:, 4 * k + b, :])
                    close_bank(ins, ("h0T", L, j, k))
                acc = open_bank(("inter", L, j))
                put(acc[:, TS:2 * TS], sel2[:, j, :], dts[0:SH, 3, TP:T])
                for k in range(2):
                    pe.wait_ge(*drained(("h0T", L, j, k)))
                for b in range(DB):
                    ins = put(acc[:, DS * b:DS * b + DS], h0T[j % 2][:, b, :],
                              xs[:, 6 + j // 2, TP + DS * b:TP + DS * b + DS])
                close_bank(ins, ("inter", L, j))
                pe.wait_ge(*at("bexp_ready", L, j // 2 + 1))
                for k in range(2):
                    acc = open_bank(("ssm_s", L, j, k))
                    ins = put(acc[:, :], xw[0:TS, 2, P * j:P * j + P],
                              bexp[j // 2][0:TS, 4 * k:4 * k + 4, :].rearrange("p b v -> p (b v)"))
                    close_bank(ins, ("ssm_s", L, j, k))

            def ssd_mean(L):
                acc = open_bank(("ssm_m", L))
                pe.wait_ge(*at("ssm_ysq", L))
                for j in range(4):
                    ins = put(acc[:, 0:T], ones[:, :], cve4[:, j, :], j == 0, j == 3)
                close_bank(ins, ("ssm_m", L))

            def qk_means(L, g):
                for k in range(4):
                    acc = open_bank(("qk_m", L, g, k))
                    if k == 0:
                        pe.wait_ge(*at("qk_sq", L, g + 1))
                    close_bank(put(acc[:, 0:T], pairs[:, :], qsq[:, k, :]), ("qk_m", L, g, k))

            def kv_rows_of(L):
                pe.wait_ge(*at("qk_ready", L, AG))
                for g in range(AG):
                    for b in range(3):
                        token_rows(("kvtok", L, g, b), att, b, range(6 * g + 2, 6 * g + 6))

            def scores(L, n):
                h, tb = n // 2, n % 2
                j, r = h // 2, 64 * (h % 2)
                for k in range(tb + 1):
                    acc = open_bank(("sc", L, n, k))
                    for g in range(AG):
                        ins = put(acc[:, P * g:P * g + P], att[r:r + 64, 6 * g + j, P * tb:P * tb + P],
                                  att[r:r + 64, 6 * g + 2 + j, P * k:P * k + P])
                    close_bank(ins, ("sc", L, n, k))

            def weigh(L, n):
                h, tb = n // 2, n % 2
                j, r = h // 2, 64 * (h % 2)
                pe.wait_ge(*at("sc_ready", L, n + 1))
                for k in range(tb + 1):
                    acc = open_bank(("pt", L, n, k))
                    for g in range(AG):
                        ins = turn(acc[:, P * g:P * g + P], sc[n % 2][:, k, P * g:P * g + P])
                    close_bank(ins, ("pt", L, n, k))
                key = ("att_o", L, j)
                acc = open_bank(key) if n % 4 == 0 else psum(key)
                for k in range(tb + 1):
                    pe.wait_ge(*drained(("pt", L, n, k)))
                    if n == 0 and k == 0:
                        for i in range(4, 9):
                            pe.wait_ge(*drained(("kvtok", L, i // 3, i % 3)))
                    for g in range(AG):
                        ins = put(acc[r:r + 64, P * tb:P * tb + P], kvtok[:, k, g, 256 + 64 * h:256 + 64 * h + 64],
                                  PT[n % 2][:, k, P * g:P * g + P], k == 0 and g == 0, k == tb and g == 2)
                if n % 4 == 3:
                    close_bank(ins, key)

            def sample_keys(L, b):
                if b == 0:
                    sS = open_bank(("sS", L))
                    pe.wait_ge(*at("qx_ready", L))
                sS = psum(("sS", L))
                kk = kb[b % 2]
                pe.wait_ge(k_in[b % 2], 48 * (8 * L + b // 2 + 1))
                for k in range(4):
                    acc = open_bank(("kT", L, b, k))
                    if k == 0:
                        for p in range(2):
                            ins = turn(acc[:, P * p:P * p + P], kk[:, 0, P * p:P * p + P])
                    elif k < 3:
                        for i in range(4):
                            r, p = 2 * (k - 1) + i // 2, i % 2
                            ins = turn(acc[:, P * i:P * i + P], kk[:, 1 + r, P * p:P * p + P])
                    else:
                        for i in range(8):
                            ins = turn(acc[:, 64 * i:64 * i + 64], kk[0:64, 5 + i // 2, P * (i % 2):P * (i % 2) + P])
                    close_bank(ins, ("kT", L, b, k))

            def sample_scores(L, b):
                sS = psum(("sS", L))
                for k in range(4):
                    pe.wait_ge(*drained(("kT", L, b, k)))
                for p in range(2):
                    q = qx[:, :, p, 8 * b:8 * b + 8]
                    c = 16 * b + 8 * p
                    put(sS[:, c:c + 8], KTb[:, P * p:P * p + P], q[:, 0, :])
                    for r in range(4):
                        k0 = 256 + (2 * r + p) * P
                        put(sS[:, P + c + r:P + c + 8:4], KTb[:, k0:k0 + P], q[:, 1, r:8:4])
                        k0 = 1280 + (2 * r + p) * 64
                        ins = put(sS[0:64, 2 * P + c + r:2 * P + c + 8:4], KTb[:, k0:k0 + 64], q[:, 2, r:8:4])
                if b == DB - 1:
                    close_bank(ins, ("sS", L))

            def sample_rows(L):
                acc = open_bank(("sN", L))
                for g in range(AG):
                    for p in range(2):
                        o = acc[0:TS, P * g:P * g + P].rearrange("t (b c) -> t b c", b=DB)[:, :, 8 * p:8 * p + 8]
                        ins = put(o, att[:, 6 * g + 2 + p, TP:T], qx[:, g, p, :])
                close_bank(ins, ("sN", L))
                acc = open_bank(("rows", L))
                pe.wait_ge(*drained(("sS", L)))
                pe.wait_ge(*drained(("sN", L)))
                turn(acc[:, 0:P], sTs[:, 0, :])
                turn(acc[:, P:2 * P], sTs[:, 1, :])
                turn(acc[:, 2 * P:2 * P + 64], sTs[0:64, 2, :])
                for g in range(AG):
                    ins = turn(acc[:, 320 + TS * g:320 + TS * g + TS], sTn[0:TS, g, :])
                close_bank(ins, ("rows", L))

            def sample_weights(L):
                acc = open_bank(("pS", L))
                pe.wait_ge(*at("ss_ready", L))
                turn(acc[:, 0:P], kv_rows[:, 0:P])
                turn(acc[:, P:2 * P], kv_rows[:, P:2 * P])
                close_bank(turn(acc[0:64, 2 * P:3 * P], kv_rows[:, 2 * P:2 * P + 64]), ("pS", L))
                acc = open_bank(("pN", L))
                for g in range(AG):
                    ins = turn(acc[0:TS, P * g:P * g + P], kv_rows[:, 320 + TS * g:320 + TS * g + TS])
                close_bank(ins, ("pN", L))

            def sample_new_values(L):
                oT = open_bank(("oT", L))
                pe.wait_ge(*drained(("pS", L)))
                pe.wait_ge(*drained(("pN", L)))
                for g in range(AG):
                    for p in range(2):
                        pr = sTn[0:TS, g, :].rearrange("t (b c) -> t b c", b=DB)[:, :, 8 * p:8 * p + 8]
                        o = oT[:, 0:P].rearrange("t (b c) -> t b c", b=DB)[:, :, 8 * p:8 * p + 8]
                        put(o, kvtok[0:TS, 2, g, 256 + P * p:256 + P * p + P], pr, g == 0 and p == 0, False)

            def sample_values(L, b):
                oT = psum(("oT", L))
                vv = kb[b % 2]
                pe.wait_ge(k_in[b % 2], 48 * (8 * L + 4 + b // 2 + 1))
                for p in range(2):
                    c = 16 * b + 8 * p
                    put(oT[:, c:c + 8], vv[:, 0, P * p:P * p + P], sTs[:, 0, c:c + 8], False, False)
                    for r in range(4):
                        put(oT[:, c + r:c + 8:4], vv[:, 1 + r, P * p:P * p + P], sTs[:, 1, c + r:c + 8:4],
                            False, False)
                        ins = put(oT[:, c + r:c + 8:4], vv[0:64, 5 + r, P * p:P * p + P],
                                  sTs[0:64, 2, c + r:c + 8:4], False, False)
                if b == DB - 1:
                    close_bank(ins, ("oT", L))
                else:
                    ins.then_inc(v_used, 1)

            def mixer(L):
                mean_over_features(L, 0)
                new_h[0] = (L, 0)
                for s in range(NS_HG):
                    proj_slab(L, [("proj", L, 2 * s + i) for i in range(2)])
                for b in range(3):
                    if b == 0:
                        for t in range(8, 12):
                            pe.wait_ge(*drained(("proj", L, t)))
                    token_rows(("vtok", L, b), hgp, b, range(8, 12))
                acc = open_bank(("cstate", L))
                pe.wait_ge(cstate_in, 16 * (L + 1))
                for m in range(KT):
                    ins = turn(acc[:, 24 * m:24 * m + 24], crows[0:24, P * m:P * m + P])
                close_bank(ins, ("cstate", L))
                for s in range(NS_HG, NS_HG + NS_SSM):
                    proj_slab(L, [("proj", L, 2 * s + i) for i in range(2)])
                pe.wait_ge(wdt_in, 16 * (L + 1))
                close_bank(contract(("dt", L), wdt, 0, KT, hT, SH), ("dt", L))
                for s in range(NS_AG):
                    def between(i):
                        h = 2 * (s - 14) + i
                        if 0 <= h < SH:
                            ssd_head(L, h)
                        if 0 < h <= SH:
                            ssd_y(L, h - 1)
                    proj_slab(L, [("proj", L, 28 + 2 * s + i) for i in range(2)], between)
                    if s < 8:
                        level(L, s)
                    if s == 0:
                        level(L, "same")
                    if s == 7:
                        hgrn_tail(L)
                    if 8 <= s < 12:
                        hgrn_head(L, s - 8)
                    if 9 <= s < 12:
                        qk_means(L, s - 9)
                    if s == 12:
                        hgrn_means(L)
                        conv_tails(L)
                    if s == 13:
                        ssd_rows(L)
                    if s == 18:
                        ssd_prompt_state(L)
                    if s >= 19:
                        for j in ((0, 1) if s == 19 else (2, 3)):
                            ssd_state(L, j)
                ssd_mean(L)
                kv_rows_of(L)
                for n in range(9):
                    if n < 8:
                        scores(L, n)
                        sample_keys(L, n)
                    if n > 0:
                        weigh(L, n - 1)
                    if n < 8:
                        sample_scores(L, n)
                sample_rows(L)

                def out_slab(br, s):
                    nk = 2 if br == 2 else 4
                    w = KT if br == 2 else 4
                    proj_slab(L, [("out", L, br, w * s + i) for i in range(w)], None, nk,
                              yall[:, 4 * br:4 * br + nk, :])
                pe.wait_ge(*at("hg_done", L))
                pe.wait_ge(*at("ssm_done", L))
                out_slab(0, 0)
                sample_weights(L)
                out_slab(0, 1)
                sample_new_values(L)
                for b in range(DB):
                    sample_values(L, b)
                    if b in (2, 5):
                        out_slab(1, b // 3)
                pe.wait_ge(*drained(("att_o", L, 1)))
                pe.wait_ge(*drained(("oT", L)))
                out_slab(2, 0)
                for s in range(NS_WO):
                    w = take_slab(KT, 256)
                    for i in range(2):
                        key = ("wo", L, 2 * s + i)
                        acc = open_bank(key)
                        for k in range(KT):
                            if s == 0 and i == 0:
                                pe.wait_ge(*at("mixed_ready", L, k + 1))
                            ins = put(acc[:, 0:T], w[:, k, P * i:P * i + P], gates[:, k, :], k == 0, k == KT - 1)
                        close_bank(ins, key)
                    n_slab[0] += 1

            def dense(L):
                mean_over_features(L, 1)
                new_h[0] = (L, KT)
                for s in range(NS_DUP):
                    w = take_slab(2 * KT, P)
                    for t in range(2):
                        key = ("up", L, s, t)
                        close_bank(contract(key, w[:, KT * t:KT * t + KT, :], 0, KT, hT), key)
                    n_slab[0] += 1
                h = NDT // 2
                for m in range(KT):
                    acc = open_bank(("down", L, m))
                    for half in range(2):
                        w = take_slab(h, P)
                        for k in range(h):
                            if m == 0:
                                pe.wait_ge(*drained(("up", L, half * h + k, 1)))
                            ins = put(acc[:, 0:T], w[:, k, :], ff[:, half * h + k, :],
                                      half == 0 and k == 0, half == 1 and k == h - 1)
                        n_slab[0] += 1
                    close_bank(ins, ("down", L, m))

            pe.wait_ge(ident_ready, 1)
            pe.wait_ge(x_in, 48)
            for b, (t0, n) in enumerate(BLK):
                for k in range(2):
                    acc = open_bank(("xin", b, k))
                    for i in range(4):
                        m = 4 * k + i
                        ins = turn(acc[:, P * i:P * i + n], arena[0:n, b * D + P * m:b * D + P * m + P])
                    close_bank(ins, ("xin", b, k))
            pe.wait_ge(vecs_in, 16 * 14 * DEPTH)
            for L in range(DEPTH):
                acc = open_bank(("vecs", L))
                ins = turn(acc[:, 0:V_N], arena[0:V_N, 3 * D + P * L:3 * D + P * L + P])
                close_bank(ins, ("vecs", L))
            pe.wait_ge(consts_ready, 1)
            for L in range(DEPTH):
                acc = open_bank(("dskip", L))
                for j in range(4):
                    ins = put(acc[:, j:j + 1], sel2[:, j, :], hv[:, L, 2:3])
                close_bank(ins, ("dskip", L))
            for L in range(DEPTH):
                mixer(L)
                if L == 0:
                    dense(L)
            pe.wait_ge(*drained(("wo", 1, KT - 1)))
            advance(pe, "m_gu", "m_down")
            mean_over_features(1, 1)
            pe.wait_ge(*at("h_ready", 1, 2 * KT))
            for k in range(6):
                token_rows(("htok", k // 2, k % 2), hT, k // 2, range(4 * (k % 2), 4 * (k % 2) + 4))
            pe.wait_ge(w_router_in, 16)
            acc = open_bank(("logits", 0))
            for b, (t0, n) in enumerate(BLK):
                for k in range(KT):
                    ins = put(acc[0:n, 8 * b:8 * b + 8], hT[:, k, t0:t0 + n], wr[:, k, :], k == 0, k == KT - 1)
            close_bank(ins, ("logits", 0))
            acc = open_bank(("choice", 0))
            pe.wait_ge(chosen_ready, 1)
            for b, (t0, n) in enumerate(BLK):
                ins = put(acc[0:NEXP, t0:t0 + n], chosen[0:n, b, :], ident[0:n, 0:n])
            close_bank(ins, ("choice", 0))
            acc = open_bank(("place", 0))
            pe.wait_ge(places_ready, 1)
            for b, (t0, n) in enumerate(BLK):
                ins = put(acc[0:n, 8 * b:8 * b + 8], placeT[:, t0:t0 + n], ident[0:NEXP, 0:NEXP])
            close_bank(ins, ("place", 0))
            acc = open_bank(("count", 0))
            close_bank(put(acc[0:1, 0:NEXP], chosenT[:, T - 1:T], ident[0:NEXP, 0:NEXP]), ("count", 0))
            for k in range(6):
                pe.wait_ge(*drained(("htok", k // 2, k % 2)))
            pe.wait_ge(*drained(("place", 0)))
            pe.wait_ge(*drained(("count", 0)))
            advance(pe, "m_gathered", "m_turned", "m_hidden", "m_scattered")
            gate_bank, up_bank, turn_bank, y_bank = (0, 1), 2, 3, (4, 5)
            nr = load_rounds(pe)

            def gather(gi, after, count):
                pe.wait_ge(*lat("m_sel", gi, 1))
                for w in after:
                    pe.wait_ge(*w)
                for half in range(2):
                    for i in range(4):
                        m = 4 * half + i
                        for b, (t0, n) in enumerate(BLK):
                            ins = put(bank[6 + half][:, CAP * i:CAP * i + CAP], htok[0:n, b, P * m:P * m + P],
                                      Pm[0:n, b, :], b == 0, b == 2)
                    ins.then_inc(loop_signals["m_gathered"], 1)
                    if count:
                        loop_raised["m_gathered"] += 1

            def scatter(gi, count):
                pe.wait_ge(*lat("m_weights", gi, 1))
                for m in range(KT):
                    if m >= 2:
                        pe.wait_ge(*lat("m_added", gi, m - 1))
                    ins = put(bank[6 + m % 2][:, 0:T], yb[:, P * m:P * m + P], Cm)
                    ins.then_inc(loop_signals["m_scattered"], 1)
                    if count:
                        loop_raised["m_scattered"] += 1

            with pe.Fori(0, nr) as r:
                gi = r * (NEXP + 1)
                pe.wait_ge(*lat("m_added", gi - 1, 8))
                gather(gi, (), False)
                with pe.Fori(0, NEXP) as e:
                    it = r * NEXP + e
                    gi = r * (NEXP + 1) + e

                    def product(kind, c, out):
                        n = eslabs.index((kind, c))
                        pe.wait_ge(*eslab_in(it, n))
                        w = eslot[n % MRING].rearrange("p (k n) -> p k n", k=KT)
                        for k in range(KT):
                            ins = put(out[0:CAP, :], hg[:, k, :], w[:, k, :], k == 0, k == KT - 1)
                        ins.then_inc(*lup("m_gu"))

                    for c in range(NCH + 1):
                        if c == 0:
                            pe.wait_ge(*lat("m_hg", gi, 2))
                        if c < NCH:
                            pe.wait_ge(*lat("m_hid", it, max(c - 1, 0)))
                            product("g", c, bank[gate_bank[c % 2]])
                        if c > 0:
                            pe.wait_ge(*lat("m_hid", it, c))
                            pe.wait_ge(*lat("m_hidT", it, c - 1))
                            for i in range(4):
                                ins = turn(bank[turn_bank][:, CAP * i:CAP * i + CAP], hid[(c - 1) % 2][:, P * i:P * i + P])
                            ins.then_inc(*lup("m_hidden"))
                        if c < NCH:
                            pe.wait_ge(*lat("m_hid", it, c))
                            product("u", c, bank[up_bank])
                        if c == 0:
                            pe.wait_ge(*lat("m_y", it, 0))
                            scatter(gi, True)
                            pe.wait_ge(*lat("m_added", gi, 7))
                            for b, (t0, n) in enumerate(BLK):
                                ins = turn(bank[6][0:CAP, t0:t0 + n], Pc[0:n, b, :])
                            ins.then_inc(*lup("m_turned"))
                        else:
                            d = c - 1
                            if c == NCH:
                                gather(gi + 1, (lat("m_weights", gi + 1, 1), lat("m_added", gi, 8)), True)
                            n = eslabs.index(("d", d))
                            pe.wait_ge(*eslab_in(it, n))
                            pe.wait_ge(*lat("m_hidT", it, d + 1))
                            w = eslot[n % MRING].rearrange("p (k n) -> p k n", k=4)
                            for i in range(4):
                                for half in range(2):
                                    ins = put(bank[y_bank[half]][0:CAP, :], hidT[d % 2][:, i, :],
                                              w[:, i, 512 * half:512 * half + 512], d == 0 and i == 0,
                                              d == NCH - 1 and i == 3)
                            ins.then_inc(*lup("m_down"))
                pe.wait_ge(*lat("m_y", r * NEXP + NEXP - 1, 2))
                gi = r * (NEXP + 1) + NEXP
                pe.wait_ge(*lat("m_hg", gi, 2))
                scatter(gi, False)
            pe.wait_ge(*lat("m_added", (nr - 1) * (NEXP + 1) + NEXP, 8))
            for b in range(3):
                for k in range(2):
                    token_rows(("y", b, k), xT, b, range(4 * k, 4 * k + 4))

        @block.scalar
        def _(act):
            count = [0]

            def step(ins):
                count[0] += 1
                ins.then_inc(act_order, 1)
                act.wait_ge(act_order, count[0])

            def say(ins, name, L, k=1):
                ins.then_inc(*up(name))
                act.wait_ge(*at(name, L, k))

            def empty(ins, key):
                ins.then_inc(bank_drained[jobs[key][0]], 1)
                act.wait_ge(*drained(key))

            def fn(out, in_, f, **kw):
                return nc.scalar.activation(out, in_, f, **kw)

            def copy_out(out, key, src):
                act.wait_ge(*filled(key))
                empty(fn(out, src, ACT.Copy), key)

            def features_mean(L, which):
                for half in range(2):
                    if L > 0 and which == 0:
                        act.wait_ge(*drained(("down", L - 1, 4 * half + 3)))
                    if which == 1:
                        act.wait_ge(*drained(("wo", L, 4 * half + 3)))
                    m = slice(4 * half, 4 * half + 4)
                    say(fn(hT[:, m, :], xT[:, m, :], ACT.Square), "x_squared", L, 2 * which + half + 1)
                key = ("norm", L, which)
                act.wait_ge(*filled(key))
                empty(fn(rstd, psum(key)[:, 0:T], ACT.Ln, scale=1.0 / D, bias=eps[:, :]), key)
                say(fn(rstd, rstd, ACT.Exp, scale=-0.5), "rstd_ready", L, which + 1)

            def level_decay(L, i):
                act.wait_ge(*at("lvl_dist", L, i + 1))
                w = T if LEVELS[i] <= 16 else TP
                say(fn(dist[:, :, 0:w], dist[:, :, 0:w], ACT.Exp), "lvl_decay", L, i + 1)

            def sigmoid(v, w, plus, sig, L, k):
                act.wait_ge(*at(plus, L, k))
                step(fn(v, v, ACT.Ln))
                say(fn(w, v, ACT.Exp, scale=-1.0), sig, L, k)

            def hgrn_tail(L):
                act.wait_ge(*at("lvl_q", L, 8))
                act.wait_ge(*at("lvl_k", L, 8))
                for h in range(HH):
                    step(fn(dist[:, h, 0:TP], G[:, h, 0:TP], ACT.Exp, scale=-1.0, bias=G[:, h, TP - 1:TP]))
                act.wait_ge(*at("kd_dist", L))
                say(fn(dist[:, :, TP:T], dist[:, :, TP:T], ACT.Exp, scale=-1.0), "kd_decay", L)
                say(fn(taild.rearrange("p h b i -> p h (b i)"), G[:, :, TP:T], ACT.Exp), "hg_tail", L)
                for b, (t0, n) in enumerate(BLK):
                    key = ("kdtok", L, b)
                    copy_out(kdtok[0:n, b, :], key, psum(key)[0:n, :])
                key = ("hg_st", L)
                act.wait_ge(*at("qe_ready", L))
                copy_out(st_hg.rearrange("p h v -> p (h v)"), key, psum(key)[:, :])

            def hgrn_squares(L):
                act.wait_ge(*drained(("hg_o", L, 2)))
                act.wait_ge(*drained(("hg_o", L, 3)))
                say(fn(osq, o_hg, ACT.Square), "hg_osq", L)

            def hgrn_rstd(L):
                for h in range(HH):
                    key = ("hg_m", L, h)
                    act.wait_ge(*filled(key))
                    empty(fn(o_rstd[:, h, :], psum(key)[:, 0:T], ACT.Ln, scale=1.0 / P, bias=eps[:, :]), key)
                say(fn(o_rstd, o_rstd, ACT.Exp, scale=-0.5), "hg_rstd", L)
                for k in range(2):
                    key = ("ctail", L, k)
                    act.wait_ge(*filled(key))
                    step(fn(crows[0:3, 512 * k:512 * k + 512], psum(key)[0:3, :], ACT.Copy))
                    empty(fn(crows[32:56, 512 * k:512 * k + 512], psum(key)[32:56, :], ACT.Copy), key)

            def dt_log(L):
                act.wait_ge(*at("dt_neg", L))
                step(fn(dts[0:SH, 1, :], dts[0:SH, 1, :], ACT.Exp))
                say(fn(dts[0:SH, 1, :], dts[0:SH, 1, :], ACT.Ln, bias=ones[0:SH, 0:1]), "dt_log", L)

            def dt_exp(L):
                act.wait_ge(*at("dt_cum", L))
                step(fn(dts[0:SH, 3, :], dts[0:SH, 2, :], ACT.Exp))
                say(fn(dts[0:SH, 4, :], dts[0:SH, 4, :], ACT.Exp, scale=-1.0), "dt_exp", L)

            def ssd_rows(L):
                key = ("tokc", L)
                act.wait_ge(*filled(key))
                flat = tokc.rearrange("p a b c -> p (a b c)")
                step(fn(flat[:, 0:48], psum(key)[:, 0:48], ACT.Copy))
                empty(fn(flat[0:TS, 48:72], psum(key)[0:TS, 48:72], ACT.Copy), key)
                for b, (t0, n) in enumerate(BLK):
                    key = ("btok", L, b)
                    copy_out(btok[0:n, b, :], key, psum(key)[0:n, 0:256])

            def ssd_decays(L, h):
                act.wait_ge(*drained(("wdecay", L, h)))
                w = wb[h % 2]
                step(fn(w[:, 0:384], w[:, 0:384], ACT.Exp))
                say(fn(w[0:TS, 384:416], w[0:TS, 384:416], ACT.Exp), "w_exp", L, h + 1)

            def ssd_rstd(L):
                act.wait_ge(*at("ssm_y", L))
                say(fn(cve4, yT, ACT.Square), "ssm_ysq", L)
                key = ("ssm_m", L)
                act.wait_ge(*filled(key))
                empty(fn(zT[:, 0, :], psum(key)[:, 0:T], ACT.Ln, scale=1.0 / 512, bias=eps[:, :]), key)
                say(fn(zT[:, 0, :], zT[:, 0, :], ACT.Exp, scale=-0.5), "ssm_rstd", L)

            def qk_squares(L, g):
                if g > 0:
                    act.wait_ge(*at("qk_ready", L, g))
                else:
                    act.wait_ge(*at("xs_ready", L))
                say(fn(qsq, att[:, 6 * g:6 * g + 4, :], ACT.Square), "qk_sq", L, g + 1)

            def qk_rstd(L, g):
                for k in range(4):
                    key = ("qk_m", L, g, k)
                    act.wait_ge(*filled(key))
                    empty(fn(qsq[:, k, :], psum(key)[:, 0:T], ACT.Ln, scale=1.0 / 64, bias=eps[:, :]), key)
                say(fn(qsq, qsq, ACT.Exp, scale=-0.5), "qk_rstd", L, g + 1)

            def attention(L):
                act.wait_ge(*at("ssm_done", L))
                for g in range(AG):
                    for b, (t0, n) in enumerate(BLK):
                        key = ("kvtok", L, g, b)
                        copy_out(kvtok[0:n, b, g, :], key, psum(key)[0:n, :])
                for n in range(9):
                    if n < 8:
                        w = n % 2 + 1
                        act.wait_ge(*at("sc_neg", L, n + 1))
                        v = sc[n % 2].rearrange("p k c -> p (k c)")[:, 0:384 * w]
                        c = 4 * (n % 2)
                        say(fn(v, v, ACT.Exp, bias=col[:, c + 1:c + 2], accum_out=col[:, c + 2:c + 3]),
                            "sc_exp", L, n + 1)
                        for k in (2, 3):
                            key = ("kT", L, n, k)
                            copy_out(KTb[:, 256 + 512 * (k - 1):256 + 512 * k], key, psum(key)[:, :])
                    if n > 0:
                        m = n - 1
                        for k in range(m % 2 + 1):
                            key = ("pt", L, m, k)
                            copy_out(PT[m % 2][:, k, :], key, psum(key)[:, 0:384])
                        if m % 4 == 3:
                            key = ("att_o", L, m // 4)
                            copy_out(yall[:, 8 + m // 4, 0:TP], key, psum(key)[:, 0:TP])
                key = ("sS", L)
                act.wait_ge(*filled(key))
                step(fn(sTs[:, 0:2, :].rearrange("p a r -> p (a r)"), psum(key)[:, 0:256], ACT.Copy))
                empty(fn(sTs[0:64, 2, :], psum(key)[0:64, 256:384], ACT.Copy), key)
                key = ("sN", L)
                copy_out(sTn[0:TS].rearrange("p a r -> p (a r)"), key, psum(key)[0:TS, 0:384])
                act.wait_ge(*at("ss_neg", L))
                say(fn(kv_rows, kv_rows, ACT.Exp, bias=col[:, 9:10], accum_out=col[:, 10:11]), "ss_exp", L)
                key = ("pS", L)
                act.wait_ge(*filled(key))
                step(fn(sTs[:, 0:2, :].rearrange("p a r -> p (a r)"), psum(key)[:, 0:256], ACT.Copy))
                empty(fn(sTs[0:64, 2, :], psum(key)[0:64, 256:384], ACT.Copy), key)
                key = ("pN", L)
                copy_out(sTn[0:TS].rearrange("p a r -> p (a r)"), key, psum(key)[0:TS, 0:384])

            def mixer(L):
                features_mean(L, 0)
                if L > 0:
                    act.wait_ge(*at("mixed_ready", L - 1, KT))
                for t in range(16):
                    key = ("proj", L, t)
                    copy_out(hgp[:, t, :], key, psum(key)[:, 0:T])
                    if t == 3:
                        say(fn(qt, hgp[:, 0:4, :], ACT.Exp, scale=-1.0), "hg_exp", L, 1)
                    if t == 5:
                        sigmoid(qt, qt, "hg_plus", "hg_sig", L, 1)
                    if t == 7:
                        say(fn(dist, hgp[:, 4:8, :], ACT.Exp, scale=-1.0), "hg_exp", L, 2)
                    if t == 8:
                        sigmoid(dist, dist, "hg_plus", "hg_sig", L, 2)
                    if t == 11:
                        act.wait_ge(*at("hg_clamped", L))
                        say(fn(G, G, ACT.Ln), "hg_log", L)
                    if t == 15:
                        say(fn(kt, hgp[:, 12:16, :], ACT.Exp, scale=-1.0), "hg_exp", L, 3)
                for b, (t0, n) in enumerate(BLK):
                    key = ("vtok", L, b)
                    copy_out(vtok[0:n, b, :], key, psum(key)[0:n, :])
                sigmoid(kt, kt, "hg_plus", "hg_sig", L, 3)
                for t in range(16, 28):
                    key = ("proj", L, t)
                    if t < 20:
                        copy_out(zT[:, t - 16, :], key, psum(key)[:, 0:T])
                        if t == 19:
                            say(fn(zexp, zT, ACT.Exp, scale=-1.0), "z_exp", L)
                            level_decay(L, 0)
                    else:
                        act.wait_ge(*filled(key))
                        step(fn(xpad[:, t - 20, TAIL:PADW], psum(key)[:, 0:TP], ACT.Copy))
                        v = xpad[:, t - 20, PADW:PADT].rearrange("p (b c) -> p b c", b=DB)[:, :, TAIL:TAIL + DS]
                        empty(fn(v, tail4(psum(key)[:, TP:T]), ACT.Copy), key)
                        if t == 21:
                            sigmoid(zexp, zexp, "z_plus", "z_sig", L, 1)
                key = ("dt", L)
                copy_out(yall[0:SH, 9, :], key, psum(key)[0:SH, 0:T])
                for s in range(NS_AG):
                    if s == 9:
                        act.wait_ge(*at("qe_ready", L))
                    if s == 11:
                        act.wait_ge(*at("kd_ready", L))
                    if s == 12:
                        hgrn_squares(L)
                    if s == 13:
                        dt_log(L)
                    if s == 15:
                        act.wait_ge(*at("hg_done", L))
                    for i in range(2):
                        t = 2 * s + i
                        key = ("proj", L, 28 + t)
                        if t < 18:
                            copy_out(att[:, t, :], key, psum(key)[:, 0:T])
                        else:
                            act.wait_ge(*filled(key))
                            empty(fn(gates[:, t - 18, :], psum(key)[:, 0:T], ACT.Exp, scale=-1.0), key)
                        if i == 0 and 9 <= s < 12:
                            qk_squares(L, s - 9)
                        if i == 0 and s == 13:
                            dt_exp(L)
                        if 14 <= s < 18:
                            ssd_decays(L, 2 * (s - 14) + i)
                    if s < 7:
                        level_decay(L, s + 1)
                    if s == 4:
                        act.wait_ge(*at("conv_done", L))
                        say(fn(cve[:, :, 0:CW], cv[:, :, 0:CW], ACT.Exp, scale=-1.0), "conv_exp", L)
                    if s == 5:
                        sigmoid(cve[:, :, 0:CW], cve[:, :, 0:CW], "conv_plus", "conv_sig", L, 1)
                    if s == 7:
                        hgrn_tail(L)
                    if 9 <= s < 12:
                        qk_rstd(L, s - 9)
                    if s == 12:
                        hgrn_rstd(L)
                    if s == 13:
                        ssd_rows(L)
                    if s == 18:
                        key = ("ssm_st", L)
                        copy_out(ssm_st, key, psum(key)[:, :])
                    if s >= 19:
                        for j in ((0, 1) if s == 19 else (2, 3)):
                            for k in range(2):
                                key = ("h0T", L, j, k)
                                copy_out(h0T[j % 2][:, 4 * k:4 * k + 4, :].rearrange("n b p -> n (b p)"), key,
                                         psum(key)[:, :])
                    if s >= 9:
                        v = gates[:, 2 * (s - 9):2 * (s - 9) + 2, :]
                        sigmoid(v, v, "gate_plus", "gate_sig", L, s - 8)
                ssd_rstd(L)
                attention(L)

            def dense(L):
                features_mean(L, 1)
                for s in range(NS_DUP):
                    key = ("up", L, s, 0)
                    e = ffe[s % 4]
                    if s >= 4:
                        act.wait_ge(*drained(("up", L, s - 4, 1)))
                    act.wait_ge(*filled(key))
                    ins = fn(e, psum(key)[:, 0:T], ACT.Exp, scale=-1.0)
                    ins.then_inc(up_exp, 1)
                    act.wait_ge(up_plus, s + 1)
                    step(fn(e, e, ACT.Ln))
                    ins = fn(e, e, ACT.Exp, scale=-1.0)
                    ins.then_inc(up_sig, 1)
                    act.wait_ge(up_sig, s + 1)

            for b, (t0, n) in enumerate(BLK):
                for k in range(2):
                    key = ("xin", b, k)
                    act.wait_ge(*filled(key))
                    empty(fn(xT[:, 4 * k:4 * k + 4, t0:t0 + n],
                             psum(key)[:, :].rearrange("p (m t) -> p m t", m=4)[:, :, 0:n], ACT.Copy), key)
            for L in range(DEPTH):
                key = ("vecs", L)
                copy_out(vecs[:, L, :], key, psum(key)[:, 0:V_N])
            for L in range(DEPTH):
                key = ("dskip", L)
                copy_out(dskip[:, L, :], key, psum(key)[:, 0:4])
            for L in range(DEPTH):
                ins = fn(hv[:, L, 1:2], hv[:, L, 1:2], ACT.Exp)
                ins.then_inc(a_ready, 1)
                act.wait_ge(a_ready, L + 1)
            act.wait_ge(lb_ready, 1)
            ins = fn(lbe[:, :, :], lbe[:, :, :], ACT.Exp)
            ins.then_inc(lb_exp, 1)
            act.wait_ge(lb_exp, 1)
            for L in range(DEPTH):
                mixer(L)
                if L == 0:
                    dense(L)
            features_mean(1, 1)
            for k in range(6):
                b, half = k // 2, k % 2
                n = BLK[b][1]
                copy_out(htok[0:n, b, 512 * half:512 * half + 512], ("htok", b, half), psum(("htok", b, half))[0:n, :])
            for b, (t0, n) in enumerate(BLK):
                act.wait_ge(chosen_exp, b + 1)
                ins = fn(rw[0:n, b, 0:1], rw[0:n, b, 0:1], ACT.Exp)
                ins.then_inc(chosen_exped, 1)
                act.wait_ge(chosen_exped, b + 1)
            advance(act, "m_hg", "m_exp", "m_hidT", "m_y")
            nr = load_rounds(act)

            def hidden_out(it, d):
                act.wait_ge(*lat("m_hidden", it, d + 1))
                act.wait_ge(*lat("m_down", it, max(d - 1, 0)))
                fn(hidT[d % 2].rearrange("p a b -> p (a b)"), bank[3][:, 0:4 * CAP], ACT.Copy).then_inc(*lup("m_hidT"))

            with act.Fori(0, nr) as r:
                for half in range(2):
                    act.wait_ge(*lat("m_gathered", r * (NEXP + 1), half + 1))
                    fn(hg[:, 4 * half:4 * half + 4, :], bank[6 + half][:, 0:4 * CAP].rearrange("p (a b) -> p a b", a=4),
                       ACT.Copy).then_inc(loop_signals["m_hg"], 1)
                with act.Fori(0, NEXP) as e:
                    it = r * NEXP + e
                    gi = r * (NEXP + 1) + e
                    for c in range(NCH):
                        act.wait_ge(*lat("m_hid", it, max(c - 1, 0)))
                        act.wait_ge(*lat("m_gu", it, 2 * c + 1))
                        fn(ex[c % 2], bank[c % 2][0:CAP, :], ACT.Exp, scale=-1.0).then_inc(*lup("m_exp"))
                        if c > 0:
                            hidden_out(it, c - 1)
                    hidden_out(it, NCH - 1)
                    act.wait_ge(*lat("m_gu", it, 2 * NCH))
                    for half in range(2):
                        act.wait_ge(*lat("m_gathered", gi + 1, half + 1))
                        fn(hg[:, 4 * half:4 * half + 4, :],
                           bank[6 + half][:, 0:4 * CAP].rearrange("p (a b) -> p a b", a=4),
                           ACT.Copy).then_inc(*lup("m_hg"))
                    act.wait_ge(*lat("m_scattered", gi, 8))
                    act.wait_ge(*lat("m_down", it, NCH))
                    for half in range(2):
                        fn(yb[:, 512 * half:512 * half + 512], bank[4 + half][0:CAP, :], ACT.Copy).then_inc(*lup("m_y"))
            for b, (t0, n) in enumerate(BLK):
                for k in range(2):
                    key = ("y", b, k)
                    copy_out(yrows[0:n, b, 512 * k:512 * k + 512], key, psum(key)[0:n, :])

        @block.vector
        def _(dve):
            count = [0]
            ve = nc.vector

            def step(ins):
                count[0] += 1
                ins.then_inc(dve_order, 1)
                dve.wait_ge(dve_order, count[0])

            def say(ins, name, L, k=1):
                ins.then_inc(*up(name))
                dve.wait_ge(*at(name, L, k))

            def empty(ins, key):
                ins.then_inc(bank_drained[jobs[key][0]], 1)
                dve.wait_ge(*drained(key))

            def tt(out, a, b, op):
                return ve.tensor_tensor(out, a, b, op)

            def plus(v, name, L, k=1):
                say(ve.tensor_scalar(v, v, 1.0, SIG_MAX, ALU.add, ALU.min), name, L, k)

            def normalise(L, which):
                dve.wait_ge(*at("rstd_ready", L, which + 1))
                v = V_MIX if which == 0 else V_FFN
                for m in range(KT):
                    ins = ve.scalar_tensor_tensor(hT[:, m, :], xT[:, m, :], vecs[:, L, v + m:v + m + 1], rstd,
                                                  ALU.mult, ALU.mult)
                    say(ins, "h_ready", L, KT * which + m + 1)

            def hgrn_inputs(L):
                dve.wait_ge(*at("hg_exp", L, 1))
                plus(qt, "hg_plus", L, 1)
                dve.wait_ge(*at("hg_sig", L, 1))
                step(tt(hgp[:, 0:4, :], hgp[:, 0:4, :], qt, ALU.mult))
                dve.wait_ge(*at("hg_exp", L, 2))
                plus(dist, "hg_plus", L, 2)
                dve.wait_ge(*at("hg_sig", L, 2))
                for h in range(HH):
                    step(ve.tensor_scalar(dist[:, h, :], dist[:, h, :], lb[:, L, 1, h:h + 1], lb[:, L, 0, h:h + 1],
                                          ALU.mult, ALU.add))
                say(ve.tensor_scalar(G, dist, LN_MIN, None, ALU.max), "hg_clamped", L)
                step(ve.tensor_scalar(hgp[:, 4:8, :], dist, -1.0, 1.0, ALU.mult, ALU.add))
                dve.wait_ge(*at("hg_log", L))
                for h in range(HH):
                    step(ve.tensor_tensor_scan(G[:, h, :], reset[:, :], G[:, h, :], 0.0, ALU.mult, ALU.add))
                level_dist(L, 0)
                dve.wait_ge(*at("hg_exp", L, 3))
                plus(kt, "hg_plus", L, 3)
                dve.wait_ge(*at("hg_sig", L, 3))
                say(tt(hgp[:, 12:16, :], hgp[:, 12:16, :], kt, ALU.mult), "hg_gated", L)
                step(ve.memset(xpad[:, :, 0:TAIL], 0.0))
                key = ("cstate", L)
                dve.wait_ge(*filled(key))
                dst = xpad[:, :, PADW:PADT].rearrange("p m (b c) -> p m b c", b=DB)[:, :, :, 0:TAIL]
                src = psum(key)[:, 0:192].rearrange("p (m b c) -> p m b c", m=KT, b=DB)
                empty(ve.tensor_copy(dst, src), key)
                dve.wait_ge(*at("z_exp", L))
                plus(zexp, "z_plus", L)

            def level_dist(L, i):
                h = LEVELS[i]
                if i > 0:
                    dve.wait_ge(*at("lvl_k", L, i))
                if h <= 16:
                    g = G.rearrange("p h t -> p (h t)").rearrange("p (n w) -> p n w", w=2 * h)
                    d = dist.rearrange("p h t -> p (h t)").rearrange("p (n w) -> p n w", w=2 * h)
                    step(tt(d, g, g[:, :, h - 1:h].to_broadcast([P, HH * T // (2 * h), 2 * h]), ALU.subtract))
                    d = dist
                else:
                    g = G[:, :, 0:TP].rearrange("p h (n w) -> p h n w", w=2 * h)
                    d = dist[:, :, 0:TP].rearrange("p h (n w) -> p h n w", w=2 * h)
                    step(tt(d, g, g[:, :, :, h - 1:h].to_broadcast([P, HH, TP // (2 * h), 2 * h]), ALU.subtract))
                    d = dist[:, :, 0:TP]
                say(ve.scalar_tensor_tensor(d, d, -1.0, d, ALU.mult, ALU.min), "lvl_dist", L, i + 1)

            def level_mask(L, i):
                if i == 7:
                    key = ("lvl", L, 7, 0)
                    dve.wait_ge(*filled(key))
                    empty(ve.tensor_copy(a01.rearrange("p h t -> p (h t)"), psum(key)[:, :]), key)
                    return
                m = ident[:, :] if i == "same" else lmask[:, i, :]
                for b, a in enumerate((a00, a11, aS)):
                    key = ("lvl", L, i, b)
                    if key not in jobs:
                        continue
                    n = P if b < 2 else TS
                    dve.wait_ge(*filled(key))
                    mk = m[0:n, 0:n].unsqueeze(1).to_broadcast([n, HH, n]).bitcast(U32)
                    src = psum(key)[0:n, 0:HH * n].rearrange("p (h t) -> p h t", h=HH)
                    empty(ve.copy_predicated(a[0:n], mk, src), key)

            def hgrn_levels(L):
                dve.wait_ge(*at("hg_zeroed", L))
                for i in range(8):
                    dve.wait_ge(*at("lvl_decay", L, i + 1))
                    if i > 0:
                        dve.wait_ge(*filled(level_end(L, i - 1)))
                    w = T if LEVELS[i] <= 16 else TP
                    say(tt(qt[:, :, 0:w], hgp[:, 0:4, 0:w], dist[:, :, 0:w], ALU.mult), "lvl_q", L, i + 1)
                    if i < 7:
                        level_dist(L, i + 1)
                    else:
                        dve.wait_ge(*at("lvl_k", L, 8))
                        s = G[:, :, TP:T].rearrange("p h (b i) -> p h b i", i=DS)
                        d = dist[:, :, TP:T].rearrange("p h (b i) -> p h b i", i=DS)
                        say(tt(d, s, s[:, :, :, DS - 1:DS].to_broadcast([P, HH, DB, DS]), ALU.subtract), "kd_dist", L)
                    if i < 4:
                        for m in (2 * i, 2 * i + 1):
                            convolve(L, m)
                    if i == 3:
                        new_conv_rows(L)
                    if i == 4:
                        dve.wait_ge(*at("conv_exp", L))
                        plus(cve[:, :, 0:CW], "conv_plus", L)
                    level_mask(L, i)
                    if i == 0:
                        level_mask(L, "same")
                        dve.wait_ge(*at("z_sig", L))
                        say(tt(zT, zT, zexp, ALU.mult), "z_gated", L)
                    if i == 5:
                        conv_silu(L)

            def hgrn_head(L, h):
                if h == 0:
                    dve.wait_ge(*at("kd_ready", L))
                key = ("hg_o", L, h)
                dve.wait_ge(*filled(key))
                empty(ve.tensor_copy(o_hg[:, h, :], psum(key)[:, 0:T]), key)
                dve.wait_ge(*at("s0_scaled", L, h + 1))
                for k in range(2):
                    key = ("hg_s", L, h, k)
                    v = S0[h % 2][:, 4 * k:4 * k + 4, :].rearrange("p b v -> p (b v)")
                    dve.wait_ge(*filled(key))
                    empty(tt(v, v, psum(key)[:, :], ALU.add), key)

            def values_by_sequence(L, h):
                if h > 0:
                    dve.wait_ge(*filled(("hg_s", L, h - 1, 1)))
                say(tt(vexp[0:TS], vtok[0:TS, 2, P * h:P * h + P].unsqueeze(1).to_broadcast([TS, DB, P]),
                       seqm[:, :].unsqueeze(2).to_broadcast([TS, DB, P]), ALU.mult), "vexp_ready", L, h + 1)

            def hgrn_norm_out(L):
                dve.wait_ge(*at("hg_rstd", L))
                step(ve.scalar_tensor_tensor(o_hg, o_hg, vecs[:, L, V_HN:V_HN + 1], o_rstd, ALU.mult, ALU.mult))
                say(tt(yall[:, 0:4, :], o_hg, hgp[:, 12:16, :], ALU.mult), "hg_done", L)

            def gate_plus(L, k):
                for t in (18 + 2 * k, 19 + 2 * k):
                    dve.wait_ge(*drained(("proj", L, 28 + t)))
                plus(gates[:, 2 * k:2 * k + 2, :], "gate_plus", L, k + 1)

            def convolve(L, m):
                dve.wait_ge(*drained(("proj", L, 20 + m)))
                w = [vecs[:, L, V_CW + 8 * j + m:V_CW + 8 * j + m + 1] for j in range(CONV)]
                step(ve.tensor_scalar(cv[:, m, 0:CW], xpad[:, m, 0:CW], w[0],
                                      vecs[:, L, V_CB + m:V_CB + m + 1], ALU.mult, ALU.add))
                for j in range(1, CONV):
                    ins = ve.scalar_tensor_tensor(cv[:, m, 0:CW], xpad[:, m, j:j + CW], w[j], cv[:, m, 0:CW],
                                                  ALU.mult, ALU.add)
                    if m == 7 and j == CONV - 1:
                        say(ins, "conv_done", L)
                    else:
                        step(ins)

            def new_conv_rows(L):
                step(ve.tensor_copy(ctail[:, :, 0:TAIL], xpad[:, :, PADW - TAIL:PADW]))
                for m in range(KT):
                    v = xpad[:, m, PADW:PADT].rearrange("p (b c) -> p b c", b=DB)[:, :, DS:DS + TAIL]
                    ins = ve.tensor_copy(ctail[:, m, TAIL:27].rearrange("p (b c) -> p b c", b=DB), v)
                    if m < KT - 1:
                        step(ins)
                    else:
                        say(ins, "conv_tail", L)

            def conv_silu(L):
                dve.wait_ge(*at("conv_sig", L))
                step(tt(xs[:, :, 0:TP], cv[:, :, 0:TP], cve[:, :, 0:TP], ALU.mult))
                for m in range(KT):
                    a, b = (v[:, m, PADW:PADT].rearrange("p (b c) -> p b c", b=DB)[:, :, 0:DS] for v in (cv, cve))
                    ins = tt(tail4(xs[:, m, TP:T]), a, b, ALU.mult)
                    if m < KT - 1:
                        step(ins)
                    else:
                        say(ins, "xs_ready", L)

            u, dt_tmp, cum, wl = (dts[0:SH, i, :] for i in (0, 1, 2, 4))

            def dt_start(L):
                for i in range(2):
                    dve.wait_ge(s0_in[i], 16 * (4 * L + 4))
                dve.wait_ge(st_out, 16 * (2 * L + 1))
                dve.wait_ge(*drained(("dt", L)))
                step(ve.tensor_scalar(u, yall[0:SH, 9, :], hv[:, L, 0:1], None, ALU.add))
                say(ve.scalar_tensor_tensor(dt_tmp, u, -1.0, u, ALU.mult, ALU.min), "dt_neg", L)

            def dt_sums(L):
                dve.wait_ge(*at("dt_log", L))
                dve.wait_ge(a_ready, L + 1)
                step(ve.scalar_tensor_tensor(u, u, 0.0, dt_tmp, ALU.max, ALU.add))
                step(ve.tensor_scalar(cum, u, hv[:, L, 1:2], -1.0, ALU.mult, ALU.mult))
                step(ve.tensor_tensor_scan(cum, reset[0:SH, :], cum, 0.0, ALU.mult, ALU.add))
                step(ve.tensor_scalar(wl[:, 0:TP], cum[:, 0:TP], cum[:, TP - 1:TP], None, ALU.subtract))
                c4 = tail4(cum[:, TP:T])
                say(tt(tail4(wl[:, TP:T]), c4, c4[:, :, DS - 1:DS].to_broadcast([SH, DB, DS]), ALU.subtract),
                    "dt_cum", L)
                dve.wait_ge(*at("dt_exp", L))
                say(tt(wl, wl, u, ALU.mult), "dt_ready", L)

            def ssd_rows(L):
                for b, (t0, n) in enumerate(BLK):
                    key = ("xtok", L, b)
                    dve.wait_ge(*filled(key))
                    dve.wait_ge(*drained(("tokc", L)))
                    src = psum(key)[0:n, :].rearrange("p (h c) -> p h c", h=SH)
                    for i, dst in ((1, xdt), (2, xw)):
                        ins = tt(dst[0:n, b, :].rearrange("p (h c) -> p h c", h=SH), src,
                                 tokc[0:n, b, i, :].unsqueeze(2).to_broadcast([n, SH, 64]), ALU.mult)
                        step(ins) if i == 1 else empty(ins, key)
                for g in range(2):
                    key = ("cb", L, g)
                    dve.wait_ge(*filled(key))
                    a, c = psum(key), cbm[:, g, :]
                    step(tt(c[:, 0:P], a[:, 0:P], causal[:, :], ALU.mult))
                    step(ve.tensor_copy(c[:, P:TP], a[:, P:TP]))
                    step(tt(c[:, TP:384], a[:, TP:384], causal[:, :], ALU.mult))
                    empty(tt(c[0:TS, 384:416], a[0:TS, 384:416], scausal[:, :, :].rearrange("p b i -> p (b i)"),
                             ALU.mult), key)

            def ssd_head(L, h):
                key = ("wdecay", L, h)
                dve.wait_ge(*filled(key))
                w, a = wb[h % 2], psum(key)
                if h == 0:
                    dve.wait_ge(*drained(("tokc", L)))
                step(ve.tensor_scalar(w[:, 0:TP], a[:, 0:TP], tokc[:, 0, 0, h:h + 1], 0.0, ALU.subtract, ALU.min))
                step(ve.tensor_scalar(w[:, TP:384], a[:, P:TP], tokc[:, 1, 0, h:h + 1], 0.0, ALU.subtract, ALU.min))
                empty(ve.tensor_scalar(w[0:TS, 384:416], a[0:TS, TP:T], tokc[0:TS, 2, 0, h:h + 1], 0.0,
                                       ALU.subtract, ALU.min), key)

            def ssd_y(L, j):
                key = ("ssm_y", L, j)
                dve.wait_ge(*filled(key))
                empty(ve.scalar_tensor_tensor(yT[:, j, :], xs[:, j, :], dskip[:, L, j:j + 1], psum(key)[:, 0:T],
                                              ALU.mult, ALU.add), key)

            def ssd_state(L, j):
                key = ("inter", L, j)
                dve.wait_ge(*filled(key))
                say(ve.tensor_copy(ep[:, j, :], psum(key)[:, TS:2 * TS]), "ep_ready", L, j + 1)
                empty(tt(col[:, 8:40], psum(key)[:, 0:TS], ep[:, j, :], ALU.mult), key)
                step(tt(yT[:, j, TP:T], yT[:, j, TP:T], col[:, 8:40], ALU.add))
                dve.wait_ge(*at("h0_scaled", L, j + 1))
                for k in range(2):
                    key = ("ssm_s", L, j, k)
                    v = h0[j % 2][:, 4 * k:4 * k + 4, :].rearrange("p b v -> p (b v)")
                    dve.wait_ge(*filled(key))
                    empty(tt(v, v, psum(key)[:, :], ALU.add), key)

            def ssd_out(L):
                say(tt(yT, yT, zT, ALU.mult), "ssm_y", L)
                dve.wait_ge(*at("ssm_rstd", L))
                for j in range(4):
                    ins = ve.scalar_tensor_tensor(yall[:, 4 + j, :], yT[:, j, :], vecs[:, L, V_SN + j:V_SN + j + 1],
                                                  zT[:, 0, :], ALU.mult, ALU.mult)
                    step(ins) if j < 3 else say(ins, "ssm_done", L)

            def qk_normed(L, g):
                dve.wait_ge(*at("qk_rstd", L, g + 1))
                for k in range(4):
                    v = (V_QN if k < 2 else V_KN) + g
                    a = att[:, 6 * g + k, :]
                    ins = ve.scalar_tensor_tensor(a, a, vecs[:, L, v:v + 1], qsq[:, k, :], ALU.mult, ALU.mult)
                    step(ins) if k < 3 else say(ins, "qk_ready", L, g + 1)

            def sample_queries(L):
                for i in range(2):
                    dve.wait_ge(h0_in[i], 16 * (4 * L + 4))
                step(ve.memset(qx, 0.0))
                for p in range(2):
                    for e in range(2):
                        r = slice(64 * e, 64 * e + 64)
                        for g in range(AG):
                            dst = qx[r, g, p, :].rearrange("p (b c) -> p b c", b=DB)[:, :, DS * e:DS * e + DS]
                            ins = ve.tensor_copy(dst, tail4(att[r, 6 * g + p, TP:T]))
                            step(ins) if (p, e, g) != (1, 1, 2) else say(ins, "qx_ready", L)

            def prompt_scores(L, n):
                w = n % 2 + 1
                c = 4 * (n % 2)
                for k in range(w):
                    key = ("sc", L, n, k)
                    dve.wait_ge(*filled(key))
                    if n >= 2 and k == 0:
                        for kk in range(w):
                            dve.wait_ge(*filled(("pt", L, n - 2, kk)))
                    empty(ve.scalar_tensor_tensor(sc[n % 2][:, k, :], psum(key)[:, 0:384], SCALE,
                                                  amask[:, w - 1 - k, :], ALU.mult, ALU.add), key)
                v = sc[n % 2].rearrange("p k c -> p (k c)")[:, 0:384 * w]
                step(ve.tensor_reduce(col[:, c:c + 1], v, AX.X, ALU.max))
                say(ve.tensor_scalar(col[:, c + 1:c + 2], col[:, c:c + 1], -1.0, None, ALU.mult), "sc_neg", L, n + 1)
                for k in (0, 1):
                    key = ("kT", L, n, k)
                    dve.wait_ge(*filled(key))
                    if k == 0:
                        empty(ve.tensor_copy(KTb[:, 0:256], psum(key)[:, 0:256]), key)
                    else:
                        empty(ve.tensor_copy(KTb[:, 256:768], psum(key)[:, :]), key)
                dve.wait_ge(*at("sc_exp", L, n + 1))
                step(ve.reciprocal(col[:, c + 3:c + 4], col[:, c + 2:c + 3]))
                say(ve.tensor_scalar(v, v, col[:, c + 3:c + 4], None, ALU.mult), "sc_ready", L, n + 1)

            def sample_rows(L):
                key = ("rows", L)
                dve.wait_ge(*filled(key))
                empty(ve.scalar_tensor_tensor(kv_rows, psum(key)[:, 0:416], SCALE, smask[:, :], ALU.mult, ALU.add), key)
                step(ve.tensor_reduce(col[:, 8:9], kv_rows, AX.X, ALU.max))
                say(ve.tensor_scalar(col[:, 9:10], col[:, 8:9], -1.0, None, ALU.mult), "ss_neg", L)
                dve.wait_ge(*at("ss_exp", L))
                step(ve.reciprocal(col[:, 11:12], col[:, 10:11]))
                say(ve.tensor_scalar(kv_rows, kv_rows, col[:, 11:12], None, ALU.mult), "ss_ready", L)

            def sample_output(L):
                key = ("oT", L)
                dve.wait_ge(*filled(key))
                for p in range(2):
                    for e in range(2):
                        r = slice(64 * e, 64 * e + 64)
                        c = 8 * p + DS * e
                        src = psum(key)[r, 0:P].rearrange("p (b c) -> p b c", b=DB)[:, :, c:c + DS]
                        ins = ve.tensor_copy(tail4(yall[r, 8 + p, TP:T]), src)
                        step(ins) if p + e < 2 else empty(ins, key)

            def mixer(L):
                normalise(L, 0)
                if L == 0:
                    attention_masks()
                hgrn_inputs(L)
                hgrn_levels(L)
                dve.wait_ge(*at("hg_tail", L))
                say(tt(qe, hgp[:, 0:4, TP:T], taild.rearrange("p h b i -> p h (b i)"), ALU.mult), "qe_ready", L)
                for s in range(8, NS_AG):
                    if s < 12:
                        values_by_sequence(L, s - 8)
                    if s == 13:
                        dt_sums(L)
                    if 14 <= s < 19:
                        for h in range(2 * (s - 14), 2 * (s - 14) + 2):
                            if h < SH:
                                ssd_head(L, h)
                            if 0 < h <= SH and h % 2 == 0:
                                ssd_y(L, h // 2 - 1)
                    if s >= 9:
                        gate_plus(L, s - 9)
                    if s < 12:
                        hgrn_head(L, s - 8)
                    if 9 <= s < 12:
                        qk_normed(L, s - 9)
                    if s == 12:
                        hgrn_norm_out(L)
                        dt_start(L)
                    if s == 13:
                        ssd_rows(L)
                    if s >= 19:
                        for j in ((0, 1) if s == 19 else (2, 3)):
                            ssd_state(L, j)
                ssd_out(L)
                sample_queries(L)
                for n in range(8):
                    prompt_scores(L, n)
                sample_rows(L)
                dve.wait_ge(*at("gate_sig", L, 12))
                for br in range(3):
                    for m in range(KT):
                        if (br, m) == (2, 0):
                            sample_output(L)
                        key = ("out", L, br, m)
                        g = gates[:, 8 * br + m, :]
                        dve.wait_ge(*filled(key))
                        empty(tt(g, g, psum(key)[:, 0:T], ALU.mult), key)
                for m in range(KT):
                    key = ("wo", L, m)
                    dve.wait_ge(*filled(key))
                    empty(tt(xT[:, m, :], xT[:, m, :], psum(key)[:, 0:T], ALU.add), key)

            def dense(L):
                normalise(L, 1)
                for s in range(NS_DUP):
                    e = ffe[s % 4]
                    dve.wait_ge(up_exp, s + 1)
                    ins = ve.tensor_scalar(e, e, 1.0, SIG_MAX, ALU.add, ALU.min)
                    ins.then_inc(up_plus, 1)
                    dve.wait_ge(up_plus, s + 1)
                    dve.wait_ge(up_sig, s + 1)
                    key = ("up", L, s, 0)
                    empty(tt(e, e, psum(key)[:, 0:T], ALU.mult), key)
                    key = ("up", L, s, 1)
                    dve.wait_ge(*filled(key))
                    empty(tt(ff[:, s, :], e, psum(key)[:, 0:T], ALU.mult), key)
                for m in range(KT):
                    key = ("down", L, m)
                    dve.wait_ge(*filled(key))
                    empty(tt(xT[:, m, :], xT[:, m, :], psum(key)[:, 0:T], ALU.add), key)

            def attention_masks():
                dve.wait_ge(consts_ready, 1)
                dI = yall[:, 0:2, 0:P].bitcast(I32)
                tI = yall[:, 4:6, 0:P].bitcast(I32)
                tF = yall[:, 6:8, 0:P]
                nearF = yall[:, 2, 4:4 + P]
                for g, dil in enumerate((1, 4, 16)):
                    out = amask[:, :, P * g:P * g + P]
                    step(ve.tensor_scalar(tI, dI, dil - 1, None, ALU.bitwise_and))
                    step(ve.tensor_copy(tF, tI))
                    step(ve.tensor_scalar(tF, tF, 0.0, None, ALU.is_equal))
                    step(ve.tensor_copy(out, dI))
                    if g == 0:
                        step(ve.tensor_scalar(nearF, out[:, 1, :], 128.0, None, ALU.is_le))
                    step(ve.tensor_scalar(out, out, 0.0, None, ALU.is_ge))
                    step(tt(out, out, tF, ALU.mult))
                    if g == 0:
                        step(tt(out[:, 1, :], out[:, 1, :], nearF, ALU.mult))
                    step(ve.tensor_scalar(out, out, 1.0, -NEG, ALU.subtract, ALU.mult))
                pI, cI = yall[:, 2, 0:2].bitcast(I32), yall[:, 3, 0:TS].bitcast(I32)
                qI = yall[:, 3, 32:64].bitcast(I32)
                rI = yall[:, 2, 140:142].bitcast(I32)
                tok_p, seq_p = yall[:, 2, 142:143], yall[:, 2, 143:144]
                tok_c, seq_c = yall[:, 3, 64:96], yall[:, 3, 96:128]
                step(ve.tensor_scalar(rI[:, 0:1], pI[:, 0:1], 3, None, ALU.bitwise_and))
                step(ve.tensor_scalar(rI[:, 1:2], pI[:, 1:2], 4, None, ALU.logical_shift_right))
                step(ve.tensor_copy(yall[:, 2, 142:144], rI))
                step(ve.tensor_scalar(qI, cI, 3, None, ALU.bitwise_and))
                step(ve.tensor_copy(tok_c, qI))
                step(ve.tensor_scalar(cI, cI, 2, None, ALU.logical_shift_right))
                step(ve.tensor_copy(seq_c, cI))
                step(ve.memset(smask[:, :], 1.0))
                step(ve.tensor_scalar(smask[:, 0:P], iota[:, :], tok_p, None, ALU.is_ge))
                step(ve.tensor_scalar(seq_c, seq_c, seq_p, None, ALU.is_equal))
                for g in range(AG):
                    o = smask[:, 320 + TS * g:352 + TS * g]
                    step(ve.tensor_scalar(o, tok_c, tok_p, None, ALU.is_le if g == 0 else ALU.is_equal))
                    step(tt(o, o, seq_c, ALU.mult))
                step(ve.tensor_scalar(smask[:, :], smask[:, :], 1.0, -NEG, ALU.subtract, ALU.mult))

            for L in range(DEPTH):
                dve.wait_ge(*drained(("vecs", L)))
            l0, l1 = (vecs[:, L, V_LB:V_LB + 4] for L in range(DEPTH))
            m4, s4 = col[:, 0:4], col[:, 4:8]
            step(tt(m4, l0, l1, ALU.max))
            step(tt(lbe[:, 0, :], l0, m4, ALU.subtract))
            ins = tt(lbe[:, 1, :], l1, m4, ALU.subtract)
            ins.then_inc(lb_ready, 1)
            dve.wait_ge(lb_ready, 1)
            dve.wait_ge(lb_exp, 1)
            step(tt(s4, lbe[:, 0, :], lbe[:, 1, :], ALU.add))
            step(ve.reciprocal(s4, s4))
            for L in range(DEPTH):
                step(tt(lbe[:, L, :], lbe[:, L, :], s4, ALU.mult))
            step(tt(s4, lbe[:, 0, :], lbe[:, 1, :], ALU.add))
            step(tt(lb[:, 0, 0, :], lbe[:, 0, :], lbe[:, 0, :], ALU.subtract))
            step(tt(lb[:, 1, 0, :], s4, lbe[:, 0, :], ALU.subtract))
            step(ve.tensor_scalar(lb[:, :, 1, :], lb[:, :, 0, :], -1.0, 1.0, ALU.mult, ALU.add))
            for L in range(DEPTH):
                mixer(L)
                if L == 0:
                    dense(L)
            normalise(1, 1)
            key = ("logits", 0)
            dve.wait_ge(*filled(key))
            step(ve.tensor_copy(lg[:, 0:2, :].rearrange("p b e -> p (b e)"), psum(key)[:, 0:16]))
            empty(ve.tensor_copy(lg[0:TS, 2, :], psum(key)[0:TS, 16:24]), key)
            for b, (t0, n) in enumerate(BLK):
                step(ve.max(top[0:n, b, :], lg[0:n, b, :]))
                step(ve.max_index(topi[0:n, b, :], top[0:n, b, :], lg[0:n, b, :]))
                step(ve.tensor_copy(topf[0:n, b, :], topi[0:n, b, :]))
                ins = tt(rw[0:n, b, 0:1], top[0:n, b, 1:2], top[0:n, b, 0:1], ALU.subtract)
                ins.then_inc(chosen_exp, 1)
                dve.wait_ge(chosen_exp, b + 1)
                dve.wait_ge(chosen_exped, b + 1)
                e1, den, p1, p2 = (rw[0:n, b, i:i + 1] for i in range(4))
                step(ve.tensor_scalar(den, e1, 1.0, None, ALU.add))
                step(ve.reciprocal(p1, den))
                step(tt(p2, p1, e1, ALU.mult))
                for i in range(2):
                    step(ve.tensor_scalar(pick[0:n, i, :], iota[0:n, 0:NEXP], topf[0:n, b, i:i + 1], None, ALU.is_equal))
                step(tt(chosen[0:n, b, :], pick[0:n, 0, :], pick[0:n, 1, :], ALU.add))
                step(ve.tensor_scalar(comb[0:n, b, 0:NEXP], pick[0:n, 0, :], p1, None, ALU.mult))
                ins = ve.scalar_tensor_tensor(comb[0:n, b, 0:NEXP], pick[0:n, 1, :], p2, comb[0:n, b, 0:NEXP], ALU.mult, ALU.add)
                if b < 2:
                    step(ins)
                else:
                    ins.then_inc(chosen_ready, 1)
                    dve.wait_ge(chosen_ready, 1)
            key = ("choice", 0)
            dve.wait_ge(*filled(key))
            empty(ve.tensor_copy(placeT, psum(key)[0:NEXP, 0:T]), key)
            step(ve.tensor_tensor_scan(chosenT, placeT, placeT, 0.0, ALU.add, ALU.max))
            step(tt(placeT, placeT, chosenT, ALU.mult))
            ins = ve.tensor_scalar(placeT, placeT, -1.0, None, ALU.add)
            ins.then_inc(places_ready, 1)
            dve.wait_ge(places_ready, 1)
            key = ("place", 0)
            dve.wait_ge(*filled(key))
            step(ve.tensor_copy(rank[:, 0:2, 0:NEXP], psum(key)[:, 0:16].rearrange("p (b e) -> p b e", b=2)))
            empty(ve.tensor_copy(rank[0:TS, 2, 0:NEXP], psum(key)[0:TS, 16:24]), key)
            for b, (t0, n) in enumerate(BLK):
                step(ve.memset(rank[0:n, b, NEXP:NEXP + 1], -1.0))
                step(ve.memset(comb[0:n, b, NEXP:NEXP + 1], 0.0))
            key = ("count", 0)
            dve.wait_ge(*filled(key))
            empty(ve.tensor_reduce(rcount[:, 0:1], psum(key)[0:1, 0:NEXP], AX.X, ALU.max), key)
            step(ve.tensor_scalar(rcount[:, 1:2], rcount[:, 0:1], float(CAP), 1.0, ALU.is_gt, ALU.add))
            step(ve.tensor_scalar(rcount[:, 2:3], rcount[:, 0:1], 2.0 * CAP, None, ALU.is_gt))
            step(tt(rcount[:, 3:4], rcount[:, 1:2], rcount[:, 2:3], ALU.add))
            ins = ve.tensor_copy(rounds, rcount[:, 3:4])
            ins.then_inc(rounds_ready, 1)
            dve.wait_ge(rounds_ready, 1)
            advance(dve, "m_sel", "m_weights", "m_hid", "m_added")
            nr = load_rounds(dve)

            def select(gi, it, e, base, count):
                order = [0]

                def lstep(ins):
                    order[0] += 1
                    ins.then_inc(dve_loop, 1)
                    dve.wait_ge(dve_loop, base + order[0])

                dve.wait_ge(*lat("m_gathered", gi - 1, 2))
                dve.wait_ge(*lat("m_turned", it, 1))
                for b, (t0, n) in enumerate(BLK):
                    lstep(ve.tensor_scalar(Pm[0:n, b, :], iota[0:n, 0:CAP], rank[0:n, b, bass.ds(e, 1)], None,
                                           ALU.is_equal))
                for b, (t0, n) in enumerate(BLK):
                    ins = ve.tensor_scalar(Pc[0:n, b, :], Pm[0:n, b, :], comb[0:n, b, bass.ds(e, 1)], None, ALU.mult)
                    if b < 2:
                        lstep(ins)
                ins.then_inc(loop_signals["m_sel"], 1)
                if count:
                    loop_raised["m_sel"] += 1

            def add_scattered(gi, count):
                for m in range(KT):
                    dve.wait_ge(*lat("m_scattered", gi, m + 1))
                    tt(xT[:, m, :], xT[:, m, :], bank[6 + m % 2][:, 0:T], ALU.add).then_inc(loop_signals["m_added"], 1)
                    if count:
                        loop_raised["m_added"] += 1

            with dve.Fori(0, nr) as r:
                start = r * (NEXP * NDVE + NSEL + 1)
                gi = r * (NEXP + 1)
                select(gi, r * NEXP - 1, 0, start, False)
                ins = ve.memset(yb, 0.0)
                ins.then_inc(dve_loop, 1)
                dve.wait_ge(dve_loop, start + NSEL + 1)
                ve.memset(Cm, 0.0).then_inc(loop_signals["m_weights"], 1)
                with dve.Fori(0, NEXP) as e:
                    it = r * NEXP + e
                    gi = r * (NEXP + 1) + e
                    order = [0]
                    base = r * (NEXP * NDVE + NSEL + 1) + NSEL + 1 + e * NDVE

                    def lstep(ins):
                        order[0] += 1
                        ins.then_inc(dve_loop, 1)
                        dve.wait_ge(dve_loop, base + order[0])

                    add_scattered(gi, True)
                    dve.wait_ge(*lat("m_turned", it, 1))
                    ve.tensor_copy(Cm, bank[6][0:CAP, 0:T]).then_inc(*lup("m_weights"))
                    for c in range(NCH):
                        if c == NCH - 1:
                            select(gi + 1, it, e + 1, base + order[0], True)
                            order[0] += NSEL
                        x = ex[c % 2]
                        dve.wait_ge(*lat("m_exp", it, c + 1))
                        lstep(ve.tensor_scalar(x, x, 1.0, None, ALU.add))
                        lstep(ve.reciprocal(x, x))
                        lstep(tt(x, x, bank[c % 2][0:CAP, :], ALU.mult))
                        dve.wait_ge(*lat("m_hidden", it, max(c - 1, 0)))
                        dve.wait_ge(*lat("m_gu", it, 2 * c + 2))
                        tt(hid[c % 2], x, bank[2][0:CAP, :], ALU.mult).then_inc(*lup("m_hid"))
                    assert order[0] == NDVE, order
                gi = r * (NEXP + 1) + NEXP
                add_scattered(gi, False)
                dve.wait_ge(*lat("m_added", gi, 8))
                for b, (t0, n) in enumerate(BLK):
                    ve.tensor_scalar(rank[0:n, b, :], rank[0:n, b, :], float(-CAP), None, ALU.add
                                     ).then_inc(rank_moved, 1)
                dve.wait_ge(rank_moved, r * 3 + 3)

        assert raised == {k: DEPTH * v for k, v in PER.items()}, {k: v for k, v in raised.items() if v != DEPTH * PER[k]}
        assert loop_raised == LOOP, loop_raised


_INS = ['x_prompt', 'x_sample', 'state_hgrn', 'state_ssm', 'state_conv', 'cache_kv_w128', 'cache_kv_w512',
        'cache_kv_w2048', 'w_in', 'mix_norm', 'hgrn_lb_logits', 'hgrn_norm', 'ssm_conv_w', 'ssm_conv_b',
        'ssm_dt_bias', 'ssm_a_log', 'ssm_d', 'ssm_norm', 'att_q_norm', 'att_k_norm', 'w_out_hgrn', 'w_out_ssm',
        'w_out_att', 'w_o', 'ffn_norm', 'w_ffn_up', 'w_ffn_down', 'w_router', 'w_moe_up', 'w_moe_down']
_OUTS = [(1, 256, 1024), (8, 4, 1024), (2, 1, 4, 128, 128), (2, 1, 8, 64, 128), (2, 1, 3, 1024),
         (2, 1, 128, 2, 4, 64), (2, 1, 256, 2, 4, 64), (2, 1, 256, 2, 4, 64),
         (2, 8, 4, 128, 128), (2, 8, 8, 64, 128), (2, 8, 3, 1024),
         (2, 8, 4, 2, 4, 64), (2, 8, 4, 2, 4, 64), (2, 8, 4, 2, 4, 64)]


def kernel(**inputs):
    import numpy as _np
    import concourse.bacc as _bacc
    from concourse import mybir as _mybir
    from concourse.bass_utils import run_bass_kernel_spmd as _run

    nc = _bacc.Bacc("TRN2", target_bir_lowering=False, num_devices=1)
    arrays, args = {}, []
    for name in _INS:
        a = _np.ascontiguousarray(inputs[name])
        arrays[f"in_{name}_dram"] = a
        args.append(nc.dram_tensor(f"in_{name}_dram", a.shape, _mybir.dt.from_np(a.dtype), kind="ExternalInput").ap())
    for i, shape in enumerate(_OUTS):
        args.append(nc.dram_tensor(f"out_{i}_dram", shape, _mybir.dt.float32, kind="ExternalOutput").ap())
    hybrid_decoder(nc, *args)
    r = _run(nc, [arrays], core_ids=[0])
    return tuple(r.results[0][f"out_{i}_dram"] for i in range(len(_OUTS)))
```
